# Optimizing a Trainium2 kernel written in Bass

```python
import jax, jax.numpy as jnp
from jax import lax
import numpy as np

D_MODEL = 1024
BATCH = 1
SEQ = 1024
DEPTH = 1

PLE_DIM = 256
HG_WIDTH = D_MODEL // 2
HG_KDIM = 128
HG_HEADS = HG_WIDTH // HG_KDIM
HG_VDIM = HG_WIDTH // HG_HEADS
HG_CHUNK = 64
FOX_WIDTH = D_MODEL // 2
FOX_HDIM = 64
FOX_HEADS = FOX_WIDTH // FOX_HDIM
FOX_BLOCK = 128
D_FF = 4 * D_MODEL
N_IN = 4 * HG_WIDTH + 3 * FOX_WIDTH + FOX_HEADS + 2 * D_MODEL
LN_EPS = 1e-5
RMS_EPS = 1e-6
DEEPNORM_ALPHA = (2.0 * DEPTH) ** 0.25
DEEPNORM_BETA = (8.0 * DEPTH) ** -0.25

kernel_name = "hybrid_hgrn2_fox_deepnorm_block"

def layer_norm(x, g, b):
    xf = x.astype(jnp.float32)
    mu = jnp.mean(xf, axis=-1, keepdims=True)
    var = jnp.mean(jnp.square(xf - mu), axis=-1, keepdims=True)
    y = (xf - mu) * lax.rsqrt(var + LN_EPS)
    return (y * g.astype(jnp.float32) + b.astype(jnp.float32)).astype(x.dtype)

def hgrn2_lower_bound(lb_logits, layer):
    probs = jax.nn.softmax(lb_logits.astype(jnp.float32), axis=0)
    return jnp.cumsum(probs, axis=0)[layer]

def _hgrn2_chunk_step(state, chunk):
    q_c, k_c, v_c, g_c = chunk
    C = q_c.shape[2]
    b = jnp.cumsum(g_c, axis=2)
    causal = jnp.tril(jnp.ones((C, C), dtype=bool))[:, :, None]
    diff = b[:, :, :, None, :] - b[:, :, None, :, :]
    decay = jnp.exp(jnp.where(causal, diff, -jnp.inf))
    scores = jnp.einsum('bhtk,bhtsk,bhsk->bhts', q_c, decay, k_c)
    o = (jnp.einsum('bhts,bhsv->bhtv', scores, v_c)
         + jnp.einsum('bhtk,bhkv->bhtv', q_c * jnp.exp(b), state))
    b_last = b[:, :, -1:, :]
    new_state = (jnp.exp(b_last[:, :, 0, :])[..., None] * state
                 + jnp.einsum('bhsk,bhsv->bhkv', k_c * jnp.exp(b_last - b), v_c))
    return new_state, o

def hgrn2_branch(q_lin, f_lin, i_lin, og_lin, lb, norm_g):
    B, S, _ = q_lin.shape
    n_chunks = S // HG_CHUNK
    q = jax.nn.silu(q_lin.astype(jnp.float32))
    f = lb + (1.0 - lb) * jax.nn.sigmoid(f_lin.astype(jnp.float32))
    log_f = jnp.log(f)
    k = 1.0 - f
    v = i_lin.astype(jnp.float32)

    def to_chunks(t, d):
        return t.reshape(B, n_chunks, HG_CHUNK, HG_HEADS, d).transpose(1, 0, 3, 2, 4)

    xs = (to_chunks(q, HG_KDIM), to_chunks(k, HG_KDIM), to_chunks(v, HG_VDIM), to_chunks(log_f, HG_KDIM))
    state0 = jnp.zeros((B, HG_HEADS, HG_KDIM, HG_VDIM), jnp.float32)
    _, o = lax.scan(_hgrn2_chunk_step, state0, xs)
    o = o.transpose(1, 0, 3, 2, 4).reshape(B, S, HG_HEADS, HG_VDIM)
    o = o * lax.rsqrt(jnp.mean(jnp.square(o), axis=-1, keepdims=True) + RMS_EPS)
    o = o.reshape(B, S, HG_WIDTH) * norm_g.astype(jnp.float32) * jax.nn.silu(og_lin.astype(jnp.float32))
    return o.astype(q_lin.dtype)

def fox_branch(q_lin, k_lin, v_lin, f_lin, f_bias):
    B, S, _ = q_lin.shape
    def heads(t):
        return t.reshape(B, S, FOX_HEADS, FOX_HDIM).transpose(0, 2, 1, 3)
    q, k, v = heads(q_lin), heads(k_lin), heads(v_lin)
    log_f = jax.nn.log_sigmoid(f_lin.astype(jnp.float32) + f_bias.astype(jnp.float32))
    c = jnp.cumsum(log_f.transpose(0, 2, 1), axis=-1)
    scale = FOX_HDIM ** -0.5
    outs = []
    for blk in range(S // FOX_BLOCK):
        start, end = blk * FOX_BLOCK, (blk + 1) * FOX_BLOCK
        qb = q[:, :, start:end]
        kb, vb = k[:, :, :end], v[:, :, :end]
        logits = jnp.einsum('bhqd,bhkd->bhqk', qb, kb).astype(jnp.float32) * scale
        logits = logits + (c[:, :, start:end, None] - c[:, :, None, :end])
        q_pos = jnp.arange(start, end)
        k_pos = jnp.arange(end)
        mask = k_pos[None, :] <= q_pos[:, None]
        probs = jax.nn.softmax(jnp.where(mask, logits, -jnp.inf), axis=-1)
        outs.append(jnp.einsum('bhqk,bhkd->bhqd', probs.astype(vb.dtype), vb))
    o = jnp.concatenate(outs, axis=2)
    return o.transpose(0, 2, 1, 3).reshape(B, S, FOX_WIDTH)

def setup_inputs(seed: int = 0) -> dict:
    key = jax.random.key(seed)
    ks = jax.random.split(key, 20)
    f32 = jnp.float32
    nrm = lambda k, shape, s: jax.random.normal(k, shape, f32) * s
    beta = DEEPNORM_BETA
    return {
        "x": nrm(ks[0], (BATCH, SEQ, D_MODEL), 1.0),
        "p": nrm(ks[1], (DEPTH, BATCH, SEQ, PLE_DIM), 1.0),
        "ln0_g": 1.0 + nrm(ks[2], (D_MODEL,), 0.02),
        "ln0_b": nrm(ks[3], (D_MODEL,), 0.02),
        "w_in": nrm(ks[4], (DEPTH, D_MODEL, N_IN), D_MODEL ** -0.5),
        "hg_lb": nrm(ks[5], (DEPTH + 1, HG_WIDTH), 1.0),
        "hg_norm_g": 1.0 + nrm(ks[6], (DEPTH, HG_WIDTH), 0.02),
        "fox_fb": jnp.linspace(1.0, 4.0, FOX_HEADS, dtype=f32)[None, :] + nrm(ks[7], (DEPTH, FOX_HEADS), 0.1),
        "w_a": nrm(ks[8], (DEPTH, HG_WIDTH, D_MODEL), beta * HG_WIDTH ** -0.5),
        "w_b": nrm(ks[9], (DEPTH, FOX_WIDTH, D_MODEL), beta * FOX_WIDTH ** -0.5),
        "w_o": nrm(ks[10], (DEPTH, D_MODEL, D_MODEL), beta * D_MODEL ** -0.5),
        "ln1_g": 1.0 + nrm(ks[11], (DEPTH, D_MODEL), 0.02),
        "ln1_b": nrm(ks[12], (DEPTH, D_MODEL), 0.02),
        "w_ff1": nrm(ks[13], (DEPTH, D_MODEL, D_FF), beta * D_MODEL ** -0.5),
        "w_ff2": nrm(ks[14], (DEPTH, D_FF, D_MODEL), beta * D_FF ** -0.5),
        "w_pg": nrm(ks[15], (DEPTH, D_MODEL, D_MODEL), D_MODEL ** -0.5),
        "w_p": nrm(ks[16], (DEPTH, PLE_DIM, D_MODEL), beta * PLE_DIM ** -0.5),
        "ln2_g": 1.0 + nrm(ks[17], (DEPTH, D_MODEL), 0.02),
        "ln2_b": nrm(ks[18], (DEPTH, D_MODEL), 0.02),
    }

def reference(x, p, ln0_g, ln0_b, w_in, hg_lb, hg_norm_g, fox_fb, w_a, w_b, w_o,
              ln1_g, ln1_b, w_ff1, w_ff2, w_pg, w_p, ln2_g, ln2_b):
    sizes = [HG_WIDTH] * 4 + [FOX_WIDTH] * 3 + [FOX_HEADS] + [D_MODEL] * 2
    split_at = [int(s) for s in np.cumsum(sizes)[:-1]]
    h = layer_norm(x, ln0_g, ln0_b)
    for i in range(DEPTH):
        proj = jnp.einsum('bsd,dn->bsn', h, w_in[i])
        (hg_q, hg_f, hg_i, hg_g, fx_q, fx_k, fx_v, fx_f, gate_a, gate_b) = jnp.split(proj, split_at, axis=-1)
        lb = hgrn2_lower_bound(hg_lb, i)
        y_a = hgrn2_branch(hg_q, hg_f, hg_i, hg_g, lb, hg_norm_g[i])
        y_b = fox_branch(fx_q, fx_k, fx_v, fx_f, fox_fb[i])
        merged = (jax.nn.sigmoid(gate_a) * jnp.einsum('bsc,cd->bsd', y_a, w_a[i])
                  + jax.nn.sigmoid(gate_b) * jnp.einsum('bsc,cd->bsd', y_b, w_b[i]))
        mix = jnp.einsum('bsd,de->bse', merged, w_o[i])
        h = layer_norm(DEEPNORM_ALPHA * h + mix, ln1_g[i], ln1_b[i])
        ff = jnp.einsum('bsf,fd->bsd', jnp.square(jax.nn.relu(jnp.einsum('bsd,df->bsf', h, w_ff1[i]))), w_ff2[i])
        ple = jax.nn.sigmoid(jnp.einsum('bsd,de->bse', h, w_pg[i])) * jnp.einsum('bsp,pd->bsd', p[i], w_p[i])
        h = layer_norm(DEEPNORM_ALPHA * h + ff + ple, ln2_g[i], ln2_b[i])
    return h


_drawn_inputs = setup_inputs


def setup_inputs(seed=0):
    import zlib

    import numpy as np

    out = dict(_drawn_inputs(seed))
    spreads = {}
    factors = {'ln0_g': 2.819,
     'ln0_b': 2.917,
     'hg_lb': 6.58,
     'hg_norm_g': 30.343,
     'ln1_g': 7.846,
     'ln1_b': 8.111,
     'ln2_g': 23.703,
     'ln2_b': 23.957,
     'fox_fb': 2.685,
     'w_pg': 3.901}
    for name, (base, spread) in spreads.items():
        noise = np.random.default_rng([zlib.crc32(name.encode()), seed]).standard_normal(out[name].shape)
        drawn = base * np.exp(spread * noise) if base else spread * noise
        out[name] = __import__('jax').numpy.asarray(drawn.astype(out[name].dtype))
    for name, factor in factors.items():
        out[name] = (out[name] * factor).astype(out[name].dtype)
    return out
```

```python
from contextlib import ExitStack

import numpy as np

import concourse.bass as bass
from concourse import mybir

F32 = mybir.dt.float32
F32R = mybir.dt.float32r
BF16 = mybir.dt.bfloat16
U8 = mybir.dt.uint8
ALU = mybir.AluOpType
ACT = mybir.ActivationFunctionType

P = 128
S = 1024
D = 1024
KD = D // P
TT = S // P
HALF = 512
HG = 512
NHG = 4
FX = 512
NFX = 8
NPAIR = 4
FF = 4096
PLE = 256
LN_EPS = 1e-5
RMS_EPS = 1e-6
ALPHA = 2.0 ** 0.25
LEVELS = 8
F_FLOOR = 2.0 ** -63

C_HQ, C_HF, C_HI, C_HGATE = 0, 512, 1024, 1536
C_FQ, C_FK, C_FV, C_FF = 2048, 2560, 3072, 3584
C_GA, C_GB = 3592, 4616

CHUNKS = []


def _plan():
    add = CHUNKS.append
    for j in range(4):
        add(("in", C_HI + 128 * j))
    add(("in", C_HQ))
    add(("in", C_HF))
    for n in range(3):
        add(("in", C_HGATE + 128 * n))
        add(("in", C_HQ + 128 * (n + 1)))
        add(("in", C_HF + 128 * (n + 1)))
    add(("in", C_HGATE + 384))
    add(("in", C_FQ))
    add(("in", C_FK))
    add(("in", C_GA))
    add(("in", C_FF))
    for j in range(4):
        add(("in", C_FV + 128 * j))
    for n in range(1, 4):
        add(("in", C_FQ + 128 * n))
        add(("in", C_FK + 128 * n))
    for m in range(1, 8):
        add(("in", C_GA + 128 * m))
    for m in range(8):
        add(("in", C_GB + 128 * m))
    for m in range(8):
        add(("ab", 128 * m))
    for m in range(8):
        add(("o", 128 * m))
    for m in range(2):
        add(("p", 512 * m))
    for m in range(8):
        add(("pg", 128 * m))
    for g in range(8):
        for m in range(4):
            add(("ff1", 512 * g + 128 * m))
        for m in range(4):
            add(("ff2", 512 * g, 256 * m))


_plan()
C_VHG, C_Q0 = 0, 4
C_VFX = 20
C_AB = 45
C_O = 53
C_PW = 61
C_PG = 63
C_FFN = 71
NG = 8

NPAGES = 50
RAW = 0
SPARE = 2
WHI, WLO = 3, 7
XHI, XLO = 11, 19
PG_X, PG_H, PG_G0, PG_B0 = 27, 36, 38, 39
PG_HQ, PG_HB, PG_HK, PG_GATE = 27, 29, 31, 33
PG_AB, PG_S, PG_KT, PG_ST, PG_T1, PG_T2, PG_T3 = 34, 36, 37, 38, 39, 40, 41
PG_VHG, PG_YA = 42, 46
PG_FQ, PG_FK, PG_CROW, PG_NEGC = 27, 29, 32, (33, 41)
PG_VFX, PG_XP, PG_PT, PG_O, PG_YB = 34, 38, 40, SPARE, 42
PG_GA = [31, 27, 29, 32, 28, 30, 33, 34]
PG_GB = [35, 36, 37, 38, 39, 40, 41, SPARE]
PG_YAH, PG_YAL, PG_YBH, PG_YBL = 11, 15, 19, 23
PG_M1, PG_M2 = 46, 47
PG_MIX = 11
PG_R, PG_G1, PG_B1, PG_PTH, PG_PTL, PG_PRAW = 19, 21, 22, 23, 25, 19
PG_H1H, PG_H1L = 27, 42
PG_ACC = [35, 36, 37, 38, 39, 40, 41, SPARE]
PG_SG = (11, 12)
PG_ACTH, PG_ACTL = 13, 17
PG_RELU = (21, 22)
PG_OUT, PG_G2, PG_B2 = 11, 23, 24


def block_kernel(nc, x, p, ln0_g, ln0_b, w_in, hg_lb, hg_norm_g, fox_fb, w_a, w_b, w_o, ln1_g, ln1_b,
                 w_ff1, w_ff2, w_pg, w_p, ln2_g, ln2_b, c_ident, c_causal, c_masks,
                 h_scratch, c_scratch, out):
    with ExitStack() as ctx:
        sb = lambda name, shape, dt: ctx.enter_context(nc.sbuf_tensor(name, shape, dt))
        sem = lambda name: ctx.enter_context(nc.semaphore(name))

        def view(name, dt, runs, stack):
            found, page = {}, 0
            while page < NPAGES:
                n = runs.get(page, 1)
                t = stack.enter_context(nc.sbuf_tensor(f"{name}{page}", [P, n * 1024], dt))
                for i in range(n):
                    found[page + i] = (t, i * 1024)
                page += n
            return found

        with ExitStack() as plain:
            f32_pages = view("page", F32, {PG_PRAW: 2}, plain)
        f32r_pages = view("parts", F32R, {WHI: 4, WLO: 4, XHI: 8, XLO: 8, PG_H1H: 8, PG_H1L: 8}, ctx)

        def F(page, off=0, n=1024):
            t, at = f32_pages[page + off // 1024]
            return t[:, at + off % 1024:at + off % 1024 + n]

        def R(page, off=0, n=1024):
            t, at = f32r_pages[page]
            return t[:, at + off:at + off + n]

        ident = sb("ident", [P, P], F32)
        ones = sb("ones", [P, P], F32)
        mean_w = sb("mean_w", [P, P], F32)
        identb = sb("identb", [P, P], BF16)
        causal = sb("causal", [P, P], BF16)
        masks = sb("masks", [P, LEVELS, P], U8)
        lbl = sb("lbl", [P, 2, NHG], F32)
        lb = sb("lb", [P, NHG], F32)
        omlb = sb("omlb", [P, NHG], F32)
        lbt = sb("lbt", [P, 4, NHG], F32)
        ng = sb("ng", [P, NHG], F32)
        fb = sb("fb", [P, 1], F32)
        stats = sb("stats", [P, 2, 2, 6], F32)
        mv = sb("mv", [P, 2, 2], F32)
        rstd = sb("rstd", [P, 2, 3], F32)
        eps = sb("eps", [P, 2], F32)
        eb_last = sb("eb_last", [P, 2, TT], F32)
        mx = sb("mx", [P, 2, 1], F32)
        nmx = sb("nmx", [P, 2, 1], F32)
        psm = sb("psm", [P, 4, 1], F32)
        rinv = sb("rinv", [P, 2, 1], F32)

        dense = [ctx.enter_context(nc.psum_tensor(f"dense{i}", [P, 2 * HALF], F32)) for i in range(2)]
        mixA = ctx.enter_context(nc.psum_tensor("mixA", [P, 2 * HALF], F32))
        mixB = ctx.enter_context(nc.psum_tensor("mixB", [P, 2 * HALF], F32))
        bankM = [mixA[:, 0:HALF], mixA[:, HALF:], mixB[:, 0:HALF], mixB[:, HALF:]]

        consts_in, rows_in, cols_in = sem("consts_in"), sem("rows_in"), sem("cols_in")
        const_set, lb_mx, lb_exp, lb_ready = sem("const_set"), sem("lb_mx"), sem("lb_exp"), sem("lb_ready")
        x_in = [sem(f"x_in{t}") for t in range(TT)]
        w_landed = [sem(f"w_landed{i}") for i in range(2)]
        w_hi, w_split = sem("w_hi"), sem("w_split")
        mm_done = sem("mm_done")
        dve_step, act_step, rms_log = sem("dve_step"), sem("act_step"), sem("rms_log")
        var_ready, rs_est = sem("var_ready"), sem("rs_est")
        h_ready, h_turned, h_hi, h_split = sem("h_ready"), sem("h_turned"), sem("h_hi"), sem("h_split")
        h_stored = [sem("h_stored0"), sem("h_stored1")]
        v_ready = sem("v_ready")
        q_exp, q_ready, f_exp, f_ready, f_log, b_ready = (
            sem("q_exp"), sem("q_ready"), sem("f_exp"), sem("f_ready"), sem("f_log"), sem("b_ready"))
        g_exp, gate_ready = sem("g_exp"), sem("gate_ready")
        eb_exp, qe_ready = sem("eb_exp"), sem("qe_ready")
        kd_sub, kd_exp, kd_ready, kt_turned, kt_done = (
            sem("kd_sub"), sem("kd_exp"), sem("kd_ready"), sem("kt_turned"), sem("kt_done"))
        ab_sub, ab_exp, ab_ready, lvl_done, pred_done = (
            sem("ab_sub"), sem("ab_exp"), sem("ab_ready"), sem("lvl_done"), sem("pred_done"))
        upd_done, st_ready, o_done, sq_done, rms_done, rs_ready, y_done = (
            sem("upd_done"), sem("st_ready"), sem("o_done"), sem("sq_done"), sem("rms_done"), sem("rs_ready"), sem("y_done"))
        fq_ready, fk_ready = sem("fq_ready"), sem("fk_ready")
        c_lin, c_abs, c_exp, c_log, c_ready, c_stored = (
            sem("c_lin"), sem("c_abs"), sem("c_exp"), sem("c_log"), sem("c_ready"), sem("c_stored"))
        negc_in = [sem("negc_in0"), sem("negc_in1")]
        qk_done, x_ready, nmx_ready, p_ready, p_turned, pt_done, pv_done, o_ready = (
            sem("qk_done"), sem("x_ready"), sem("nmx_ready"), sem("p_ready"), sem("p_turned"), sem("pt_done"),
            sem("pv_done"), sem("o_ready"))
        rinv_ready = sem("rinv_ready")
        ot_done, yb_done = sem("ot_done"), sem("yb_done")
        gx_exp, gx_ready = sem("gx_exp"), sem("gx_ready")
        y_hi, y_split = sem("y_hi"), sem("y_split")
        a_used, b_used, m_sum, m_hi, m_split = sem("a_used"), sem("b_used"), sem("m_sum"), sem("m_hi"), sem("m_split")
        mix_ready = sem("mix_ready")
        pe_in, pe_turned, pe_hi, pe_split = sem("pe_in"), sem("pe_turned"), sem("pe_hi"), sem("pe_split")
        rows1_in = sem("rows1_in")
        hr_in = [sem("hr_in0"), sem("hr_in1")]
        mt_turned, r_done, h1_ready, h1_turned, h1_hi, h1_split = (
            sem("mt_turned"), sem("r_done"), sem("h1_ready"), sem("h1_turned"), sem("h1_hi"), sem("h1_split"))
        pw_ready, pg_done, acc_init = sem("pw_ready"), sem("pg_done"), sem("acc_init")
        relu_done, act_sq, act_hi, act_split, acc_done = (
            sem("relu_done"), sem("act_sq"), sem("act_hi"), sem("act_split"), sem("acc_done"))
        rows2_in = sem("rows2_in")
        fin_turned, fin_ready = sem("fin_turned"), sem("fin_ready")
        out_stored = [sem("out_stored0"), sem("out_stored1")]

        JOB, FREED, CHUNK_OF, USED_BY = {}, [], [], {}

        def job(name, chunk, freed):
            JOB[name] = len(FREED)
            for c in range(chunk - 3, chunk + 1) if name[0] in ("vhg", "vfx") else (chunk,):
                USED_BY[c] = len(FREED)
            FREED.append(freed)
            CHUNK_OF.append(chunk)

        for t in range(TT):
            job(("vhg", t), C_VHG + 3, (v_ready, t + 1))
        job(("q", 0), 4, (q_ready, 1))
        job(("f", 0), 5, (f_exp, 1))
        for n in range(NHG):
            c = 6 + 3 * n
            job(("g", n), c, (gate_ready, n + 1))
            if n < NHG - 1:
                job(("q", n + 1), c + 1, (q_ready, n + 2))
                job(("f", n + 1), c + 2, (f_exp, n + 2))
        job(("fq", 0), 16, (fq_ready, 1))
        job(("fk", 0), 17, (fk_ready, 1))
        job(("gx", 0), 18, (gx_exp, 1))
        job(("crow",), 19, (c_lin, 1))
        for t in range(TT):
            job(("vfx", t), C_VFX + 3, (v_ready, TT + t + 1))
        for n in range(1, NPAIR):
            job(("fq", n), 22 + 2 * n, (fq_ready, n + 1))
            job(("fk", n), 23 + 2 * n, (fk_ready, n + 1))
        for i in range(1, 16):
            job(("gx", i), 29 + i, (gx_exp, i + 1))
        for m in range(KD):
            job(("A", m), C_AB + m, (a_used, m + 1))
            job(("B", m), C_AB + m, (b_used, m + 1))
        for m in range(KD):
            job(("mix", m), C_O + m, (mix_ready, m + 1))
        for m in range(KD):
            job(("pw", m), C_PW + m // 4, (pw_ready, m + 1))
        for m in range(KD):
            job(("pg", m), C_PG + m, (pg_done, m + 1))
        for g in range(NG):
            for m in range(4):
                job(("ff1", 4 * g + m), C_FFN + 8 * g + m, (relu_done, 4 * g + m + 1))
            for m in range(KD):
                job(("ff2", 8 * g + m), C_FFN + 8 * g + 4 + m // 2, (acc_done, 8 * g + m + 1))

        def done(eng, *name):
            eng.wait_ge(mm_done, JOB[name] + 1)

        kview = lambda w: w.rearrange("a (k p) n -> p (a k) n", p=P)
        w_views = {"in": kview(w_in), "o": kview(w_o), "pg": kview(w_pg), "p": kview(w_p),
                   "ff1": kview(w_ff1), "ff2": kview(w_ff2), "a": kview(w_a), "b": kview(w_b)}
        x_t = x.rearrange("a (t p) d -> (a t) p d", p=P)
        out_t = out.rearrange("a (t p) d -> (a t) p d", p=P)

        def vtile(page, t):
            return F(page + t // 2, (t % 2) * HG, HG)

        def row(vec):
            return vec.partition_broadcast(P)

        block = ctx.enter_context(nc.Block())

        @block.sync
        def _(sp):
            def load_chunk(c):
                kind, at = CHUNKS[c][0], CHUNKS[c][-1]
                if c >= 2:
                    sp.wait_ge(w_split, c - 1)
                k4 = [F(RAW + c % 2, 0, HALF), F(RAW + c % 2, HALF, HALF)]
                if kind == "ab":
                    src = [w_views["a"][:, 0:4, at:at + P], w_views["b"][:, 0:4, at:at + P]]
                elif kind == "p":
                    src = [w_views["p"][:, k, at:at + HALF] for k in range(2)]
                elif kind == "ff2":
                    k0 = 4 * (CHUNKS[c][1] // HALF)
                    src = [w_views["ff2"][:, k0 + 2 * i:k0 + 2 * i + 2, at:at + 256] for i in range(2)]
                else:
                    src = [w_views[kind][:, 4 * i:4 * i + 4, at:at + P] for i in range(2)]
                for dst, s in zip(k4, src):
                    if len(s.shape) == 3:
                        dst = dst.rearrange("q (k n) -> q k n", k=s.shape[1])
                    sp.dma_start(dst, s).then_inc(w_landed[c % 2], 16)

            def load_negc(hh):
                if hh >= 2:
                    sp.wait_ge(x_ready, 8 * (hh - 1))
                sp.dma_start(F(PG_NEGC[hh % 2]), row(c_scratch[hh, :])).then_inc(negc_in[hh % 2], 16)

            for c in range(len(CHUNKS)):
                load_chunk(c)
                if c == 25:
                    sp.wait_ge(c_ready, 1)
                    sp.dma_start(c_scratch[:, :], F(PG_CROW)[0:NFX, :]).then_inc(c_stored, 16)
                    sp.wait_ge(c_stored, 16)
                    load_negc(0)
                    load_negc(1)
                if 29 <= c < 35:
                    load_negc(c - 27)
                if c == C_O + 4:
                    done(sp, "B", KD - 1)
                    sp.dma_start(F(PG_PRAW, 0, 2048).rearrange("q (t d) -> q t d", d=PLE),
                                 p.rearrange("l a (t q) d -> q (l a t) d", q=P)).then_inc(pe_in, 16)
                    sp.dma_start(F(PG_G1), row(ln1_g[0, :])).then_inc(rows1_in, 16)
                    sp.dma_start(F(PG_B1), row(ln1_b[0, :])).then_inc(rows1_in, 16)
                if c == C_PG + 1:
                    for t in range(TT):
                        if t < 2:
                            sp.wait_ge(pe_turned, 2)
                        else:
                            sp.wait_ge(h1_turned, t - 1)
                        sp.dma_start(F(PG_R + t % 2), h_scratch[t]).then_inc(hr_in[t % 2], 16)
                if c == C_FFN + 8:
                    done(sp, "pw", KD - 1)
                    sp.dma_start(F(PG_G2), row(ln2_g[0, :])).then_inc(rows2_in, 16)
                    sp.dma_start(F(PG_B2), row(ln2_b[0, :])).then_inc(rows2_in, 16)
            for t in range(TT):
                sp.wait_ge(fin_ready, t + 1)
                sp.dma_start(out_t[t], F(PG_OUT + t % 2)).then_inc(out_stored[t % 2], 16)
            for i in range(2):
                sp.wait_ge(out_stored[i], 16 * (TT // 2))
                sp.wait_ge(h_stored[i], 16 * (TT // 2))

        @block.gpsimd
        def _(pool):
            for c in range(len(CHUNKS)):
                slot = c % 4
                pool.wait_ge(w_landed[c % 2], 32 * (c // 2 + 1))
                if c >= 4:
                    pool.wait_ge(mm_done, USED_BY[c - 4] + 1)
                nc.gpsimd.tensor_copy(R(WHI + slot), F(RAW + c % 2)).then_inc(w_hi, 1)
                pool.wait_ge(w_hi, c + 1)
                nc.gpsimd.tensor_tensor(R(WLO + slot), F(RAW + c % 2), R(WHI + slot).bitcast(F32),
                                        ALU.subtract).then_inc(w_split, 1)

        @block.tensor
        def _(pe):
            mm = nc.tensor.matmul

            def three_pass(out2, whi, wlo, xhi2, xlo2, first, last):
                for o, x_ in zip(out2, xhi2):
                    mm(o, whi, x_, start=first, stop=False)
                for o, x_ in zip(out2, xlo2):
                    mm(o, whi, x_, start=False, stop=False)
                for o, x_ in zip(out2, xhi2):
                    ins = mm(o, wlo, x_, start=False, stop=last)
                return ins

            def begin(j):
                pe.wait_ge(w_split, CHUNK_OF[j] + 1)
                if j >= 2:
                    pe.wait_ge(*FREED[j - 2])

            def end(ins, j):
                ins.then_inc(mm_done, 1)

            def halves(ap):
                return [ap[:, 0:HALF], ap[:, HALF:2 * HALF]]

            def feature_job(name, col, stride, acts_hi, acts_lo, ready=None):
                j = JOB[name]
                begin(j)
                slot = CHUNK_OF[j] % 4
                out2 = halves(dense[j % 2][:, :])
                K = len(acts_hi)
                for k in range(K):
                    if ready is not None:
                        pe.wait_ge(ready[0], ready[1](k))
                    at = col + k * stride
                    ins = three_pass(out2, R(WHI + slot, at, P), R(WLO + slot, at, P),
                                     halves(acts_hi[k]), halves(acts_lo[k]), k == 0, k == K - 1)
                    if k == K - 1:
                        end(ins, j)
                    yield

            h_hi_p = [R(XHI + k) for k in range(KD)]
            h_lo_p = [R(XLO + k) for k in range(KD)]

            def value_job(name, t):
                j = JOB[name, t]
                begin(j)
                wide = lambda base, k: R(base, 0, 4096).rearrange(
                    "q (s n) -> q s n", s=4)[:, :, k * P:(k + 1) * P]
                out1 = dense[j % 2][:, 0:HALF].rearrange("q (s n) -> q s n", s=4)
                for k in range(KD):
                    xh, xl = R(XHI + k, t * P, P), R(XLO + k, t * P, P)
                    mm(out1, xh, wide(WHI, k), start=k == 0, stop=False)
                    mm(out1, xh, wide(WLO, k), start=False, stop=False)
                    ins = mm(out1, xl, wide(WHI, k), start=False, stop=k == KD - 1)
                end(ins, j)

            def std(name):
                return feature_job(name, 0, P, h_hi_p, h_lo_p)

            pe.wait_ge(consts_in, 16 * 3)
            pe.wait_ge(const_set, 2)
            for t in range(TT + 1):
                if t < TT:
                    dst = (mixA, mixB)[t % 2]
                    pe.wait_ge(h_ready, t + 1)
                    if t >= 2:
                        pe.wait_ge(h_split, t - 1)
                    for k in range(KD):
                        ins = nc.tensor.transpose(dst[:, k * P:(k + 1) * P], F(PG_H + t % 2, k * P, P), ident[:, :])
                    ins.then_inc(h_turned, 1)
                if t >= 1:
                    pe.wait_ge(h_split, t)
                    value_job("vhg", t - 1)

            for name in (("q", 0), ("f", 0)):
                for _ in std(name):
                    pass

            def hg_step(n, i):
                par = n % 2
                if i < 2:
                    pe.wait_ge(kd_ready, n + 1)
                    if n:
                        pe.wait_ge(rs_ready, 2 * (n - 1) + i + 1)
                    for c in range(4 * i, 4 * i + 4):
                        ins = nc.tensor.transpose(bankM[i][:, (c % 4) * P:(c % 4 + 1) * P],
                                                  F(PG_T2, c * P, P), ident[:, :])
                    ins.then_inc(kt_turned, 1)
                elif i < 18:
                    hl = i - 2
                    lv, hf = hl // 2, hl % 2
                    if lv < LEVELS - 1:
                        pe.wait_ge(ab_ready, 14 * n + hl + 1)
                        base = PG_AB + (hl % 4) // 2
                        lhs = rhs = F(base, (hl % 2) * HALF, HALF)
                    else:
                        pe.wait_ge(q_ready, n + 1)
                        lhs, rhs = F(PG_HK + par, hf * HALF, HALF), F(PG_HQ + par, hf * HALF, HALF)
                    if lv == 0:
                        pe.wait_ge(kt_done, 2 * n + hf + 1)
                    else:
                        pe.wait_ge(pred_done, 16 * n + hl - 1)
                    for c in range(4):
                        ins = mm(bankM[hf][:, c * P:(c + 1) * P], lhs[:, c * P:(c + 1) * P],
                                 rhs[:, c * P:(c + 1) * P], start=True, stop=True)
                    ins.then_inc(lvl_done, 1)
                elif i < 20:
                    u = i - 18
                    pe.wait_ge(pred_done, 16 * n + 14 + u + 1)
                    pe.wait_ge(kt_done, 2 * n + u + 1)
                    pe.wait_ge(v_ready, TT)
                    for c in range(4 * u, min(4 * u + 4, TT - 1)):
                        ins = mm(bankM[u][:, (c % 4) * P:(c % 4 + 1) * P], F(PG_KT, c * P, P),
                                 vtile(PG_VHG, c)[:, n * P:(n + 1) * P], start=True, stop=True)
                    ins.then_inc(upd_done, 1)
                elif i < 22:
                    hf = i - 20
                    pe.wait_ge(st_ready, 2 * n + hf + 1)
                    pe.wait_ge(qe_ready, n + 1)
                    pe.wait_ge(pred_done, 16 * n + 16)
                    for c in range(4 * hf, 4 * hf + 4):
                        o = bankM[2 + hf][:, (c % 4) * P:(c % 4 + 1) * P]
                        ins = mm(o, vtile(PG_VHG, c)[:, n * P:(n + 1) * P], F(PG_S, c * P, P),
                                 start=True, stop=c == 0)
                        if c:
                            ins = mm(o, F(PG_ST, c * P, P), F(PG_T1, c * P, P), start=False, stop=True)
                    ins.then_inc(o_done, 1)
                else:
                    hf = i - 22
                    pe.wait_ge(sq_done, 2 * n + hf + 1)
                    mm(bankM[hf], mean_w[:, :], F(PG_T3, hf * HALF, HALF), start=True,
                       stop=True).then_inc(rms_done, 1)

            def dense_stream(names):
                for name in names:
                    yield from std(name)

            stream = dense_stream([("g", 0), ("q", 1), ("f", 1), ("g", 1), ("q", 2), ("f", 2), ("g", 2),
                                   ("q", 3), ("f", 3), ("g", 3), ("fq", 0), ("fk", 0), ("gx", 0)])
            for step in range(8 + 24 * NHG):
                next(stream)
                if step >= 8:
                    hg_step(*divmod(step - 8, 24))
            for _ in stream:
                pass
            for _ in std(("crow",)):
                pass
            for t in range(TT):
                value_job("vfx", t)

            def scores(G):
                n, e, i = G // 16, (G // 8) % 2, G % 8
                lo = 64 * e
                pe.wait_ge(fk_ready, n + 1)
                pe.wait_ge(fq_ready, n + 1)
                if G:
                    pe.wait_ge(x_ready, G)
                else:
                    pe.wait_ge(y_done, 2 * NHG)
                if G >= 18:
                    pe.wait_ge(yb_done, (G - 18) // 16 + 1)
                q = F(PG_FQ + n % 2, i * P, P)[lo:lo + 64, :]
                k = F(PG_FK + n % 2)[lo:lo + 64, :]
                L = (i + 1) * P
                if L > HALF:
                    mm(mixA[:, 0:HALF], q, k[:, 0:HALF], start=True, stop=True)
                at = HALF if L > HALF else 0
                mm(mixA[:, at:L], q, k[:, at:L], start=True, stop=False)
                mm(mixA[:, L - P:L], identb[:, :], causal[:, :], start=False, stop=True,
                   ).then_inc(qk_done, 1)

            def turn_probs(G):
                i = G % 8
                pe.wait_ge(p_ready, G + 1)
                if G:
                    pe.wait_ge(pt_done, G)
                    pe.wait_ge(o_ready, G)
                for j in range(i + 1):
                    ins = nc.tensor.transpose(mixB[:, j * P:(j + 1) * P], F(PG_XP + G % 2, j * P, P), ident[:, :])
                ins.then_inc(p_turned, 1)

            def weigh_values(G):
                i, hh = G % 8, G // 8
                pe.wait_ge(pt_done, G + 1)
                for j in range(i + 1):
                    ins = mm(mixB[:, HALF:HALF + 64], F(PG_PT, j * P, P),
                             vtile(PG_VFX, j)[:, 64 * hh:64 * hh + 64], start=j == 0, stop=j == i)
                ins.then_inc(pv_done, 1)

            def turn_outputs(n):
                pe.wait_ge(o_ready, 16 * (n + 1))
                pe.wait_ge(x_ready, min(16 * (n + 1) + 2, 64))
                for i in range(TT):
                    ins = nc.tensor.transpose(mixA[:, i * P:(i + 1) * P], F(PG_O, i * P, P), ident[:, :])
                ins.then_inc(ot_done, 1)

            pe.wait_ge(v_ready, 2 * TT)
            stream = dense_stream([(x, n) for n in range(1, NPAIR) for x in ("fq", "fk")]
                                  + [("gx", i) for i in range(1, 16)])
            for G in range(16 * NPAIR + 3):
                if G >= 18 and (G - 18) % 16 == 0:
                    turn_outputs((G - 18) // 16)
                if G < 64:
                    scores(G)
                if 2 <= G < 66:
                    weigh_values(G - 2)
                next(stream)
                if 1 <= G < 65:
                    turn_probs(G - 1)
            for _ in stream:
                pass

            for m in range(KD):
                for name, hi, lo, first in (("A", PG_YAH, PG_YAL, 0), ("B", PG_YBH, PG_YBL, 4)):
                    for _ in feature_job((name, m), first * P, P, [R(hi + k) for k in range(4)],
                                         [R(lo + k) for k in range(4)],
                                         (y_split, lambda k: first + k + 1) if m == 0 else None):
                        pass

            for m in range(KD):
                for _ in feature_job(("mix", m), 0, P, [R(i) for i in PG_GA], [R(i) for i in PG_GB],
                                     (m_split, lambda k: k + 1) if m == 0 else None):
                    pass
                if m == 5:
                    pe.wait_ge(pe_in, 16)
                    pe.wait_ge(yb_done, NPAIR)
                    for k in range(2):
                        for t in range(TT):
                            ins = nc.tensor.transpose(
                                (mixA, mixB)[k][:, t * P:(t + 1) * P],
                                F(PG_PRAW + t // 4, (t % 4) * PLE + k * P, P),
                                ident[:, :])
                        ins.then_inc(pe_turned, 1)

            def turn_mix(t):
                pe.wait_ge(mix_ready, KD)
                if t:
                    pe.wait_ge(r_done, t)
                else:
                    pe.wait_ge(pe_split, 1)
                for k in range(KD):
                    ins = nc.tensor.transpose(mixA[:, k * P:(k + 1) * P], F(PG_MIX + k, t * P, P), ident[:, :])
                ins.then_inc(mt_turned, 1)

            def turn_h1(t):
                pe.wait_ge(h1_ready, t + 1)
                if t:
                    pe.wait_ge(h1_split, t)
                for k in range(KD):
                    ins = nc.tensor.transpose(mixB[:, k * P:(k + 1) * P], F(PG_R + t % 2, k * P, P), ident[:, :])
                ins.then_inc(h1_turned, 1)

            def emb_job(m):
                for _ in feature_job(("pw", m), (m % 4) * P, HALF, [R(PG_PTH + k) for k in range(2)],
                                     [R(PG_PTL + k) for k in range(2)], (pe_split, lambda k: 2) if m == 0 else None):
                    pass

            turn_mix(0)
            for t in range(TT):
                emb_job(t)
                if t + 1 < TT:
                    turn_mix(t + 1)
                turn_h1(t)

            h1_hi_p = [R(PG_H1H + k) for k in range(KD)]
            h1_lo_p = [R(PG_H1L + k) for k in range(KD)]
            pe.wait_ge(h1_split, TT)
            for m in range(KD):
                for _ in feature_job(("pg", m), 0, P, h1_hi_p, h1_lo_p):
                    pass

            for g in range(NG):
                for m in range(4):
                    for _ in feature_job(("ff1", 4 * g + m), 0, P, h1_hi_p, h1_lo_p):
                        pass
                for m in range(KD):
                    for _ in feature_job(("ff2", 8 * g + m), (m % 2) * P, 256,
                                         [R(PG_ACTH + k) for k in range(4)], [R(PG_ACTL + k) for k in range(4)],
                                         (act_split, lambda k: 4 * g + k + 1) if m == 0 else None):
                        pass

            pe.wait_ge(acc_done, NG * KD)
            for t in range(TT):
                if t >= 2:
                    pe.wait_ge(fin_ready, t - 1)
                else:
                    pe.wait_ge(h1_split, TT)
                for k in range(KD):
                    ins = nc.tensor.transpose((mixA, mixB)[t % 2][:, k * P:(k + 1) * P],
                                              F(PG_ACC[k], t * P, P), ident[:, :])
                ins.then_inc(fin_turned, 1)

        @block.scalar
        def _(act):
            A = nc.scalar.activation
            nc.scalar.preload_act_table_set("natural_log_exp_and_others")
            for t in range(2):
                act.dma_start(F(PG_X + t), x_t[t]).then_inc(x_in[t], 16)
            act.dma_start(F(PG_G0), row(ln0_g)).then_inc(rows_in, 16)
            act.dma_start(F(PG_B0), row(ln0_b)).then_inc(rows_in, 16)
            act.dma_start(ident[:, :], c_ident).then_inc(consts_in, 16)
            for t in range(2, TT):
                act.dma_start(F(PG_X + t), x_t[t]).then_inc(x_in[t], 16)
            act.dma_start(F(PG_T3, 0, P), c_causal).then_inc(consts_in, 16)
            act.dma_start(F(PG_T2), c_masks.rearrange("q a n -> q (a n)")).then_inc(consts_in, 16)
            with nc.allow_non_contiguous_dma(reason="a few hundred words, once"):
                for i in range(2):
                    act.dma_start(lbl[:, i, :], hg_lb[i].rearrange("(h q) -> q h", q=P)).then_inc(cols_in, 16)
                act.dma_start(ng[:, :], hg_norm_g[0].rearrange("(h q) -> q h", q=P)).then_inc(cols_in, 16)
                act.dma_start(fb[0:NFX, :], fox_fb.rearrange("a h -> h a")).then_inc(cols_in, 16)
            act.wait_ge(lb_mx, 1)
            A(lbt[:, 2:4, :], lbt[:, 0:2, :], ACT.Exp).then_inc(lb_exp, 1)

            act.wait_ge(const_set, 4)

            def rstd_estimate(tile):
                i = tile % 2
                act.wait_ge(var_ready, tile + 1)
                A(rstd[:, i, 0:1], mv[:, i, 1:2], ACT.Ln, bias=eps[:, 0:1]).then_inc(act_step, 1)
                act.wait_ge(act_step, tile + 1)
                A(rstd[:, i, 0:1], rstd[:, i, 0:1], ACT.Exp, scale=-0.5).then_inc(rs_est, 1)

            x_hi_all = R(XHI, 0, KD * 1024).rearrange("q (k n) -> q k n", k=KD)

            def store_values(page, name, t, count):
                done(act, name, t)
                nc.scalar.copy(vtile(page, t), dense[JOB[name, t] % 2][:, 0:HG]).then_inc(v_ready, 1)

            rstd_estimate(0)
            for t in range(TT + 1):
                if t + 1 < TT:
                    rstd_estimate(t + 1)
                if t < TT:
                    act.wait_ge(h_turned, t + 1)
                    nc.scalar.copy(x_hi_all[:, :, t * P:(t + 1) * P],
                                   (mixA, mixB)[t % 2][:, :].rearrange("q (k n) -> q k n", k=KD)).then_inc(h_hi, 1)
                    act.dma_start(h_scratch[t], F(PG_H + t % 2)).then_inc(h_stored[t % 2], 16)
                if t >= 1:
                    store_values(PG_VHG, "vhg", t - 1, 0)

            def neg_exp(page, sem_, *name):
                done(act, *name)
                A(F(page), dense[JOB[name] % 2][:, :], ACT.Exp, scale=-1.0).then_inc(sem_, 1)

            def sigmoid(page, sem_, *name):
                done(act, *name)
                A(F(page), dense[JOB[name] % 2][:, :], ACT.Sigmoid).then_inc(sem_, 1)

            def f_part(n):
                par = n % 2
                if n >= 2:
                    act.wait_ge(y_done, 2 * (n - 1))
                neg_exp(PG_HB + par, f_exp, "f", n)
                act.wait_ge(f_ready, n + 1)
                A(F(PG_HB + par), F(PG_HB + par), ACT.Ln).then_inc(f_log, 1)

            def kd_part(n):
                par = n % 2
                act.wait_ge(kd_sub, n + 1)
                A(eb_last[:, par, :], F(PG_HB + par)[:, P - 1::P], ACT.Exp)
                A(F(PG_T2), F(PG_T2), ACT.Exp).then_inc(kd_exp, 1)

            def eb_part(n):
                act.wait_ge(b_ready, n + 1)
                if n:
                    act.wait_ge(o_done, 2 * n)
                A(F(PG_T1), F(PG_HB + n % 2), ACT.Exp).then_inc(eb_exp, 1)

            def gate_part(n):
                if n:
                    act.wait_ge(y_done, 2 * n)
                neg_exp(PG_GATE, g_exp, "g", n)

            def scaled_copy(page, sem_, scale, *name):
                done(act, *name)
                nc.scalar.mul(F(page), dense[JOB[name] % 2][:, :], scale).then_inc(sem_, 1)

            neg_exp(PG_HQ, q_exp, "q", 0)
            f_part(0)
            kd_part(0)
            for n in range(NHG):
                eb_part(n)
                gate_part(n)
                for hl in range(14):
                    act.wait_ge(ab_sub, 14 * n + hl + 1)
                    ab = F(PG_AB + (hl % 4) // 2, (hl % 2) * HALF, HALF)
                    A(ab, ab, ACT.Exp).then_inc(ab_exp, 1)
                    if hl < 2:
                        act.wait_ge(kt_turned, 2 * n + hl + 1)
                        nc.scalar.copy(F(PG_KT, hl * HALF, HALF), bankM[hl]).then_inc(kt_done, 1)
                    if hl == 8:
                        if n < NHG - 1:
                            if n >= 1:
                                act.wait_ge(y_done, 2 * n)
                            neg_exp(PG_HQ + (n + 1) % 2, q_exp, "q", n + 1)
                        else:
                            scaled_copy(PG_FQ, fq_ready, 0.125, "fq", 0)
                if n < NHG - 1:
                    f_part(n + 1)
                    kd_part(n + 1)
                else:
                    scaled_copy(PG_FK, fk_ready, 1.0, "fk", 0)
                for hf in range(2):
                    act.wait_ge(o_done, 2 * n + hf + 1)
                    A(F(PG_T3, hf * HALF, HALF), bankM[2 + hf], ACT.Square).then_inc(sq_done, 1)
                for hf in range(2):
                    t3 = F(PG_T3, hf * HALF, HALF)
                    act.wait_ge(rms_done, 2 * n + hf + 1)
                    A(t3, bankM[hf], ACT.Ln, bias=eps[:, 1:2]).then_inc(rms_log, 1)
                    act.wait_ge(rms_log, 2 * n + hf + 1)
                    A(t3, t3, ACT.Exp, scale=-0.5).then_inc(rs_ready, 1)
            neg_exp(PG_GA[0], gx_exp, "gx", 0)

            tmp = F(PG_XP)[0:NFX, :]
            act.wait_ge(c_abs, 1)
            A(tmp, tmp, ACT.Exp, scale=-1.0).then_inc(c_exp, 1)
            act.wait_ge(c_exp, 1)
            A(tmp, tmp, ACT.Ln, bias=1.0).then_inc(c_log, 1)
            for t in range(TT):
                store_values(PG_VFX, "vfx", t, 8)

            G_PAGES = PG_GA + PG_GB
            for G in range(16 * NPAIR + 3):
                if G >= 18 and (G - 18) % 16 == 0:
                    n = (G - 18) // 16
                    act.wait_ge(ot_done, n + 1)
                    nc.scalar.copy(F(PG_YB + n), mixA[:, :]).then_inc(yb_done, 1)
                if G < 64:
                    L = (G % 8 + 1) * P
                    act.wait_ge(nmx_ready, G + 1)
                    x_ = F(PG_XP + G % 2, 0, L)
                    if G >= 4:
                        act.wait_ge(rinv_ready, G - 3)
                    A(x_, x_, ACT.Exp, bias=nmx[:, G % 2, :], accum_out=psm[:, G % 4, :]).then_inc(p_ready, 1)
                if 1 <= G < 65:
                    L = ((G - 1) % 8 + 1) * P
                    act.wait_ge(p_turned, G)
                    if G >= 2:
                        act.wait_ge(pv_done, G - 1)
                    nc.scalar.copy(F(PG_PT, 0, L), mixB[:, 0:L]).then_inc(pt_done, 1)
                if G % 16 == 8 or (G % 16 == 15):
                    n = G // 16 + 1
                    first = G % 16 == 8
                    if n < NPAIR:
                        if first:
                            scaled_copy(PG_FQ + n % 2, fq_ready, 0.125, "fq", n)
                        else:
                            scaled_copy(PG_FK + n % 2, fk_ready, 1.0, "fk", n)
                    elif n == NPAIR:
                        i = 1 if first else 2
                        neg_exp(G_PAGES[i], gx_exp, "gx", i)
            for i in range(3, 16):
                sigmoid(G_PAGES[i], gx_exp, "gx", i)

            done(act, "gx", 15)
            for k in range(4):
                nc.scalar.copy(R(PG_YAH + k), F(PG_YA + k)).then_inc(y_hi, 1)
            for k in range(4):
                nc.scalar.copy(R(PG_YBH + k), F(PG_YB + k)).then_inc(y_hi, 1)
            for m in range(KD):
                act.wait_ge(m_sum, m + 1)
                nc.scalar.copy(R(PG_GA[m]), F(PG_M1 + 2 * (m % 2))).then_inc(m_hi, 1)

            def pe_parts():
                for k in range(2):
                    act.wait_ge(pe_turned, k + 1)
                    nc.scalar.copy(R(PG_PTH + k), (mixA, mixB)[k][:, :]).then_inc(pe_hi, 1)

            for m in range(KD):
                scaled_copy(PG_MIX + m, mix_ready, 1.0, "mix", m)
                if m == 5:
                    pe_parts()
            h1_hi_all = R(PG_H1H, 0, KD * 1024).rearrange("q (k n) -> q k n", k=KD)
            for t in range(TT):
                rstd_estimate(TT + t)
                scaled_copy(PG_ACC[t], pw_ready, 1.0, "pw", t)
                act.wait_ge(h1_turned, t + 1)
                nc.scalar.copy(h1_hi_all[:, :, t * P:(t + 1) * P],
                               mixB[:, :].rearrange("q (k n) -> q k n", k=KD)).then_inc(h1_hi, 1)
            for m in range(KD):
                if m >= 2:
                    act.wait_ge(acc_init, m - 1)
                sigmoid(PG_SG[m % 2], pg_done, "pg", m)
            for i in range(4 * NG):
                done(act, "ff1", i)
                if i >= 2:
                    act.wait_ge(act_split, i - 1)
                A(F(PG_RELU[i % 2]), dense[JOB["ff1", i] % 2][:, :], ACT.Relu).then_inc(relu_done, 1)
                act.wait_ge(act_sq, i + 1)
                nc.scalar.copy(R(PG_ACTH + i % 4), F(PG_RELU[i % 2])).then_inc(act_hi, 1)
            for t in range(TT):
                rstd_estimate(2 * TT + t)

        @block.vector
        def _(dve):
            V = nc.vector
            count = [0]

            def then(ins):
                count[0] += 1
                ins.then_inc(dve_step, 1)
                dve.wait_ge(dve_step, count[0])

            V.memset(ones[:, :], 1.0).then_inc(const_set, 1)
            V.memset(mean_w[:, :], 1.0 / P).then_inc(const_set, 1)
            V.memset(eps[:, 0:1], LN_EPS).then_inc(const_set, 1)
            V.memset(eps[:, 1:2], RMS_EPS).then_inc(const_set, 1)
            dve.wait_ge(cols_in, 64)
            then(V.tensor_tensor(lbt[:, 2, :], lbl[:, 0, :], lbl[:, 1, :], ALU.max))
            V.tensor_tensor(lbt[:, 0, :], lbl[:, 0, :], lbt[:, 2, :], ALU.subtract)
            V.tensor_tensor(lbt[:, 1, :], lbl[:, 1, :], lbt[:, 2, :], ALU.subtract).then_inc(lb_mx, 1)
            dve.wait_ge(lb_exp, 1)
            then(V.tensor_tensor(lbt[:, 0, :], lbt[:, 2, :], lbt[:, 3, :], ALU.add))
            then(V.reciprocal(lbt[:, 1, :], lbt[:, 0, :]))
            then(V.tensor_tensor(lb[:, :], lbt[:, 2, :], lbt[:, 1, :], ALU.mult))
            then(V.tensor_scalar(omlb[:, :], lb[:, :], -1.0, 1.0, ALU.mult, ALU.add))

            def norm_stats(src, i):
                V.bn_stats(stats[:, i, 0, :], src[:, 0:HALF])
                then(V.bn_stats(stats[:, i, 1, :], src[:, HALF:]))
                V.bn_aggr(mv[:, i, :], stats[:, i, :, :]).then_inc(var_ready, 1)

            def norm_apply(dst, src, i, g, b, tile):
                est, work, res = (rstd[:, i, j:j + 1] for j in range(3))
                dve.wait_ge(var_ready, tile + 1)
                then(V.scalar_tensor_tensor(out=dst, in0=src, scalar=mv[:, i, 0:1], in1=g,
                                            op0=ALU.subtract, op1=ALU.mult))
                dve.wait_ge(rs_est, tile + 1)
                then(V.tensor_tensor(work, est, est, ALU.mult))
                then(V.scalar_tensor_tensor(out=work, in0=mv[:, i, 1:2], scalar=LN_EPS, in1=work,
                                            op0=ALU.add, op1=ALU.mult))
                then(V.tensor_scalar(work, work, -0.5, 1.5, ALU.mult, ALU.add))
                then(V.tensor_tensor(res, est, work, ALU.mult))
                return V.scalar_tensor_tensor(out=dst, in0=dst, scalar=res, in1=b,
                                              op0=ALU.mult, op1=ALU.add)

            def low_part(lo_all, hi_all, src, t):
                cols = slice(t * P, (t + 1) * P)
                return V.tensor_tensor(lo_all[:, :, cols], src[:, :].rearrange("q (k n) -> q k n", k=KD),
                                       hi_all[:, :, cols].bitcast(F32), ALU.subtract)

            all8 = lambda page: R(page, 0, KD * 1024).rearrange("q (k n) -> q k n", k=KD)
            for t in range(-1, TT + 1):
                if t + 1 < TT:
                    dve.wait_ge(x_in[t + 1], 16)
                    norm_stats(F(PG_X + t + 1), (t + 1) % 2)
                if 0 <= t < TT:
                    if t == 0:
                        dve.wait_ge(rows_in, 32)
                    if t >= 2:
                        dve.wait_ge(h_turned, t - 1)
                        dve.wait_ge(h_stored[t % 2], 16 * (t // 2))
                    norm_apply(F(PG_H + t % 2), F(PG_X + t), t % 2, F(PG_G0), F(PG_B0), t).then_inc(h_ready, 1)
                if t >= 1:
                    dve.wait_ge(h_hi, t)
                    low_part(all8(XLO), all8(XHI), (mixA, mixB)[(t - 1) % 2], t - 1).then_inc(h_split, 1)
            for i in range(2):
                dve.wait_ge(h_stored[i], 16 * (TT // 2))
            dve.wait_ge(consts_in, 48)
            V.tensor_copy(identb[:, :], ident[:, :])
            V.tensor_copy(causal[:, :], F(PG_T3, 0, P))
            then(V.tensor_copy(masks[:, :, :], F(PG_T2).rearrange("q (a n) -> q a n", n=P)))
            then(V.memset(F(PG_S), 0.0))

            def sigmoid_from_exp(ap):
                then(V.tensor_scalar(ap, ap, 1.0, None, ALU.add))
                then(V.reciprocal(ap, ap))

            def q_part(n):
                q = F(PG_HQ + n % 2)
                dve.wait_ge(q_exp, n + 1)
                sigmoid_from_exp(q)
                V.tensor_tensor(q, dense[JOB["q", n] % 2][:, :], q, ALU.mult).then_inc(q_ready, 1)

            def f_part(n):
                b, k = F(PG_HB + n % 2), F(PG_HK + n % 2)
                dve.wait_ge(f_exp, n + 1)
                sigmoid_from_exp(b)
                then(V.tensor_scalar(b, b, omlb[:, n:n + 1], lb[:, n:n + 1], ALU.mult, ALU.add))
                then(V.tensor_scalar(k, b, -1.0, 1.0, ALU.mult, ALU.add))
                V.tensor_scalar(b, b, F_FLOOR, None, ALU.max).then_inc(f_ready, 1)

            def decay_part(n):
                b = F(PG_HB + n % 2)
                dve.wait_ge(f_log, n + 1)
                for c in range(TT):
                    ins = V.tensor_tensor_scan(b[:, c * P:(c + 1) * P], ones[:, :], b[:, c * P:(c + 1) * P],
                                               0.0, ALU.mult, ALU.add)
                ins.then_inc(b_ready, 1)
                dve.wait_ge(b_ready, n + 1)
                bt = b.rearrange("q (c n) -> q c n", n=P)
                if n:
                    dve.wait_ge(kt_turned, 2 * n)
                V.tensor_tensor(F(PG_T2).rearrange("q (c n) -> q c n", n=P),
                                bt[:, :, P - 1:P].to_broadcast([P, TT, P]), bt, ALU.subtract).then_inc(kd_sub, 1)

            def kd_part(n):
                dve.wait_ge(kd_exp, n + 1)
                V.tensor_tensor(F(PG_T2), F(PG_T2), F(PG_HK + n % 2), ALU.mult).then_inc(kd_ready, 1)

            def gate_part(n):
                g = F(PG_GATE)
                dve.wait_ge(g_exp, n + 1)
                sigmoid_from_exp(g)
                V.scalar_tensor_tensor(out=g, in0=dense[JOB["g", n] % 2][:, :], scalar=ng[:, n:n + 1], in1=g,
                                       op0=ALU.mult, op1=ALU.mult).then_inc(gate_ready, 1)

            def level_views(page, off, m):
                v = F(page, off, HALF).rearrange("q (a n) -> q a n", n=2 * m)
                return v[:, :, 0:m], v[:, :, m:2 * m], v[:, :, m - 1:m]

            def level_sub(n, hl):
                m, hf = 64 >> (hl // 2), hl % 2
                early, late, mid = level_views(PG_HB + n % 2, hf * HALF, m)
                to_early, to_late, _ = level_views(PG_AB + (hl % 4) // 2, (hl % 2) * HALF, m)
                if hl >= 4:
                    dve.wait_ge(lvl_done, 16 * n + hl - 3)
                mid = mid.to_broadcast([P, HALF // (2 * m), m])
                V.tensor_tensor(to_early, mid, early, ALU.subtract)
                V.tensor_tensor(to_late, late, mid, ALU.subtract).then_inc(ab_sub, 1)

            def level_mul(n, hl):
                m, hf = 64 >> (hl // 2), hl % 2
                early, late, _ = level_views(PG_AB + (hl % 4) // 2, (hl % 2) * HALF, m)
                k = level_views(PG_HK + n % 2, hf * HALF, m)[0]
                q = level_views(PG_HQ + n % 2, hf * HALF, m)[1]
                dve.wait_ge(ab_exp, 14 * n + hl + 1)
                V.tensor_tensor(early, early, k, ALU.mult)
                V.tensor_tensor(late, late, q, ALU.mult).then_inc(ab_ready, 1)

            def level_take(n, hl):
                lv, hf = hl // 2, hl % 2
                dve.wait_ge(lvl_done, 16 * n + hl + 1)
                V.copy_predicated(F(PG_S, hf * HALF, HALF).rearrange("q (c n) -> q c n", n=P),
                                  masks[:, lv:lv + 1, :].to_broadcast([P, 4, P]),
                                  bankM[hf].rearrange("q (c n) -> q c n", n=P)).then_inc(pred_done, 1)

            def states(n, u):
                dve.wait_ge(upd_done, 2 * n + u + 1)
                last = min(4 * u + 4, TT - 1) - 1
                for c in range(4 * u, last + 1):
                    new, U = F(PG_ST, (c + 1) * P, P), bankM[u][:, (c % 4) * P:(c % 4 + 1) * P]
                    if c == 0:
                        ins = V.tensor_copy(new, U)
                    else:
                        ins = V.scalar_tensor_tensor(out=new, in0=F(PG_ST, c * P, P),
                                                     scalar=eb_last[:, n % 2, c:c + 1], in1=U,
                                                     op0=ALU.mult, op1=ALU.add)
                    if c < last:
                        then(ins)
                ins.then_inc(st_ready, 1)
                dve.wait_ge(st_ready, 2 * n + u + 1)

            def head_out(n, hf):
                t3 = F(PG_T3, hf * HALF, HALF)
                dve.wait_ge(rs_ready, 2 * n + hf + 1)
                then(V.tensor_tensor(t3, bankM[2 + hf], t3, ALU.mult))
                V.tensor_tensor(F(PG_YA + n, hf * HALF, HALF), t3, F(PG_GATE, hf * HALF, HALF),
                                ALU.mult).then_inc(y_done, 1)

            q_part(0)
            f_part(0)
            decay_part(0)
            kd_part(0)
            for n in range(NHG):
                gate_part(n)
                dve.wait_ge(eb_exp, n + 1)
                dve.wait_ge(q_ready, n + 1)
                V.tensor_tensor(F(PG_T1), F(PG_T1), F(PG_HQ + n % 2), ALU.mult).then_inc(qe_ready, 1)
                for i in range(19):
                    if i < 14:
                        level_sub(n, i)
                    if 1 <= i < 15:
                        level_mul(n, i - 1)
                    if i >= 3:
                        level_take(n, i - 3)
                    if i == 10 and n < NHG - 1:
                        q_part(n + 1)
                    if i == 16 and n < NHG - 1:
                        f_part(n + 1)
                if n < NHG - 1:
                    decay_part(n + 1)
                for u in range(2):
                    states(n, u)
                if n < NHG - 1:
                    kd_part(n + 1)
                for hf in range(2):
                    head_out(n, hf)

            def gate_sigmoid(i):
                g = F((PG_GA + PG_GB)[i])
                dve.wait_ge(gx_exp, i + 1)
                then(V.tensor_scalar(g, g, 1.0, None, ALU.add))
                V.reciprocal(g, g).then_inc(gx_ready, 1)

            gate_sigmoid(0)
            z, tmp = F(PG_CROW)[0:NFX, :], F(PG_XP)[0:NFX, :]
            done(dve, "crow")
            V.tensor_scalar(z, dense[JOB["crow",] % 2][0:NFX, :], fb[0:NFX, :], None, ALU.add).then_inc(c_lin, 1)
            dve.wait_ge(c_lin, 1)
            V.scalar_tensor_tensor(out=tmp, in0=z, scalar=-1.0, in1=z, op0=ALU.mult, op1=ALU.max).then_inc(c_abs, 1)
            dve.wait_ge(c_log, 1)
            then(V.scalar_tensor_tensor(out=z, in0=z, scalar=0.0, in1=tmp, op0=ALU.min, op1=ALU.subtract))
            then(V.memset(tmp, 1.0))
            then(V.tensor_tensor_scan(tmp, tmp, z, 0.0, ALU.mult, ALU.add))
            V.tensor_scalar(z, tmp, -1.0, None, ALU.mult).then_inc(c_ready, 1)

            for G in range(16 * NPAIR + 2):
                if G < 64:
                    hh, L = G // 8, (G % 8 + 1) * P
                    dve.wait_ge(qk_done, G + 1)
                    if G % 8 == 0:
                        dve.wait_ge(negc_in[hh % 2], 16 * (hh // 2 + 1))
                    if G == 0:
                        dve.wait_ge(c_ready, 1)
                    if G >= 2:
                        dve.wait_ge(p_turned, G - 1)
                    V.tensor_tensor_reduce(out=F(PG_XP + G % 2, 0, L), in0=mixA[:, 0:L],
                                           in1=F(PG_NEGC[hh % 2], 0, L), scale=1.0, scalar=-3.0e38,
                                           op0=ALU.add, op1=ALU.max,
                                           accum_out=mx[:, G % 2, :]).then_inc(x_ready, 1)
                    dve.wait_ge(x_ready, G + 1)
                    V.tensor_scalar(nmx[:, G % 2, :], mx[:, G % 2, :], -1.0, None, ALU.mult).then_inc(nmx_ready, 1)
                if G >= 2:
                    g, n, e, i = G - 2, (G - 2) // 16, ((G - 2) // 8) % 2, (G - 2) % 8
                    dve.wait_ge(p_ready, g + 1)
                    V.reciprocal(rinv[:, g % 2, :], psm[:, g % 4, :]).then_inc(rinv_ready, 1)
                    dve.wait_ge(rinv_ready, g + 1)
                    dve.wait_ge(pv_done, g + 1)
                    if g % 16 == 0 and n:
                        dve.wait_ge(ot_done, n)
                    V.tensor_scalar(F(PG_O, i * P + 64 * e, 64), mixB[:, HALF:HALF + 64], rinv[:, g % 2, :], None,
                                    ALU.mult).then_inc(o_ready, 1)
                if G == 60:
                    gate_sigmoid(1)
            gate_sigmoid(2)

            for k in range(8):
                dve.wait_ge(y_hi, k + 1)
                src, hi, lo = ((F(PG_YA + k), PG_YAH + k, PG_YAL + k) if k < 4
                               else (F(PG_YB + k - 4), PG_YBH + k - 4, PG_YBL + k - 4))
                V.tensor_tensor(R(lo), src, R(hi).bitcast(F32), ALU.subtract).then_inc(y_split, 1)
            dve.wait_ge(gx_ready, 3)
            dve.wait_ge(gx_exp, 16)
            for m in range(KD + 1):
                if m < KD:
                    t1, t2 = F(PG_M1 + 2 * (m % 2)), F(PG_M2 + 2 * (m % 2))
                    if m >= 2:
                        dve.wait_ge(m_split, m - 1)
                    done(dve, "A", m)
                    V.tensor_tensor(t1, dense[JOB["A", m] % 2][:, :], F(PG_GA[m]), ALU.mult).then_inc(a_used, 1)
                    done(dve, "B", m)
                    V.tensor_tensor(t2, dense[JOB["B", m] % 2][:, :], F(PG_GB[m]), ALU.mult).then_inc(b_used, 1)
                    dve.wait_ge(b_used, m + 1)
                    V.tensor_tensor(t1, t1, t2, ALU.add).then_inc(m_sum, 1)
                if m >= 1:
                    i = m - 1
                    dve.wait_ge(m_hi, i + 1)
                    V.tensor_tensor(R(PG_GB[i]), F(PG_M1 + 2 * (i % 2)), R(PG_GA[i]).bitcast(F32),
                                    ALU.subtract).then_inc(m_split, 1)
            for k in range(2):
                dve.wait_ge(pe_hi, k + 1)
                V.tensor_tensor(R(PG_PTL + k), (mixA, mixB)[k][:, :], R(PG_PTH + k).bitcast(F32),
                                ALU.subtract).then_inc(pe_split, 1)

            dve.wait_ge(rows1_in, 32)
            for t in range(TT + 1):
                if t < TT:
                    r = F(PG_R + t % 2)
                    dve.wait_ge(hr_in[t % 2], 16 * (t // 2 + 1))
                    dve.wait_ge(mt_turned, t + 1)
                    V.scalar_tensor_tensor(out=r, in0=r, scalar=ALPHA, in1=mixA[:, :], op0=ALU.mult,
                                           op1=ALU.add).then_inc(r_done, 1)
                    dve.wait_ge(r_done, t + 1)
                    norm_stats(r, t % 2)
                    norm_apply(r, r, t % 2, F(PG_G1), F(PG_B1), TT + t).then_inc(h1_ready, 1)
                if t >= 1:
                    dve.wait_ge(h1_hi, t)
                    low_part(all8(PG_H1L), all8(PG_H1H), mixB, t - 1).then_inc(h1_split, 1)

            for m in range(KD):
                sg, acc = F(PG_SG[m % 2]), F(PG_ACC[m])
                dve.wait_ge(pg_done, m + 1)
                dve.wait_ge(pw_ready, m + 1)
                then(V.tensor_tensor(acc, acc, sg, ALU.mult))
                then(V.scalar_tensor_tensor(out=acc, in0=R(PG_H1H + m).bitcast(F32), scalar=ALPHA, in1=acc,
                                            op0=ALU.mult, op1=ALU.add))
                V.scalar_tensor_tensor(out=acc, in0=R(PG_H1L + m).bitcast(F32), scalar=ALPHA, in1=acc,
                                       op0=ALU.mult, op1=ALU.add).then_inc(acc_init, 1)
            dve.wait_ge(acc_init, KD)

            for g in range(NG):
                for m in range(4):
                    i = 4 * g + m
                    r = F(PG_RELU[i % 2])
                    dve.wait_ge(relu_done, i + 1)
                    V.tensor_tensor(r, r, r, ALU.mult).then_inc(act_sq, 1)
                    dve.wait_ge(act_hi, i + 1)
                    V.tensor_tensor(R(PG_ACTL + m), r, R(PG_ACTH + m).bitcast(F32),
                                    ALU.subtract).then_inc(act_split, 1)
                for m in range(KD):
                    j = 8 * g + m
                    acc = F(PG_ACC[m])
                    done(dve, "ff2", j)
                    if j >= KD:
                        dve.wait_ge(acc_done, j - KD + 1)
                    V.tensor_tensor(acc, dense[JOB["ff2", j] % 2][:, :], acc, ALU.add).then_inc(acc_done, 1)

            dve.wait_ge(rows2_in, 32)
            for t in range(TT):
                src = (mixA, mixB)[t % 2][:, :]
                dve.wait_ge(fin_turned, t + 1)
                norm_stats(src, t % 2)
                if t >= 2:
                    dve.wait_ge(out_stored[t % 2], 16 * (t // 2))
                norm_apply(F(PG_OUT + t % 2), src, t % 2, F(PG_G2), F(PG_B2), 2 * TT + t).then_inc(fin_ready, 1)


_INS = ["x", "p", "ln0_g", "ln0_b", "w_in", "hg_lb", "hg_norm_g", "fox_fb", "w_a", "w_b", "w_o", "ln1_g", "ln1_b",
        "w_ff1", "w_ff2", "w_pg", "w_p", "ln2_g", "ln2_b"]


def constants():
    eye = np.eye(P, dtype=np.float32)
    s, t = np.arange(P)[:, None], np.arange(P)[None, :]
    causal = np.where(t > s, -1.0e30, 0.0).astype(np.float32)
    masks = np.zeros((P, LEVELS, P), np.float32)
    for lv in range(LEVELS - 1):
        m = 64 >> lv
        masks[:, lv, :] = (s // (2 * m) == t // (2 * m)) & (s % (2 * m) < m) & (t % (2 * m) >= m)
    masks[:, LEVELS - 1, :] = s == t
    return {"c_ident": eye, "c_causal": causal, "c_masks": masks}


def kernel(**inputs):
    import numpy as _np
    import concourse.bacc as _bacc
    from concourse import mybir as _mybir
    from concourse.bass_utils import run_bass_kernel_spmd as _run

    nc = _bacc.Bacc("TRN2", target_bir_lowering=False, num_devices=1)
    arrays, args = {}, []
    named = [(n, _np.ascontiguousarray(inputs[n])) for n in _INS] + list(constants().items())
    for name, a in named:
        arrays[f"in_{name}"] = a
        args.append(nc.dram_tensor(f"in_{name}", a.shape, _mybir.dt.from_np(a.dtype), kind="ExternalInput").ap())
    args.append(nc.dram_tensor("h_scratch", (TT, P, D), F32).ap())
    args.append(nc.dram_tensor("c_scratch", (NFX, S), F32).ap())
    args.append(nc.dram_tensor("out_h", (1, S, D), F32, kind="ExternalOutput").ap())
    block_kernel(nc, *args)
    r = _run(nc, [arrays], core_ids=[0])
    return r.results[0]["out_h"]
```

```python
from contextlib import ExitStack

import numpy as np

import concourse.bass as bass
from concourse import mybir

F32 = mybir.dt.float32
F32R = mybir.dt.float32r
BF16 = mybir.dt.bfloat16
U8 = mybir.dt.uint8
ALU = mybir.AluOpType
ACT = mybir.ActivationFunctionType

P = 128
S = 1024
D = 1024
KD = D // P
TT = S // P
HALF = 512
HG = 512
NHG = 4
FX = 512
NFX = 8
NPAIR = 4
FF = 4096
PLE = 256
LN_EPS = 1e-5
RMS_EPS = 1e-6
ALPHA = 2.0 ** 0.25
LEVELS = 8
F_FLOOR = 2.0 ** -63

C_HQ, C_HF, C_HI, C_HGATE = 0, 512, 1024, 1536
C_FQ, C_FK, C_FV, C_FF = 2048, 2560, 3072, 3584
C_GA, C_GB = 3592, 4616

CHUNKS = []


def _plan():
    add = CHUNKS.append
    for j in range(4):
        add(("in", C_HI + 128 * j))
    add(("in", C_HF))
    add(("in", C_HQ))
    for n in range(3):
        add(("in", C_HGATE + 128 * n))
        add(("in", C_HQ + 128 * (n + 1)))
        add(("in", C_HF + 128 * (n + 1)))
    add(("in", C_HGATE + 384))
    add(("in", C_FQ))
    add(("in", C_FK))
    add(("in", C_GA))
    add(("in", C_FF))
    for j in range(4):
        add(("in", C_FV + 128 * j))
    for n in range(1, 4):
        add(("in", C_FQ + 128 * n))
        add(("in", C_FK + 128 * n))
    for m in range(1, 8):
        add(("in", C_GA + 128 * m))
    for m in range(8):
        add(("in", C_GB + 128 * m))
    for m in range(8):
        add(("ab", 128 * m))
    for _ in range(2):
        for m in range(8):
            add(("o", 128 * m))
    for m in range(2):
        add(("p", 512 * m))
    for m in range(8):
        add(("pg", 128 * m))
    for g in range(8):
        for m in range(4):
            add(("ff1", 512 * g + 128 * m))
        for m in range(4):
            add(("ff2", 512 * g, 256 * m))


_plan()
C_VHG, C_Q0 = 0, 4
C_VFX = 20
C_AB = 45
C_O = 53
C_PW = 69
C_PG = 71
C_FFN = 79
NG = 8

NPAGES = 50
RAW = 0
SPARE = 2
WHI, WLO = 3, 7
XHI, XLO = 11, 19
PG_X, PG_H, PG_G0, PG_B0 = 27, 36, 38, 39
PG_HQ, PG_HB, PG_HK, PG_GATE = 27, 29, 31, (33, SPARE)
PG_AB, PG_S, PG_KT, PG_ST, PG_T1, PG_T2, PG_T3 = 34, 36, 37, 38, 39, 40, 41
PG_VHG, PG_YA = 42, 46
PG_FQ, PG_FK, PG_CROW, PG_NEGC = 27, 29, 32, (33, 41)
PG_VFX, PG_XP, PG_PT, PG_O, PG_YB = 34, 38, (40, 32), SPARE, 42
PG_GA = [31, 27, 29, 32, 28, 30, 33, 34]
PG_GB = [35, 36, 37, 38, 39, 40, 41, SPARE]
PG_YAH, PG_YAL, PG_YBH, PG_YBL = 11, 15, 19, 23
PG_M1, PG_M2 = 46, 47
PG_MIX = 11
PG_R, PG_G1, PG_B1, PG_PTH, PG_PTL, PG_PRAW = 19, 21, 22, 23, 25, 19
PG_H1H, PG_H1L = 11, 42
PG_ACC = [35, 36, 37, 38, 39, 40, 41, SPARE]
PG_SG = (19, 20)
PG_ACTH, PG_ACTL = 27, 31
PG_RELU, PG_SQ = (21, 22), (25, 26)
PG_OUT, PG_G2, PG_B2 = 19, 23, 24
PG_W0 = 42
BESIDE = {4: (46, 47), 5: (48, 49), 19: (33, 40), 24: (42, 43), 25: (44, 45)}
PARTS, LAST_IN = {}, {}
for _c in range(len(CHUNKS)):
    PARTS[_c] = BESIDE.get(_c, (WHI + _c % 4, WLO + _c % 4))
    LAST_IN[_c] = max([b for b in range(_c) if PARTS[b] == PARTS[_c]], default=None)
HG_LEAD = 12


def block_kernel(nc, x, p, ln0_g, ln0_b, w_in, hg_lb, hg_norm_g, fox_fb, w_a, w_b, w_o, ln1_g, ln1_b,
                 w_ff1, w_ff2, w_pg, w_p, ln2_g, ln2_b, c_ident, c_causal, c_masks,
                 h_scratch, c_scratch, out):
    with ExitStack() as ctx:
        sb = lambda name, shape, dt: ctx.enter_context(nc.sbuf_tensor(name, shape, dt))
        sem = lambda name: ctx.enter_context(nc.semaphore(name))

        def view(name, dt, runs, stack):
            found, page = {}, 0
            while page < NPAGES:
                n = runs.get(page, 1)
                t = stack.enter_context(nc.sbuf_tensor(f"{name}{page}", [P, n * 1024], dt))
                for i in range(n):
                    found[page + i] = (t, i * 1024)
                page += n
            return found

        with ExitStack() as plain:
            f32_pages = view("page", F32, {PG_PRAW: 2}, plain)
        f32r_pages = view("parts", F32R, {WHI: 4, WLO: 4, XHI: 8, XLO: 8, PG_H1L: 8}, ctx)

        def F(page, off=0, n=1024):
            t, at = f32_pages[page + off // 1024]
            return t[:, at + off % 1024:at + off % 1024 + n]

        def R(page, off=0, n=1024):
            t, at = f32r_pages[page]
            return t[:, at + off:at + off + n]

        ident = sb("ident", [P, P], F32)
        ones = sb("ones", [P, P], F32)
        mean_w = sb("mean_w", [P, P], F32)
        identb = sb("identb", [P, P], BF16)
        causal = sb("causal", [P, P], BF16)
        masks = sb("masks", [P, LEVELS, P], U8)
        lbl = sb("lbl", [P, 2, NHG], F32)
        lb = sb("lb", [P, NHG], F32)
        omlb = sb("omlb", [P, NHG], F32)
        lbt = sb("lbt", [P, 4, NHG], F32)
        ng = sb("ng", [P, NHG], F32)
        fb = sb("fb", [P, 1], F32)
        stats = sb("stats", [P, 2, 2, 6], F32)
        mv = sb("mv", [P, 2, 2], F32)
        rstd = sb("rstd", [P, 2, 3], F32)
        eps = sb("eps", [P, 2], F32)
        eb_last = sb("eb_last", [P, 2, TT], F32)
        mx = sb("mx", [P, 2, 1], F32)
        nmx = sb("nmx", [P, 2, 1], F32)
        psm = sb("psm", [P, 4, 1], F32)
        rinv = sb("rinv", [P, 2, 1], F32)

        dense = [ctx.enter_context(nc.psum_tensor(f"dense{i}", [P, 2 * HALF], F32)) for i in range(2)]
        mixA = ctx.enter_context(nc.psum_tensor("mixA", [P, 2 * HALF], F32))
        mixB = ctx.enter_context(nc.psum_tensor("mixB", [P, 2 * HALF], F32))
        bankM = [mixA[:, 0:HALF], mixA[:, HALF:], mixB[:, 0:HALF], mixB[:, HALF:]]

        ident_in, consts_in, rows_in, cols_in = sem("ident_in"), sem("consts_in"), sem("rows_in"), sem("cols_in")
        const_set, lb_mx, lb_exp, lb_ready = sem("const_set"), sem("lb_mx"), sem("lb_exp"), sem("lb_ready")
        x_in = [sem(f"x_in{t}") for t in range(TT)]
        w_landed = [sem(f"w_landed{i}") for i in range(2)]
        w0_landed = [sem(f"w0_landed{i}") for i in range(4)]
        w0_hi, w0_split = sem("w0_hi"), sem("w0_split")
        w_hi, w_split = sem("w_hi"), sem("w_split")
        mm_done = sem("mm_done")
        dve_step, act_step, sig_step, rms_log = sem("dve_step"), sem("act_step"), sem("sig_step"), sem("rms_log")
        var_ready, rs_est = sem("var_ready"), sem("rs_est")
        h_ready, h_turned, h_hi, h_split = sem("h_ready"), sem("h_turned"), sem("h_hi"), sem("h_split")
        h_stored = [sem("h_stored0"), sem("h_stored1")]
        v_ready = sem("v_ready")
        q_exp, q_ready, f_exp, f_ready, f_log, b_ready = (
            sem("q_exp"), sem("q_ready"), sem("f_exp"), sem("f_ready"), sem("f_log"), sem("b_ready"))
        g_exp, gate_ready = sem("g_exp"), sem("gate_ready")
        eb_exp, qe_ready = sem("eb_exp"), sem("qe_ready")
        kd_sub, kd_exp, kd_ready, kt_turned, kt_done = (
            sem("kd_sub"), sem("kd_exp"), sem("kd_ready"), sem("kt_turned"), sem("kt_done"))
        ab_sub, ab_exp, ab_ready, lvl_done, pred_done = (
            sem("ab_sub"), sem("ab_exp"), sem("ab_ready"), sem("lvl_done"), sem("pred_done"))
        upd_done, st_ready, o_done, sq_done, rms_done, rs_ready, y_done = (
            sem("upd_done"), sem("st_ready"), sem("o_done"), sem("sq_done"), sem("rms_done"), sem("rs_ready"), sem("y_done"))
        fq_ready, fk_ready = sem("fq_ready"), sem("fk_ready")
        c_lin, c_abs, c_exp, c_log, c_ready, c_stored = (
            sem("c_lin"), sem("c_abs"), sem("c_exp"), sem("c_log"), sem("c_ready"), sem("c_stored"))
        negc_in = [sem("negc_in0"), sem("negc_in1")]
        qk_done, x_ready, nmx_ready, p_ready, p_turned, pt_done, pv_done, o_ready = (
            sem("qk_done"), sem("x_ready"), sem("nmx_ready"), sem("p_ready"), sem("p_turned"), sem("pt_done"),
            sem("pv_done"), sem("o_ready"))
        rinv_ready = sem("rinv_ready")
        ot_done, yb_done = sem("ot_done"), sem("yb_done")
        gx_exp, gx_ready = sem("gx_exp"), sem("gx_ready")
        y_hi, y_split = sem("y_hi"), sem("y_split")
        a_used, b_used, m_sum, m_hi, m_split = sem("a_used"), sem("b_used"), sem("m_sum"), sem("m_hi"), sem("m_split")
        mix_ready = sem("mix_ready")
        pe_in, pe_turned, pe_hi, pe_split = sem("pe_in"), sem("pe_turned"), sem("pe_hi"), sem("pe_split")
        rows1_in = sem("rows1_in")
        hr_in = [sem("hr_in0"), sem("hr_in1")]
        mt_turned, r_done, h1_ready, h1_turned, h1_hi, h1_split = (
            sem("mt_turned"), sem("r_done"), sem("h1_ready"), sem("h1_turned"), sem("h1_hi"), sem("h1_split"))
        pw_ready, pg_done, acc_init = sem("pw_ready"), sem("pg_done"), sem("acc_init")
        relu_done, act_sq, act_hi, act_split, acc_done = (
            sem("relu_done"), sem("act_sq"), sem("act_hi"), sem("act_split"), sem("acc_done"))
        rows2_in = sem("rows2_in")
        fin_turned, fin_ready = sem("fin_turned"), sem("fin_ready")
        out_stored = [sem("out_stored0"), sem("out_stored1")]

        JOB, FREED, CHUNK_OF, USED_BY, SET, BEFORE = {}, [], [], {}, [], []

        def job(name, chunk, freed, on=None):
            JOB[name] = len(FREED)
            SET.append((1 - SET[-1] if SET else 0) if on is None else on)
            earlier = [j for j in range(len(FREED)) if SET[j] == SET[-1]]
            BEFORE.append(earlier[-1] if earlier else None)
            for c in range(chunk - 3, chunk + 1) if name[0] in ("vhg", "vfx") else (chunk,):
                USED_BY[c] = len(FREED)
            FREED.append(freed)
            CHUNK_OF.append(chunk)

        for t in range(TT):
            job(("vhg", t), C_VHG + 3, (v_ready, t + 1))
        job(("f", 0), 4, (f_exp, 1))
        job(("q", 0), 5, (q_ready, 1))
        for n in range(NHG):
            c = 6 + 3 * n
            job(("g", n), c, (gate_ready, n + 1))
            if n < NHG - 1:
                job(("q", n + 1), c + 1, (q_ready, n + 2))
                job(("f", n + 1), c + 2, (f_exp, n + 2))
        job(("fq", 0), 16, (fq_ready, 1))
        job(("fk", 0), 17, (fk_ready, 1))
        job(("gx", 0), 18, (gx_exp, 1))
        job(("crow",), 19, (c_lin, 1))
        for t in range(TT):
            job(("vfx", t), C_VFX + 3, (v_ready, TT + t + 1))
        for n in range(1, NPAIR):
            job(("fq", n), 22 + 2 * n, (fq_ready, n + 1), on=0)
            job(("fk", n), 23 + 2 * n, (fk_ready, n + 1), on=0)
        for i in range(1, 16):
            job(("gx", i), 29 + i, (gx_exp, i + 1), on=0 if i <= 3 else None)
        for m in range(KD):
            job(("A", m), C_AB + m, (a_used, m + 1))
            job(("B", m), C_AB + m, (b_used, m + 1))
        for h in range(2):
            for m in range(KD):
                job(("mix", h, m), C_O + 8 * h + m, (mix_ready, 8 * h + m + 1))
        for m in range(KD):
            job(("pw", m), C_PW + m // 4, (pw_ready, m + 1))
        for m in range(KD):
            job(("pg", m), C_PG + m, (pg_done, m + 1))
        for g in range(NG):
            for m in range(4):
                job(("ff1", 4 * g + m), C_FFN + 8 * g + m, (relu_done, 4 * g + m + 1))
            if g < NG - 1:
                for m in range(KD):
                    job(("ff2", 8 * g + m), C_FFN + 8 * g + 4 + m // 2, (acc_done, 8 * g + m + 1))
        for h in range(2):
            for m in range(KD):
                job(("last", h, m), C_FFN + 8 * NG - 4 + m // 2, (acc_done, 8 * (NG - 1) + 8 * h + m + 1))

        def out_of(*name):
            return dense[SET[JOB[name]]]

        def o_bank(G):
            return dense[1][:, (G % 2) * HALF:(G % 2) * HALF + 64]

        def done(eng, *name):
            eng.wait_ge(mm_done, JOB[name] + 1)

        kview = lambda w: w.rearrange("a (k p) n -> p (a k) n", p=P)
        w_views = {"in": kview(w_in), "o": kview(w_o), "pg": kview(w_pg), "p": kview(w_p),
                   "ff1": kview(w_ff1), "ff2": kview(w_ff2), "a": kview(w_a), "b": kview(w_b)}
        x_t = x.rearrange("a (t p) d -> (a t) p d", p=P)
        out_t = out.rearrange("a (t p) d -> (a t) p d", p=P)

        def vtile(page, t):
            return F(page + t // 2, (t % 2) * HG, HG)

        def level_views(page, off, m):
            v = F(page, off, HALF).rearrange("q (a n) -> q a n", n=2 * m)
            return v[:, :, 0:m], v[:, :, m:2 * m], v[:, :, m - 1:m]

        def row(vec):
            return vec.partition_broadcast(P)

        block = ctx.enter_context(nc.Block())

        @block.sync
        def _(sp):
            def load_chunk(c):
                kind, at = CHUNKS[c][0], CHUNKS[c][-1]
                if c >= 6:
                    sp.wait_ge(w_split, c - 5)
                page, landed = (PG_W0 + c, w0_landed[c]) if c < 4 else (RAW + c % 2, w_landed[c % 2])
                k4 = [F(page, 0, HALF), F(page, HALF, HALF)]
                if kind == "ab":
                    src = [w_views["a"][:, 0:4, at:at + P], w_views["b"][:, 0:4, at:at + P]]
                elif kind == "p":
                    src = [w_views["p"][:, k, at:at + HALF] for k in range(2)]
                elif kind == "ff2":
                    k0 = 4 * (CHUNKS[c][1] // HALF)
                    src = [w_views["ff2"][:, k0 + 2 * i:k0 + 2 * i + 2, at:at + 256] for i in range(2)]
                else:
                    src = [w_views[kind][:, 4 * i:4 * i + 4, at:at + P] for i in range(2)]
                for dst, s in zip(k4, src):
                    if len(s.shape) == 3:
                        dst = dst.rearrange("q (k n) -> q k n", k=s.shape[1])
                    sp.dma_start(dst, s).then_inc(landed, 16)

            def load_negc(hh):
                if hh >= 2:
                    sp.wait_ge(x_ready, 8 * (hh - 1))
                sp.dma_start(F(PG_NEGC[hh % 2]), row(c_scratch[hh, :])).then_inc(negc_in[hh % 2], 16)

            sp.dma_start(F(PG_X), x_t[0]).then_inc(x_in[0], 16)
            for c in range(len(CHUNKS)):
                load_chunk(c)
                if c == 3:
                    for t in range(4, TT):
                        sp.dma_start(F(PG_X + t), x_t[t]).then_inc(x_in[t], 16)
                if c == 5:
                    sp.dma_start(F(PG_T3, 0, P), c_causal).then_inc(consts_in, 16)
                    sp.dma_start(F(PG_T2), c_masks.rearrange("q a n -> q (a n)")).then_inc(consts_in, 16)
                    with nc.allow_non_contiguous_dma(reason="a few hundred words, once"):
                        for i in range(2):
                            sp.dma_start(lbl[:, i, :], hg_lb[i].rearrange("(h q) -> q h", q=P)).then_inc(cols_in, 16)
                        sp.dma_start(ng[:, :], hg_norm_g[0].rearrange("(h q) -> q h", q=P)).then_inc(cols_in, 16)
                        sp.dma_start(fb[0:NFX, :], fox_fb.rearrange("a h -> h a")).then_inc(cols_in, 16)
                if c == 25:
                    sp.wait_ge(c_ready, 1)
                    sp.dma_start(c_scratch[:, :], F(PG_CROW)[0:NFX, :]).then_inc(c_stored, 16)
                    sp.wait_ge(c_stored, 16)
                    load_negc(0)
                    load_negc(1)
                if 29 <= c < 35:
                    load_negc(c - 27)
                if c == C_O + 4:
                    done(sp, "B", KD - 1)
                    sp.dma_start(F(PG_PRAW, 0, 2048).rearrange("q (t d) -> q t d", d=PLE),
                                 p.rearrange("l a (t q) d -> q (l a t) d", q=P)).then_inc(pe_in, 16)
                    sp.dma_start(F(PG_G1), row(ln1_g[0, :])).then_inc(rows1_in, 16)
                    sp.dma_start(F(PG_B1), row(ln1_b[0, :])).then_inc(rows1_in, 16)
                t = c - (C_O + 13)
                if 0 <= t < TT:
                    if t < 2:
                        sp.wait_ge(pe_turned, 2)
                    else:
                        sp.wait_ge(h1_turned, t - 1)
                    sp.dma_start(F(PG_R + t % 2), h_scratch[t]).then_inc(hr_in[t % 2], 16)
                if c == C_FFN + 8:
                    done(sp, "pw", KD - 1)
                    sp.dma_start(F(PG_G2), row(ln2_g[0, :])).then_inc(rows2_in, 16)
                    sp.dma_start(F(PG_B2), row(ln2_b[0, :])).then_inc(rows2_in, 16)
            for t in range(TT):
                sp.wait_ge(fin_ready, t + 1)
                sp.dma_start(out_t[t], F(PG_OUT + t % 2)).then_inc(out_stored[t % 2], 16)
            for i in range(2):
                sp.wait_ge(out_stored[i], 16 * (TT // 2))
                sp.wait_ge(h_stored[i], 16 * (TT // 2))

        @block.gpsimd
        def _(pool):
            for j in (2, 3):
                pool.wait_ge(w0_hi, j + 1)
                nc.gpsimd.tensor_tensor(R(WLO + j), F(PG_W0 + j), R(WHI + j).bitcast(F32),
                                        ALU.subtract).then_inc(w0_split, 1)
            for c in range(4, len(CHUNKS)):
                hi, lo = PARTS[c]
                pool.wait_ge(w_landed[c % 2], 32 * (c // 2 - 1))
                if LAST_IN[c] is not None:
                    pool.wait_ge(mm_done, USED_BY[LAST_IN[c]] + 1)
                elif c == 19:
                    pool.wait_ge(kt_turned, 2 * NHG)
                    pool.wait_ge(y_done, 2 * (NHG - 1))
                elif c == 24:
                    pool.wait_ge(o_done, 2 * NHG)
                nc.gpsimd.tensor_copy(R(hi), F(RAW + c % 2)).then_inc(w_hi, 1)
                pool.wait_ge(w_hi, c - 3)
                nc.gpsimd.tensor_tensor(R(lo), F(RAW + c % 2), R(hi).bitcast(F32),
                                        ALU.subtract).then_inc(w_split, 1)

        @block.tensor
        def _(pe):
            mm = nc.tensor.matmul

            def three_pass(out2, whi, wlo, xhi2, xlo2, first, last):
                for o, x_ in zip(out2, xhi2):
                    mm(o, whi, x_, start=first, stop=False)
                for o, x_ in zip(out2, xlo2):
                    mm(o, whi, x_, start=False, stop=False)
                for o, x_ in zip(out2, xhi2):
                    ins = mm(o, wlo, x_, start=False, stop=last)
                return ins

            def begin(j):
                if CHUNK_OF[j] < 4:
                    pe.wait_ge(w0_split, 4)
                else:
                    pe.wait_ge(w_split, CHUNK_OF[j] - 3)
                if BEFORE[j] is not None:
                    pe.wait_ge(*FREED[BEFORE[j]])

            def end(ins, j):
                ins.then_inc(mm_done, 1)

            def halves(ap):
                return [ap[:, 0:HALF], ap[:, HALF:2 * HALF]]

            def feature_job(name, col, stride, acts_hi, acts_lo, ready=None, cut=halves):
                j = JOB[name]
                begin(j)
                hi, lo = PARTS[CHUNK_OF[j]]
                out2 = halves(dense[SET[j]][:, :])[:len(cut(acts_hi[0]))]
                K = len(acts_hi)
                for k in range(K):
                    if ready is not None:
                        pe.wait_ge(ready[0], ready[1](k))
                    at = col + k * stride
                    ins = three_pass(out2, R(hi, at, P), R(lo, at, P),
                                     cut(acts_hi[k]), cut(acts_lo[k]), k == 0, k == K - 1)
                    if k == K - 1:
                        end(ins, j)
                    yield

            h_hi_p = [R(XHI + k) for k in range(KD)]
            h_lo_p = [R(XLO + k) for k in range(KD)]

            def value_job(name, t):
                j = JOB[name, t]
                begin(j)
                wide = lambda base, k: R(base, 0, 4096).rearrange(
                    "q (s n) -> q s n", s=4)[:, :, k * P:(k + 1) * P]
                out1 = dense[SET[j]][:, 0:HALF].rearrange("q (s n) -> q s n", s=4)
                for k in range(KD):
                    xh, xl = R(XHI + k, t * P, P), R(XLO + k, t * P, P)
                    mm(out1, xh, wide(WHI, k), start=k == 0, stop=False)
                    mm(out1, xh, wide(WLO, k), start=False, stop=False)
                    ins = mm(out1, xl, wide(WHI, k), start=False, stop=k == KD - 1)
                end(ins, j)

            def std(name):
                return feature_job(name, 0, P, h_hi_p, h_lo_p)

            pe.wait_ge(ident_in, 16)
            pe.wait_ge(const_set, 2)
            for t in range(TT + 1):
                if t < TT:
                    dst = (mixA, mixB)[t % 2]
                    pe.wait_ge(h_ready, t + 1)
                    if t >= 2:
                        pe.wait_ge(h_split, t - 1)
                    for k in range(KD):
                        ins = nc.tensor.transpose(dst[:, k * P:(k + 1) * P], F(PG_H + t % 2, k * P, P), ident[:, :])
                    ins.then_inc(h_turned, 1)
                if t >= 1:
                    pe.wait_ge(h_split, t)
                    value_job("vhg", t - 1)

            for name in (("f", 0), ("q", 0)):
                for _ in std(name):
                    pass

            def hg_step(n, i):
                par = n % 2
                if i < 2:
                    pe.wait_ge(kd_ready, n + 1)
                    if n:
                        pe.wait_ge(rs_ready, 2 * (n - 1) + i + 1)
                    for c in range(4 * i, 4 * i + 4):
                        ins = nc.tensor.transpose(bankM[i][:, (c % 4) * P:(c % 4 + 1) * P],
                                                  F(PG_T2, c * P, P), ident[:, :])
                    ins.then_inc(kt_turned, 1)
                elif i < 18:
                    hl = i - 2
                    lv, hf = hl // 2, hl % 2
                    if lv < LEVELS - 1:
                        pe.wait_ge(ab_ready, 14 * n + hl + 1)
                        base = PG_AB + (hl % 4) // 2
                        lhs = rhs = F(base, (hl % 2) * HALF, HALF)
                    else:
                        pe.wait_ge(q_ready, n + 1)
                        lhs, rhs = F(PG_HK + par, hf * HALF, HALF), F(PG_HQ + par, hf * HALF, HALF)
                    if lv == 0:
                        pe.wait_ge(kt_done, 2 * n + hf + 1)
                    else:
                        pe.wait_ge(pred_done, 16 * n + hl - 1)
                    for c in range(4):
                        ins = mm(bankM[hf][:, c * P:(c + 1) * P], lhs[:, c * P:(c + 1) * P],
                                 rhs[:, c * P:(c + 1) * P], start=True, stop=True)
                    ins.then_inc(lvl_done, 1)
                elif i < 20:
                    u = i - 18
                    pe.wait_ge(pred_done, 16 * n + 14 + u + 1)
                    pe.wait_ge(kt_done, 2 * n + u + 1)
                    pe.wait_ge(v_ready, TT)
                    for c in range(4 * u, min(4 * u + 4, TT - 1)):
                        ins = mm(bankM[u][:, (c % 4) * P:(c % 4 + 1) * P], F(PG_KT, c * P, P),
                                 vtile(PG_VHG, c)[:, n * P:(n + 1) * P], start=True, stop=True)
                    ins.then_inc(upd_done, 1)
                elif i < 22:
                    hf = i - 20
                    pe.wait_ge(st_ready, 2 * n + hf + 1)
                    pe.wait_ge(qe_ready, n + 1)
                    pe.wait_ge(pred_done, 16 * n + 16)
                    for c in range(4 * hf, 4 * hf + 4):
                        o = bankM[2 + hf][:, (c % 4) * P:(c % 4 + 1) * P]
                        ins = mm(o, vtile(PG_VHG, c)[:, n * P:(n + 1) * P], F(PG_S, c * P, P),
                                 start=True, stop=c == 0)
                        if c:
                            ins = mm(o, F(PG_ST, c * P, P), F(PG_T1, c * P, P), start=False, stop=True)
                    ins.then_inc(o_done, 1)
                else:
                    hf = i - 22
                    pe.wait_ge(sq_done, 2 * n + hf + 1)
                    mm(bankM[hf], mean_w[:, :], F(PG_T3, hf * HALF, HALF), start=True,
                       stop=True).then_inc(rms_done, 1)

            def dense_stream(names):
                for name in names:
                    yield from std(name)

            stream = dense_stream([("g", 0), ("q", 1), ("f", 1), ("g", 1), ("q", 2), ("f", 2), ("g", 2),
                                   ("q", 3), ("f", 3), ("g", 3), ("fq", 0), ("fk", 0), ("gx", 0), ("crow",)])
            for step in range(HG_LEAD + 24 * NHG):
                next(stream)
                if step >= HG_LEAD:
                    hg_step(*divmod(step - HG_LEAD, 24))
            for _ in stream:
                pass
            for t in range(TT):
                value_job("vfx", t)

            def scores(G):
                n, e, i = G // 16, (G // 8) % 2, G % 8
                lo = 64 * e
                pe.wait_ge(fk_ready, n + 1)
                pe.wait_ge(fq_ready, n + 1)
                if G:
                    pe.wait_ge(x_ready, G)
                else:
                    pe.wait_ge(y_done, 2 * NHG)
                if G >= 18:
                    pe.wait_ge(yb_done, (G - 18) // 16 + 1)
                q = F(PG_FQ + n % 2, i * P, P)[lo:lo + 64, :]
                k = F(PG_FK + n % 2)[lo:lo + 64, :]
                L = (i + 1) * P
                if L > HALF:
                    mm(mixA[:, 0:HALF], q, k[:, 0:HALF], start=True, stop=True)
                at = HALF if L > HALF else 0
                mm(mixA[:, at:L], q, k[:, at:L], start=True, stop=False)
                mm(mixA[:, L - P:L], identb[:, :], causal[:, :], start=False, stop=True,
                   ).then_inc(qk_done, 1)

            def turn_probs(G):
                i = G % 8
                pe.wait_ge(p_ready, G + 1)
                if G:
                    pe.wait_ge(pt_done, G)
                for j in range(i + 1):
                    ins = nc.tensor.transpose(mixB[:, j * P:(j + 1) * P], F(PG_XP + G % 2, j * P, P), ident[:, :])
                ins.then_inc(p_turned, 1)

            def weigh_values(G):
                i, hh = G % 8, G // 8
                pe.wait_ge(pt_done, G + 1)
                if G >= 2:
                    pe.wait_ge(o_ready, G - 1)
                for j in range(i + 1):
                    ins = mm(o_bank(G), F(PG_PT[G % 2], j * P, P),
                             vtile(PG_VFX, j)[:, 64 * hh:64 * hh + 64], start=j == 0, stop=j == i)
                ins.then_inc(pv_done, 1)

            def turn_outputs(n):
                pe.wait_ge(o_ready, 16 * (n + 1))
                pe.wait_ge(x_ready, min(16 * (n + 1) + 2, 64))
                for i in range(TT):
                    ins = nc.tensor.transpose(mixA[:, i * P:(i + 1) * P], F(PG_O, i * P, P), ident[:, :])
                ins.then_inc(ot_done, 1)

            pe.wait_ge(v_ready, 2 * TT)
            stream = dense_stream([(x, n) for n in range(1, NPAIR) for x in ("fq", "fk")]
                                  + [("gx", i) for i in range(1, 16)])
            next(stream)
            for G in range(16 * NPAIR + 3):
                if G >= 18 and (G - 18) % 16 == 0:
                    turn_outputs((G - 18) // 16)
                if G < 64:
                    scores(G)
                if 1 <= G < 65:
                    turn_probs(G - 1)
                if 2 <= G < 66:
                    weigh_values(G - 2)
                next(stream)
            for _ in stream:
                pass

            for m in range(KD):
                for name, hi, lo, first in (("A", PG_YAH, PG_YAL, 0), ("B", PG_YBH, PG_YBL, 4)):
                    for _ in feature_job((name, m), first * P, P, [R(hi + k) for k in range(4)],
                                         [R(lo + k) for k in range(4)],
                                         (y_split, lambda k: first + k + 1) if m == 0 else None):
                        pass

            def turn_embeddings():
                pe.wait_ge(pe_in, 16)
                pe.wait_ge(yb_done, NPAIR)
                for k in range(2):
                    for t in range(TT):
                        ins = nc.tensor.transpose((mixA, mixB)[k][:, t * P:(t + 1) * P],
                                                  F(PG_PRAW + t // 4, (t % 4) * PLE + k * P, P), ident[:, :])
                    ins.then_inc(pe_turned, 1)

            def turn_mix(t):
                pe.wait_ge(mix_ready, KD * (1 + t // 4))
                if t:
                    pe.wait_ge(r_done, t)
                else:
                    pe.wait_ge(pe_split, 1)
                for k in range(KD):
                    ins = nc.tensor.transpose(mixA[:, k * P:(k + 1) * P], F(PG_MIX + k, t * P, P), ident[:, :])
                ins.then_inc(mt_turned, 1)

            def turn_h1(t):
                pe.wait_ge(h1_ready, t + 1)
                if t:
                    pe.wait_ge(h1_split, t)
                else:
                    pe.wait_ge(pe_split, 2)
                for k in range(KD):
                    ins = nc.tensor.transpose(mixB[:, k * P:(k + 1) * P], F(PG_R + t % 2, k * P, P), ident[:, :])
                ins.then_inc(h1_turned, 1)

            def emb_job(m):
                for _ in feature_job(("pw", m), (m % 4) * P, HALF, [R(PG_PTH + k) for k in range(2)],
                                     [R(PG_PTL + k) for k in range(2)], (pe_split, lambda k: 2) if m == 0 else None):
                    pass

            for h in range(2):
                cut = lambda ap: [ap[:, h * HALF:(h + 1) * HALF]]
                for m in range(KD):
                    for _ in feature_job(("mix", h, m), 0, P, [R(i) for i in PG_GA], [R(i) for i in PG_GB],
                                         (m_split, lambda k: k + 1) if m == h == 0 else None, cut):
                        pass
                    if h == 0 and m == 5:
                        turn_embeddings()
                    if h == 1 and m < 4:
                        turn_mix(m)
                    if h == 1 and 2 <= m < 6:
                        turn_h1(m - 2)
            turn_mix(4)
            for t in range(4, TT):
                emb_job(2 * t - 8)
                if t + 1 < TT:
                    turn_mix(t + 1)
                emb_job(2 * t - 7)
                turn_h1(t)

            h1_hi_p = [R(PG_H1H + k) for k in range(KD)]
            h1_lo_p = [R(PG_H1L + k) for k in range(KD)]
            pe.wait_ge(h1_split, TT)
            for m in range(KD):
                for _ in feature_job(("pg", m), 0, P, h1_hi_p, h1_lo_p):
                    pass

            act_hi_p = [R(PG_ACTH + k) for k in range(4)]
            act_lo_p = [R(PG_ACTL + k) for k in range(4)]
            for g in range(NG):
                for m in range(4):
                    for _ in feature_job(("ff1", 4 * g + m), 0, P, h1_hi_p, h1_lo_p):
                        pass
                if g < NG - 1:
                    for m in range(KD):
                        for _ in feature_job(("ff2", 8 * g + m), (m % 2) * P, 256, act_hi_p, act_lo_p,
                                             (act_split, lambda k: 4 * g + k + 1) if m == 0 else None):
                            pass

            def turn_result(t):
                if t >= 2:
                    pe.wait_ge(fin_ready, t - 1)
                for k in range(KD):
                    ins = nc.tensor.transpose((mixA, mixB)[t % 2][:, k * P:(k + 1) * P],
                                              F(PG_ACC[k], t * P, P), ident[:, :])
                ins.then_inc(fin_turned, 1)

            for h in range(2):
                cut = lambda ap: [ap[:, h * HALF:(h + 1) * HALF]]
                for m in range(KD):
                    for _ in feature_job(("last", h, m), (m % 2) * P, 256, act_hi_p, act_lo_p,
                                         (act_split, lambda k: 4 * (NG - 1) + k + 1) if m == h == 0 else None, cut):
                        pass
                    if h == 1 and m % 2:
                        pe.wait_ge(acc_done, 8 * NG)
                        turn_result(m // 2)
            pe.wait_ge(acc_done, 8 * NG + 8)
            for t in range(4, TT):
                turn_result(t)

        @block.scalar
        def _(act):
            A = nc.scalar.activation
            count = [0]
            nc.scalar.preload_act_table_set("natural_log_exp_and_others")
            act.dma_start(F(PG_G0), row(ln0_g)).then_inc(rows_in, 16)
            act.dma_start(F(PG_B0), row(ln0_b)).then_inc(rows_in, 16)
            act.dma_start(ident[:, :], c_ident).then_inc(ident_in, 16)
            for t in range(1, 4):
                act.dma_start(F(PG_X + t), x_t[t]).then_inc(x_in[t], 16)

            act.wait_ge(const_set, 4)

            def rstd_estimate(tile):
                i = tile % 2
                act.wait_ge(var_ready, tile + 1)
                A(rstd[:, i, 0:1], mv[:, i, 1:2], ACT.Ln, bias=eps[:, 0:1]).then_inc(act_step, 1)
                act.wait_ge(act_step, tile + 1)
                A(rstd[:, i, 0:1], rstd[:, i, 0:1], ACT.Exp, scale=-0.5).then_inc(rs_est, 1)

            x_hi_all = R(XHI, 0, KD * 1024).rearrange("q (k n) -> q k n", k=KD)

            def store_values(page, name, t, count):
                done(act, name, t)
                nc.scalar.copy(vtile(page, t), out_of(name, t)[:, 0:HG]).then_inc(v_ready, 1)

            rstd_estimate(0)
            for j in range(4):
                act.wait_ge(w0_landed[j], 32)
                nc.scalar.copy(R(WHI + j), F(PG_W0 + j)).then_inc(w0_hi, 1)
            for t in range(TT + 1):
                if t + 1 < TT:
                    rstd_estimate(t + 1)
                if t < TT:
                    act.wait_ge(h_turned, t + 1)
                    nc.scalar.copy(x_hi_all[:, :, t * P:(t + 1) * P],
                                   (mixA, mixB)[t % 2][:, :].rearrange("q (k n) -> q k n", k=KD)).then_inc(h_hi, 1)
                    act.dma_start(h_scratch[t], F(PG_H + t % 2)).then_inc(h_stored[t % 2], 16)
                if t >= 1:
                    store_values(PG_VHG, "vhg", t - 1, 0)

            def neg_exp(page, sem_, *name):
                done(act, *name)
                A(F(page), out_of(*name)[:, :], ACT.Exp, scale=-1.0).then_inc(sem_, 1)

            def own_step(ins):
                count[0] += 1
                ins.then_inc(sig_step, 1)
                act.wait_ge(sig_step, count[0])

            def sig_exp(page, *name):
                done(act, *name)
                own_step(A(F(page), out_of(*name)[:, :], ACT.Exp, scale=-1.0))

            def sig_log(page):
                own_step(A(F(page), F(page), ACT.Ln, bias=1.0))

            def sig_end(page, sem_):
                A(F(page), F(page), ACT.Exp, scale=-1.0).then_inc(sem_, 1)

            def sigmoid(page, sem_, *name):
                done(act, *name)
                A(F(page), out_of(*name)[:, :], ACT.Sigmoid).then_inc(sem_, 1)

            def f_log_part(n):
                act.wait_ge(f_ready, n + 1)
                A(F(PG_HB + n % 2), F(PG_HB + n % 2), ACT.Ln).then_inc(f_log, 1)

            def kd_part(n):
                par = n % 2
                act.wait_ge(kd_sub, n + 1)
                A(eb_last[:, par, :], F(PG_HB + par)[:, P - 1::P], ACT.Exp)
                A(F(PG_T2), F(PG_T2), ACT.Exp).then_inc(kd_exp, 1)

            def eb_part(n):
                if n:
                    act.wait_ge(o_done, 2 * n)
                A(F(PG_T1), F(PG_HB + n % 2), ACT.Exp).then_inc(eb_exp, 1)

            def scaled_copy(page, sem_, scale, *name):
                done(act, *name)
                nc.scalar.mul(F(page), out_of(*name)[:, :], scale).then_inc(sem_, 1)

            act.wait_ge(lb_mx, 1)
            A(lbt[:, 2:4, :], lbt[:, 0:2, :], ACT.Exp).then_inc(lb_exp, 1)
            sig_exp(PG_HB, "f", 0)
            sig_log(PG_HB)
            sig_end(PG_HB, f_exp)
            f_log_part(0)
            sig_exp(PG_HQ, "q", 0)
            sig_log(PG_HQ)
            sig_end(PG_HQ, q_exp)
            kd_part(0)
            sig_exp(PG_GATE[0], "g", 0)
            sig_log(PG_GATE[0])
            sig_end(PG_GATE[0], g_exp)
            for n in range(NHG):
                nxt = n + 1
                q_page, b_page = PG_HQ + nxt % 2, PG_HB + nxt % 2
                for hl in range(14):
                    act.wait_ge(ab_sub, 14 * n + hl + 1)
                    ab = F(PG_AB + (hl % 4) // 2, (hl % 2) * HALF, HALF)
                    A(ab, ab, ACT.Exp).then_inc(ab_exp, 1)
                    if hl < 2:
                        act.wait_ge(kt_turned, 2 * n + hl + 1)
                        nc.scalar.copy(F(PG_KT, hl * HALF, HALF), bankM[hl]).then_inc(kt_done, 1)
                    elif hl == 2:
                        eb_part(n)
                    elif n == NHG - 1:
                        if hl == 8:
                            scaled_copy(PG_FQ, fq_ready, 0.125, "fq", 0)
                    elif hl == 4:
                        if n:
                            act.wait_ge(y_done, 2 * n)
                        sig_exp(q_page, "q", nxt)
                    elif hl == 5:
                        sig_log(q_page)
                    elif hl == 6:
                        sig_end(q_page, q_exp)
                    elif hl == 11:
                        if n:
                            act.wait_ge(y_done, 2 * n)
                        sig_exp(b_page, "f", nxt)
                    elif hl == 12:
                        sig_log(b_page)
                    elif hl == 13:
                        sig_end(b_page, f_exp)
                if n < NHG - 1:
                    f_log_part(nxt)
                    kd_part(nxt)
                else:
                    scaled_copy(PG_FK, fk_ready, 1.0, "fk", 0)
                for hf in range(2):
                    act.wait_ge(o_done, 2 * n + hf + 1)
                    A(F(PG_T3, hf * HALF, HALF), bankM[2 + hf], ACT.Square).then_inc(sq_done, 1)
                if nxt < NHG:
                    if n:
                        act.wait_ge(y_done, 2 * n)
                    sig_exp(PG_GATE[nxt % 2], "g", nxt)
                    sig_log(PG_GATE[nxt % 2])
                for hf in range(2):
                    t3 = F(PG_T3, hf * HALF, HALF)
                    act.wait_ge(rms_done, 2 * n + hf + 1)
                    A(t3, bankM[hf], ACT.Ln, bias=eps[:, 1:2]).then_inc(rms_log, 1)
                    act.wait_ge(rms_log, 2 * n + hf + 1)
                    A(t3, t3, ACT.Exp, scale=-0.5).then_inc(rs_ready, 1)
                if nxt < NHG:
                    sig_end(PG_GATE[nxt % 2], g_exp)
            neg_exp(PG_GA[0], gx_exp, "gx", 0)

            tmp = F(PG_XP)[0:NFX, :]
            act.wait_ge(c_abs, 1)
            A(tmp, tmp, ACT.Exp, scale=-1.0).then_inc(c_exp, 1)
            act.wait_ge(c_exp, 1)
            A(tmp, tmp, ACT.Ln, bias=1.0).then_inc(c_log, 1)
            for t in range(TT):
                store_values(PG_VFX, "vfx", t, 8)

            G_PAGES = PG_GA + PG_GB
            act.wait_ge(c_stored, 16)
            for G in range(16 * NPAIR + 3):
                if G % 8 == 7 and G < 64:
                    k = G // 8
                    n = k // 2 + 1
                    if k >= 6:
                        neg_exp(G_PAGES[k - 5], gx_exp, "gx", k - 5)
                    elif k % 2 == 0:
                        scaled_copy(PG_FQ + n % 2, fq_ready, 0.125, "fq", n)
                    else:
                        scaled_copy(PG_FK + n % 2, fk_ready, 1.0, "fk", n)
                if G >= 18 and (G - 18) % 16 == 0:
                    n = (G - 18) // 16
                    act.wait_ge(ot_done, n + 1)
                    nc.scalar.copy(F(PG_YB + n), mixA[:, :]).then_inc(yb_done, 1)
                if G < 64:
                    L = (G % 8 + 1) * P
                    act.wait_ge(nmx_ready, G + 1)
                    x_ = F(PG_XP + G % 2, 0, L)
                    if G >= 4:
                        act.wait_ge(rinv_ready, G - 3)
                    A(x_, x_, ACT.Exp, bias=nmx[:, G % 2, :], accum_out=psm[:, G % 4, :]).then_inc(p_ready, 1)
                if 1 <= G < 65:
                    L = ((G - 1) % 8 + 1) * P
                    act.wait_ge(p_turned, G)
                    if G >= 3:
                        act.wait_ge(pv_done, G - 2)
                    nc.scalar.copy(F(PG_PT[(G - 1) % 2], 0, L), mixB[:, 0:L]).then_inc(pt_done, 1)
            for i in range(3):
                sig_log(G_PAGES[i])
                sig_end(G_PAGES[i], gx_ready)
            for i in range(3, 16):
                sigmoid(G_PAGES[i], gx_exp, "gx", i)

            done(act, "gx", 15)
            for k in range(4):
                nc.scalar.copy(R(PG_YAH + k), F(PG_YA + k)).then_inc(y_hi, 1)
            for k in range(4):
                nc.scalar.copy(R(PG_YBH + k), F(PG_YB + k)).then_inc(y_hi, 1)
            for m in range(KD):
                act.wait_ge(m_sum, m + 1)
                nc.scalar.copy(R(PG_GA[m]), F(PG_M1 + 2 * (m % 2))).then_inc(m_hi, 1)

            def pe_parts():
                for k in range(2):
                    act.wait_ge(pe_turned, k + 1)
                    nc.scalar.copy(R(PG_PTH + k), (mixA, mixB)[k][:, :]).then_inc(pe_hi, 1)

            h1_hi_all = R(PG_H1H, 0, KD * 1024).rearrange("q (k n) -> q k n", k=KD)

            def h1_high(t):
                act.wait_ge(h1_turned, t + 1)
                nc.scalar.copy(h1_hi_all[:, :, t * P:(t + 1) * P],
                               mixB[:, :].rearrange("q (k n) -> q k n", k=KD)).then_inc(h1_hi, 1)

            for h in range(2):
                for m in range(KD):
                    done(act, "mix", h, m)
                    nc.scalar.copy(F(PG_MIX + m, h * HALF, HALF),
                                   out_of("mix", h, m)[:, 0:HALF]).then_inc(mix_ready, 1)
                    if h == 0 and m == 5:
                        pe_parts()
                    if h == 1 and m < 4:
                        rstd_estimate(TT + m)
                    if h == 1 and 2 <= m < 6:
                        h1_high(m - 2)
            for t in range(4, TT):
                rstd_estimate(TT + t)
                for m in (2 * t - 8, 2 * t - 7):
                    scaled_copy(PG_ACC[m], pw_ready, 1.0, "pw", m)
                h1_high(t)
            for m in range(KD):
                if m >= 2:
                    act.wait_ge(acc_init, m - 1)
                sigmoid(PG_SG[m % 2], pg_done, "pg", m)
            for i in range(4 * NG):
                done(act, "ff1", i)
                if i >= 2:
                    act.wait_ge(act_split, i - 1)
                A(F(PG_RELU[i % 2]), out_of("ff1", i)[:, :], ACT.Relu).then_inc(relu_done, 1)
                act.wait_ge(relu_done, i + 1)
                A(R(PG_ACTH + i % 4), F(PG_RELU[i % 2]), ACT.Square).then_inc(act_hi, 1)
            for t in range(TT):
                rstd_estimate(2 * TT + t)

        @block.vector
        def _(dve):
            V = nc.vector
            count = [0]

            def then(ins):
                count[0] += 1
                ins.then_inc(dve_step, 1)
                dve.wait_ge(dve_step, count[0])

            V.memset(ones[:, :], 1.0).then_inc(const_set, 1)
            V.memset(mean_w[:, :], 1.0 / P).then_inc(const_set, 1)
            V.memset(eps[:, 0:1], LN_EPS).then_inc(const_set, 1)
            V.memset(eps[:, 1:2], RMS_EPS).then_inc(const_set, 1)
            def norm_stats(src, i):
                V.bn_stats(stats[:, i, 0, :], src[:, 0:HALF])
                then(V.bn_stats(stats[:, i, 1, :], src[:, HALF:]))
                V.bn_aggr(mv[:, i, :], stats[:, i, :, :]).then_inc(var_ready, 1)

            def norm_apply(dst, src, i, g, b, tile):
                est, work, res = (rstd[:, i, j:j + 1] for j in range(3))
                dve.wait_ge(var_ready, tile + 1)
                then(V.scalar_tensor_tensor(out=dst, in0=src, scalar=mv[:, i, 0:1], in1=g,
                                            op0=ALU.subtract, op1=ALU.mult))
                dve.wait_ge(rs_est, tile + 1)
                then(V.tensor_tensor(work, est, est, ALU.mult))
                then(V.scalar_tensor_tensor(out=work, in0=mv[:, i, 1:2], scalar=LN_EPS, in1=work,
                                            op0=ALU.add, op1=ALU.mult))
                then(V.tensor_scalar(work, work, -0.5, 1.5, ALU.mult, ALU.add))
                then(V.tensor_tensor(res, est, work, ALU.mult))
                return V.scalar_tensor_tensor(out=dst, in0=dst, scalar=res, in1=b,
                                              op0=ALU.mult, op1=ALU.add)

            def low_part(lo_all, hi_all, src, t):
                cols = slice(t * P, (t + 1) * P)
                return V.tensor_tensor(lo_all[:, :, cols], src[:, :].rearrange("q (k n) -> q k n", k=KD),
                                       hi_all[:, :, cols].bitcast(F32), ALU.subtract)

            all8 = lambda page: R(page, 0, KD * 1024).rearrange("q (k n) -> q k n", k=KD)
            for t in range(-1, TT + 1):
                if t + 1 < TT:
                    dve.wait_ge(x_in[t + 1], 16)
                    norm_stats(F(PG_X + t + 1), (t + 1) % 2)
                if 0 <= t < TT:
                    if t == 0:
                        dve.wait_ge(rows_in, 32)
                    if t >= 2:
                        dve.wait_ge(h_turned, t - 1)
                        dve.wait_ge(h_stored[t % 2], 16 * (t // 2))
                    norm_apply(F(PG_H + t % 2), F(PG_X + t), t % 2, F(PG_G0), F(PG_B0), t).then_inc(h_ready, 1)
                if t == 0:
                    for j in range(2):
                        dve.wait_ge(w0_hi, j + 1)
                        V.tensor_tensor(R(WLO + j), F(PG_W0 + j), R(WHI + j).bitcast(F32),
                                        ALU.subtract).then_inc(w0_split, 1)
                if t >= 1:
                    dve.wait_ge(h_hi, t)
                    low_part(all8(XLO), all8(XHI), (mixA, mixB)[(t - 1) % 2], t - 1).then_inc(h_split, 1)
            for i in range(2):
                dve.wait_ge(h_stored[i], 16 * (TT // 2))
            dve.wait_ge(ident_in, 16)
            dve.wait_ge(consts_in, 32)
            V.tensor_copy(identb[:, :], ident[:, :])
            V.tensor_copy(causal[:, :], F(PG_T3, 0, P))
            then(V.tensor_copy(masks[:, :, :], F(PG_T2).rearrange("q (a n) -> q a n", n=P)))
            then(V.memset(F(PG_S), 0.0))

            dve.wait_ge(cols_in, 64)
            then(V.tensor_tensor(lbt[:, 2, :], lbl[:, 0, :], lbl[:, 1, :], ALU.max))
            V.tensor_tensor(lbt[:, 0, :], lbl[:, 0, :], lbt[:, 2, :], ALU.subtract)
            V.tensor_tensor(lbt[:, 1, :], lbl[:, 1, :], lbt[:, 2, :], ALU.subtract).then_inc(lb_mx, 1)
            dve.wait_ge(lb_exp, 1)
            then(V.tensor_tensor(lbt[:, 0, :], lbt[:, 2, :], lbt[:, 3, :], ALU.add))
            then(V.reciprocal(lbt[:, 1, :], lbt[:, 0, :]))
            then(V.tensor_tensor(lb[:, :], lbt[:, 2, :], lbt[:, 1, :], ALU.mult))
            then(V.tensor_scalar(omlb[:, :], lb[:, :], -1.0, 1.0, ALU.mult, ALU.add))

            def q_part(n):
                q = F(PG_HQ + n % 2)
                dve.wait_ge(q_exp, n + 1)
                V.tensor_tensor(q, out_of("q", n)[:, :], q, ALU.mult).then_inc(q_ready, 1)

            def f_part(n):
                b, k = F(PG_HB + n % 2), F(PG_HK + n % 2)
                dve.wait_ge(f_exp, n + 1)
                then(V.tensor_scalar(b, b, omlb[:, n:n + 1], lb[:, n:n + 1], ALU.mult, ALU.add))
                then(V.tensor_scalar(k, b, -1.0, 1.0, ALU.mult, ALU.add))
                V.tensor_scalar(b, b, F_FLOOR, None, ALU.max).then_inc(f_ready, 1)

            def decay_part(n):
                b = F(PG_HB + n % 2)
                dve.wait_ge(f_log, n + 1)
                for c in range(TT):
                    ins = V.tensor_tensor_scan(b[:, c * P:(c + 1) * P], ones[:, :], b[:, c * P:(c + 1) * P],
                                               0.0, ALU.mult, ALU.add)
                ins.then_inc(b_ready, 1)
                dve.wait_ge(b_ready, n + 1)
                bt = b.rearrange("q (c n) -> q c n", n=P)
                if n:
                    dve.wait_ge(kt_turned, 2 * n)
                V.tensor_tensor(F(PG_T2).rearrange("q (c n) -> q c n", n=P),
                                bt[:, :, P - 1:P].to_broadcast([P, TT, P]), bt, ALU.subtract).then_inc(kd_sub, 1)

            def kd_part(n):
                dve.wait_ge(kd_exp, n + 1)
                V.tensor_tensor(F(PG_T2), F(PG_T2), F(PG_HK + n % 2), ALU.mult).then_inc(kd_ready, 1)

            def gate_part(n):
                dve.wait_ge(g_exp, n + 1)
                gate = F(PG_GATE[n % 2])
                V.tensor_tensor(gate, out_of("g", n)[:, :], gate, ALU.mult).then_inc(gate_ready, 1)

            def level_sub(n, hl):
                m, hf = 64 >> (hl // 2), hl % 2
                early, late, mid = level_views(PG_HB + n % 2, hf * HALF, m)
                to_early, to_late, _ = level_views(PG_AB + (hl % 4) // 2, (hl % 2) * HALF, m)
                if hl >= 4:
                    dve.wait_ge(lvl_done, 16 * n + hl - 3)
                mid = mid.to_broadcast([P, HALF // (2 * m), m])
                V.tensor_tensor(to_early, mid, early, ALU.subtract)
                V.tensor_tensor(to_late, late, mid, ALU.subtract).then_inc(ab_sub, 1)

            def level_mul(n, hl):
                m, hf = 64 >> (hl // 2), hl % 2
                early, late, _ = level_views(PG_AB + (hl % 4) // 2, (hl % 2) * HALF, m)
                k = level_views(PG_HK + n % 2, hf * HALF, m)[0]
                q = level_views(PG_HQ + n % 2, hf * HALF, m)[1]
                dve.wait_ge(ab_exp, 14 * n + hl + 1)
                V.tensor_tensor(early, early, k, ALU.mult)
                V.tensor_tensor(late, late, q, ALU.mult).then_inc(ab_ready, 1)

            def level_take(n, hl):
                lv, hf = hl // 2, hl % 2
                dve.wait_ge(lvl_done, 16 * n + hl + 1)
                V.copy_predicated(F(PG_S, hf * HALF, HALF).rearrange("q (c n) -> q c n", n=P),
                                  masks[:, lv:lv + 1, :].to_broadcast([P, 4, P]),
                                  bankM[hf].rearrange("q (c n) -> q c n", n=P)).then_inc(pred_done, 1)

            def states(n, u):
                dve.wait_ge(upd_done, 2 * n + u + 1)
                last = min(4 * u + 4, TT - 1) - 1
                for c in range(4 * u, last + 1):
                    new, U = F(PG_ST, (c + 1) * P, P), bankM[u][:, (c % 4) * P:(c % 4 + 1) * P]
                    if c == 0:
                        ins = V.tensor_copy(new, U)
                    else:
                        ins = V.scalar_tensor_tensor(out=new, in0=F(PG_ST, c * P, P),
                                                     scalar=eb_last[:, n % 2, c:c + 1], in1=U,
                                                     op0=ALU.mult, op1=ALU.add)
                    if c < last:
                        then(ins)
                ins.then_inc(st_ready, 1)
                dve.wait_ge(st_ready, 2 * n + u + 1)

            def head_out(n, hf):
                t3 = F(PG_T3, hf * HALF, HALF)
                dve.wait_ge(rs_ready, 2 * n + hf + 1)
                then(V.tensor_tensor(t3, bankM[2 + hf], t3, ALU.mult))
                V.scalar_tensor_tensor(out=F(PG_YA + n, hf * HALF, HALF), in0=t3, scalar=ng[:, n:n + 1],
                                       in1=F(PG_GATE[n % 2], hf * HALF, HALF), op0=ALU.mult, op1=ALU.mult).then_inc(y_done, 1)

            f_part(0)
            decay_part(0)
            q_part(0)
            kd_part(0)
            for n in range(NHG):
                for i in range(19):
                    if i < 14:
                        level_sub(n, i)
                    if 1 <= i < 15:
                        level_mul(n, i - 1)
                    if i >= 3:
                        level_take(n, i - 3)
                    if i == 3:
                        gate_part(n)
                    if i == 5:
                        dve.wait_ge(eb_exp, n + 1)
                        V.tensor_tensor(F(PG_T1), F(PG_T1), F(PG_HQ + n % 2), ALU.mult).then_inc(qe_ready, 1)
                    if n < NHG - 1:
                        if i == 9:
                            q_part(n + 1)
                        if i == 15:
                            f_part(n + 1)
                        if i == 17:
                            decay_part(n + 1)
                states(n, 0)
                if n < NHG - 1:
                    kd_part(n + 1)
                states(n, 1)
                for hf in range(2):
                    head_out(n, hf)

            z, tmp = F(PG_CROW)[0:NFX, :], F(PG_XP)[0:NFX, :]
            done(dve, "crow")
            V.tensor_scalar(z, out_of("crow")[0:NFX, :], fb[0:NFX, :], None, ALU.add).then_inc(c_lin, 1)
            dve.wait_ge(c_lin, 1)
            V.scalar_tensor_tensor(out=tmp, in0=z, scalar=-1.0, in1=z, op0=ALU.mult, op1=ALU.max).then_inc(c_abs, 1)
            dve.wait_ge(c_log, 1)
            then(V.scalar_tensor_tensor(out=z, in0=z, scalar=0.0, in1=tmp, op0=ALU.min, op1=ALU.subtract))
            then(V.memset(tmp, 1.0))
            then(V.tensor_tensor_scan(tmp, tmp, z, 0.0, ALU.mult, ALU.add))
            V.tensor_scalar(z, tmp, -1.0, None, ALU.mult).then_inc(c_ready, 1)

            for G in range(16 * NPAIR + 2):
                if G < 64:
                    hh, L = G // 8, (G % 8 + 1) * P
                    dve.wait_ge(qk_done, G + 1)
                    if G % 8 == 0:
                        dve.wait_ge(negc_in[hh % 2], 16 * (hh // 2 + 1))
                    if G == 0:
                        dve.wait_ge(c_ready, 1)
                    if G >= 2:
                        dve.wait_ge(p_turned, G - 1)
                    V.tensor_tensor_reduce(out=F(PG_XP + G % 2, 0, L), in0=mixA[:, 0:L],
                                           in1=F(PG_NEGC[hh % 2], 0, L), scale=1.0, scalar=-3.0e38,
                                           op0=ALU.add, op1=ALU.max,
                                           accum_out=mx[:, G % 2, :]).then_inc(x_ready, 1)
                    dve.wait_ge(x_ready, G + 1)
                    V.tensor_scalar(nmx[:, G % 2, :], mx[:, G % 2, :], -1.0, None, ALU.mult).then_inc(nmx_ready, 1)
                if G >= 2:
                    g, n, e, i = G - 2, (G - 2) // 16, ((G - 2) // 8) % 2, (G - 2) % 8
                    dve.wait_ge(p_ready, g + 1)
                    V.reciprocal(rinv[:, g % 2, :], psm[:, g % 4, :]).then_inc(rinv_ready, 1)
                    dve.wait_ge(rinv_ready, g + 1)
                    dve.wait_ge(pv_done, g + 1)
                    if g % 16 == 0 and n:
                        dve.wait_ge(ot_done, n)
                    V.tensor_scalar(F(PG_O, i * P + 64 * e, 64), o_bank(g), rinv[:, g % 2, :], None,
                                    ALU.mult).then_inc(o_ready, 1)

            for k in range(8):
                dve.wait_ge(y_hi, k + 1)
                src, hi, lo = ((F(PG_YA + k), PG_YAH + k, PG_YAL + k) if k < 4
                               else (F(PG_YB + k - 4), PG_YBH + k - 4, PG_YBL + k - 4))
                V.tensor_tensor(R(lo), src, R(hi).bitcast(F32), ALU.subtract).then_inc(y_split, 1)
            dve.wait_ge(gx_ready, 3)
            dve.wait_ge(gx_exp, 16)
            for m in range(KD + 1):
                if m < KD:
                    t1, t2 = F(PG_M1 + 2 * (m % 2)), F(PG_M2 + 2 * (m % 2))
                    if m >= 2:
                        dve.wait_ge(m_split, m - 1)
                    done(dve, "A", m)
                    V.tensor_tensor(t1, out_of("A", m)[:, :], F(PG_GA[m]), ALU.mult).then_inc(a_used, 1)
                    done(dve, "B", m)
                    V.tensor_tensor(t2, out_of("B", m)[:, :], F(PG_GB[m]), ALU.mult).then_inc(b_used, 1)
                    dve.wait_ge(b_used, m + 1)
                    V.tensor_tensor(t1, t1, t2, ALU.add).then_inc(m_sum, 1)
                if m >= 1:
                    i = m - 1
                    dve.wait_ge(m_hi, i + 1)
                    V.tensor_tensor(R(PG_GB[i]), F(PG_M1 + 2 * (i % 2)), R(PG_GA[i]).bitcast(F32),
                                    ALU.subtract).then_inc(m_split, 1)
            for k in range(2):
                dve.wait_ge(pe_hi, k + 1)
                V.tensor_tensor(R(PG_PTL + k), (mixA, mixB)[k][:, :], R(PG_PTH + k).bitcast(F32),
                                ALU.subtract).then_inc(pe_split, 1)

            def h1_low(t):
                dve.wait_ge(h1_hi, t + 1)
                low_part(all8(PG_H1L), all8(PG_H1H), mixB, t).then_inc(h1_split, 1)

            dve.wait_ge(rows1_in, 32)
            for t in range(TT + 1):
                if t == TT // 2:
                    h1_low(t - 2)
                    h1_low(t - 1)
                if t < TT:
                    r = F(PG_R + t % 2)
                    dve.wait_ge(hr_in[t % 2], 16 * (t // 2 + 1))
                    dve.wait_ge(mt_turned, t + 1)
                    V.scalar_tensor_tensor(out=r, in0=r, scalar=ALPHA, in1=mixA[:, :], op0=ALU.mult,
                                           op1=ALU.add).then_inc(r_done, 1)
                    dve.wait_ge(r_done, t + 1)
                    norm_stats(r, t % 2)
                    norm_apply(r, r, t % 2, F(PG_G1), F(PG_B1), TT + t).then_inc(h1_ready, 1)
                if 2 <= t < 4:
                    h1_low(t - 2)
                elif t > 4:
                    h1_low(t - 1)

            for m in range(KD):
                sg, acc = F(PG_SG[m % 2]), F(PG_ACC[m])
                dve.wait_ge(pg_done, m + 1)
                dve.wait_ge(pw_ready, m + 1)
                then(V.tensor_tensor(acc, acc, sg, ALU.mult))
                then(V.scalar_tensor_tensor(out=acc, in0=R(PG_H1H + m).bitcast(F32), scalar=ALPHA, in1=acc,
                                            op0=ALU.mult, op1=ALU.add))
                V.scalar_tensor_tensor(out=acc, in0=R(PG_H1L + m).bitcast(F32), scalar=ALPHA, in1=acc,
                                       op0=ALU.mult, op1=ALU.add).then_inc(acc_init, 1)
            dve.wait_ge(acc_init, KD)

            for g in range(NG):
                for m in range(4):
                    i = 4 * g + m
                    r = F(PG_RELU[i % 2])
                    dve.wait_ge(relu_done, i + 1)
                    V.tensor_tensor(F(PG_SQ[i % 2]), r, r, ALU.mult).then_inc(act_sq, 1)
                    dve.wait_ge(act_sq, i + 1)
                    dve.wait_ge(act_hi, i + 1)
                    V.tensor_tensor(R(PG_ACTL + m), F(PG_SQ[i % 2]), R(PG_ACTH + m).bitcast(F32),
                                    ALU.subtract).then_inc(act_split, 1)
                for m in range(KD if g < NG - 1 else 0):
                    j = 8 * g + m
                    acc = F(PG_ACC[m])
                    done(dve, "ff2", j)
                    if j >= KD:
                        dve.wait_ge(acc_done, j - KD + 1)
                    V.tensor_tensor(acc, out_of("ff2", j)[:, :], acc, ALU.add).then_inc(acc_done, 1)

            def result_tile(t):
                src = (mixA, mixB)[t % 2][:, :]
                dve.wait_ge(fin_turned, t + 1)
                norm_stats(src, t % 2)
                if t >= 2:
                    dve.wait_ge(out_stored[t % 2], 16 * (t // 2))
                norm_apply(F(PG_OUT + t % 2), src, t % 2, F(PG_G2), F(PG_B2), 2 * TT + t).then_inc(fin_ready, 1)

            dve.wait_ge(rows2_in, 32)
            for h in range(2):
                for m in range(KD):
                    acc = F(PG_ACC[m], h * HALF, HALF)
                    done(dve, "last", h, m)
                    dve.wait_ge(acc_done, 8 * (NG - 2) + m + 1)
                    V.tensor_tensor(acc, out_of("last", h, m)[:, 0:HALF], acc, ALU.add).then_inc(acc_done, 1)
                    if h == 1 and m % 2:
                        result_tile(m // 2)
            for t in range(4, TT):
                result_tile(t)


_INS = ["x", "p", "ln0_g", "ln0_b", "w_in", "hg_lb", "hg_norm_g", "fox_fb", "w_a", "w_b", "w_o", "ln1_g", "ln1_b",
        "w_ff1", "w_ff2", "w_pg", "w_p", "ln2_g", "ln2_b"]


def constants():
    eye = np.eye(P, dtype=np.float32)
    s, t = np.arange(P)[:, None], np.arange(P)[None, :]
    causal = np.where(t > s, -1.0e30, 0.0).astype(np.float32)
    masks = np.zeros((P, LEVELS, P), np.float32)
    for lv in range(LEVELS - 1):
        m = 64 >> lv
        masks[:, lv, :] = (s // (2 * m) == t // (2 * m)) & (s % (2 * m) < m) & (t % (2 * m) >= m)
    masks[:, LEVELS - 1, :] = s == t
    return {"c_ident": eye, "c_causal": causal, "c_masks": masks}


def kernel(**inputs):
    import numpy as _np
    import concourse.bacc as _bacc
    from concourse import mybir as _mybir
    from concourse.bass_utils import run_bass_kernel_spmd as _run

    nc = _bacc.Bacc("TRN2", target_bir_lowering=False, num_devices=1)
    arrays, args = {}, []
    named = [(n, _np.ascontiguousarray(inputs[n])) for n in _INS] + list(constants().items())
    for name, a in named:
        arrays[f"in_{name}"] = a
        args.append(nc.dram_tensor(f"in_{name}", a.shape, _mybir.dt.from_np(a.dtype), kind="ExternalInput").ap())
    args.append(nc.dram_tensor("h_scratch", (TT, P, D), F32).ap())
    args.append(nc.dram_tensor("c_scratch", (NFX, S), F32).ap())
    args.append(nc.dram_tensor("out_h", (1, S, D), F32, kind="ExternalOutput").ap())
    block_kernel(nc, *args)
    r = _run(nc, [arrays], core_ids=[0])
    return r.results[0]["out_h"]
```

```python
from contextlib import ExitStack

import numpy as np

import concourse.bass as bass
from concourse import mybir

F32 = mybir.dt.float32
F32R = mybir.dt.float32r
BF16 = mybir.dt.bfloat16
U8 = mybir.dt.uint8
ALU = mybir.AluOpType
ACT = mybir.ActivationFunctionType

P = 128
S = 1024
D = 1024
KD = D // P
TT = S // P
HALF = 512
HG = 512
NHG = 4
FX = 512
NFX = 8
NPAIR = 4
FF = 4096
PLE = 256
LN_EPS = 1e-5
RMS_EPS = 1e-6
ALPHA = 2.0 ** 0.25
LEVELS = 8
F_FLOOR = 2.0 ** -63

C_HQ, C_HF, C_HI, C_HGATE = 0, 512, 1024, 1536
C_FQ, C_FK, C_FV, C_FF = 2048, 2560, 3072, 3584
C_GA, C_GB = 3592, 4616

CHUNKS = []


def _plan():
    add = CHUNKS.append
    for j in range(4):
        add(("in", C_HI + 128 * j))
    add(("in", C_HF))
    add(("in", C_HQ))
    for n in range(3):
        add(("in", C_HGATE + 128 * n))
        add(("in", C_HQ + 128 * (n + 1)))
        add(("in", C_HF + 128 * (n + 1)))
    add(("in", C_HGATE + 384))
    add(("in", C_FQ))
    add(("in", C_FK))
    add(("in", C_GA))
    add(("in", C_FF))
    for j in range(4):
        add(("in", C_FV + 128 * j))
    for n in range(1, 4):
        add(("in", C_FQ + 128 * n))
        add(("in", C_FK + 128 * n))
    for m in range(1, 8):
        add(("in", C_GA + 128 * m))
    for m in range(8):
        add(("in", C_GB + 128 * m))
    for m in range(8):
        add(("ab", 128 * m))
    for _ in range(2):
        for m in range(8):
            add(("o", 128 * m))
    for m in range(2):
        add(("p", 512 * m))
    for m in range(8):
        add(("pg", 128 * m))
    for g in range(8):
        for m in range(4):
            add(("ff1", 512 * g + 128 * m))
        for m in range(4):
            add(("ff2", 512 * g, 256 * m))


_plan()
C_VHG, C_Q0 = 0, 4
C_VFX = 20
C_AB = 45
C_O = 53
C_PW = 69
C_PG = 71
C_FFN = 79
NG = 8

NPAGES = 51
RAW = 0
SPARE = 2
WHI, WLO = 3, 7
XHI, XLO = 11, 19
PG_X, PG_G0, PG_B0 = 27, 38, 39
PG_HQ, PG_HB, PG_HK, PG_GATE = 27, 29, 31, (33, SPARE)
PG_AB, PG_S, PG_KT, PG_ST, PG_T1, PG_T2, PG_T3 = 34, 36, 37, 38, 39, 40, 41
PG_VHG, PG_YA = 42, 46
PG_FQ, PG_FK, PG_CROW, PG_NEGC = 27, 29, 32, (33, 41)
PG_VFX, PG_XP, PG_PT, PG_O, PG_YB = 34, 38, (40, 32), SPARE, 42
PG_GA = [31, 27, 29, 32, 28, 30, 33, 34]
PG_GB = [35, 36, 37, 38, 39, 40, 41, SPARE]
PG_YAH, PG_YAL, PG_YBH, PG_YBL = 11, 15, 19, 23
PG_M1, PG_M2 = 46, 47
PG_MIX = 11
PG_R, PG_G1, PG_B1, PG_PTH, PG_PTL, PG_PRAW = (19, 20, 50), 21, 22, 23, 25, 19
PG_H1H, PG_H1L = 11, 42
PG_ACC = [35, 36, 37, 38, 39, 40, 41, SPARE]
PG_SG = (27, 28, 29, 30)
PG_ACTH, PG_ACTL = 27, 31
PG_RELU, PG_SQ = (21, 22), (25, 26)
PG_OUT, PG_G2, PG_B2 = 19, 23, 24
PG_W0 = 42
BESIDE = {4: (46, 47), 5: (48, 49), 19: (33, 40), 24: (42, 43), 25: (44, 45)}
PARTS, LAST_IN = {}, {}
for _c in range(len(CHUNKS)):
    PARTS[_c] = BESIDE.get(_c, (WHI + _c % 4, WLO + _c % 4))
    LAST_IN[_c] = max([b for b in range(_c) if PARTS[b] == PARTS[_c]], default=None)
HI_BY_ACT = range(C_O + 4, C_O + 16)
HG_LEAD = 12


def in_group(f, g):
    if isinstance(g, int):
        return f(g)
    step = f(2) - f(1)
    return g * step + (f(1) - step)


def like(g):
    return g if isinstance(g, int) else 1


def block_kernel(nc, x, p, ln0_g, ln0_b, w_in, hg_lb, hg_norm_g, fox_fb, w_a, w_b, w_o, ln1_g, ln1_b,
                 w_ff1, w_ff2, w_pg, w_p, ln2_g, ln2_b, c_ident, c_causal, c_masks,
                 h_scratch, c_scratch, out):
    with ExitStack() as ctx:
        sb = lambda name, shape, dt: ctx.enter_context(nc.sbuf_tensor(name, shape, dt))
        sem = lambda name: ctx.enter_context(nc.semaphore(name))

        def view(name, dt, runs, stack):
            found, page = {}, 0
            while page < NPAGES:
                n = runs.get(page, 1)
                t = stack.enter_context(nc.sbuf_tensor(f"{name}{page}", [P, n * 1024], dt))
                for i in range(n):
                    found[page + i] = (t, i * 1024)
                page += n
            return found

        with ExitStack() as plain:
            f32_pages = view("page", F32, {PG_PRAW: 2}, plain)
        f32r_pages = view("parts", F32R, {WHI: 4, WLO: 4, XHI: 8, XLO: 8, PG_H1L: 8}, ctx)

        def F(page, off=0, n=1024):
            t, at = f32_pages[page + off // 1024]
            return t[:, at + off % 1024:at + off % 1024 + n]

        def R(page, off=0, n=1024):
            t, at = f32r_pages[page]
            return t[:, at + off:at + off + n]

        ident = sb("ident", [P, P], F32)
        ones = sb("ones", [P, P], F32)
        mean_w = sb("mean_w", [P, P], F32)
        identb = sb("identb", [P, P], BF16)
        causal = sb("causal", [P, P], BF16)
        masks = sb("masks", [P, LEVELS, P], U8)
        lbl = sb("lbl", [P, 2, NHG], F32)
        lb = sb("lb", [P, NHG], F32)
        omlb = sb("omlb", [P, NHG], F32)
        lbt = sb("lbt", [P, 4, NHG], F32)
        ng = sb("ng", [P, NHG], F32)
        fb = sb("fb", [P, 1], F32)
        stats = sb("stats", [P, 2, 2, 6], F32)
        mv = sb("mv", [P, 2, 2], F32)
        rstd = sb("rstd", [P, 2, 3], F32)
        eps = sb("eps", [P, 2], F32)
        eb_last = sb("eb_last", [P, 2, TT], F32)
        mx = sb("mx", [P, 2, 1], F32)
        nmx = sb("nmx", [P, 2, 1], F32)
        psm = sb("psm", [P, 4, 1], F32)
        rinv = sb("rinv", [P, 2, 1], F32)

        dense = [ctx.enter_context(nc.psum_tensor(f"dense{i}", [P, 2 * HALF], F32)) for i in range(2)]
        mixA = ctx.enter_context(nc.psum_tensor("mixA", [P, 2 * HALF], F32))
        mixB = ctx.enter_context(nc.psum_tensor("mixB", [P, 2 * HALF], F32))
        bankM = [mixA[:, 0:HALF], mixA[:, HALF:], mixB[:, 0:HALF], mixB[:, HALF:]]

        ident_in, consts_in, rows_in, cols_in = sem("ident_in"), sem("consts_in"), sem("rows_in"), sem("cols_in")
        const_set, lb_mx, lb_exp, lb_ready = sem("const_set"), sem("lb_mx"), sem("lb_exp"), sem("lb_ready")
        x_in = [sem(f"x_in{t}") for t in range(TT)]
        w_landed = [sem(f"w_landed{i}") for i in range(2)]
        w0_landed = [sem(f"w0_landed{i}") for i in range(4)]
        w0_hi, w0_split = sem("w0_hi"), sem("w0_split")
        w_hi, w_hi_act, w_split = sem("w_hi"), sem("w_hi_act"), sem("w_split")
        mm_done = sem("mm_done")
        dve_step, act_step, sig_step, rms_log = sem("dve_step"), sem("act_step"), sem("sig_step"), sem("rms_log")
        var_ready, rs_est = sem("var_ready"), sem("rs_est")
        h_ready, h_turned, h_hi, h_split = sem("h_ready"), sem("h_turned"), sem("h_hi"), sem("h_split")
        h_stored = [sem("h_stored0"), sem("h_stored1")]
        v_ready = sem("v_ready")
        q_exp, q_ready, f_exp, f_ready, f_log, b_ready = (
            sem("q_exp"), sem("q_ready"), sem("f_exp"), sem("f_ready"), sem("f_log"), sem("b_ready"))
        g_exp, gate_ready = sem("g_exp"), sem("gate_ready")
        eb_exp, qe_ready = sem("eb_exp"), sem("qe_ready")
        kd_sub, kd_exp, kd_ready, kt_turned, kt_done = (
            sem("kd_sub"), sem("kd_exp"), sem("kd_ready"), sem("kt_turned"), sem("kt_done"))
        ab_sub, ab_exp, ab_ready, lvl_done, pred_done = (
            sem("ab_sub"), sem("ab_exp"), sem("ab_ready"), sem("lvl_done"), sem("pred_done"))
        upd_done, st_ready, o_done, sq_done, rms_done, rs_ready, y_done = (
            sem("upd_done"), sem("st_ready"), sem("o_done"), sem("sq_done"), sem("rms_done"), sem("rs_ready"), sem("y_done"))
        fq_ready, fk_ready = sem("fq_ready"), sem("fk_ready")
        c_lin, c_abs, c_exp, c_log, c_ready, c_stored = (
            sem("c_lin"), sem("c_abs"), sem("c_exp"), sem("c_log"), sem("c_ready"), sem("c_stored"))
        negc_in = [sem("negc_in0"), sem("negc_in1")]
        qk_done, x_ready, nmx_ready, p_ready, p_turned, pt_done, pv_done, o_ready = (
            sem("qk_done"), sem("x_ready"), sem("nmx_ready"), sem("p_ready"), sem("p_turned"), sem("pt_done"),
            sem("pv_done"), sem("o_ready"))
        rinv_ready = sem("rinv_ready")
        ot_done, yb_done = sem("ot_done"), sem("yb_done")
        gx_exp, gx_ready = sem("gx_exp"), sem("gx_ready")
        y_hi, y_split = sem("y_hi"), sem("y_split")
        a_used, b_used, m_sum, m_hi, m_split = sem("a_used"), sem("b_used"), sem("m_sum"), sem("m_hi"), sem("m_split")
        mix_ready = sem("mix_ready")
        pe_in, pe_turned, pe_hi, pe_split = sem("pe_in"), sem("pe_turned"), sem("pe_hi"), sem("pe_split")
        rows1_in = sem("rows1_in")
        hr_in = [sem(f"hr_in{i}") for i in range(3)]
        mt_turned, r_done, h1_ready, h1_turned, h1_hi, h1_split = (
            sem("mt_turned"), sem("r_done"), sem("h1_ready"), sem("h1_turned"), sem("h1_hi"), sem("h1_split"))
        pw_ready, pg_done, acc_init = sem("pw_ready"), sem("pg_done"), sem("acc_init")
        relu_done, act_sq, act_hi, act_split, acc_done = (
            sem("relu_done"), sem("act_sq"), sem("act_hi"), sem("act_split"), sem("acc_done"))
        rows2_in = sem("rows2_in")
        fin_turned, ln2_scale, ln2_z, ln2_zg, fin_ready, last_ready = (
            sem("fin_turned"), sem("ln2_scale"), sem("ln2_z"), sem("ln2_zg"), sem("fin_ready"), sem("last_ready"))
        out_stored = [sem("out_stored0"), sem("out_stored1")]

        JOB, FREED, CHUNK_OF, USED_BY, SET, BANK, BEFORE = {}, [], [], {}, [], [], []

        def job(name, chunk, freed, on=None):
            JOB[name] = len(FREED)
            SET.append((1 - SET[-1] if SET else 0) if on is None else on)
            BANK.append(0)
            earlier = [j for j in range(len(FREED)) if SET[j] == SET[-1]]
            BEFORE.append(earlier[-1] if earlier else None)
            for c in range(chunk - 3, chunk + 1) if name[0] in ("vhg", "vfx") else (chunk,):
                USED_BY[c] = len(FREED)
            FREED.append(freed)
            CHUNK_OF.append(chunk)

        for t in range(TT):
            job(("vhg", t), C_VHG + 3, (v_ready, t + 1))
        job(("f", 0), 4, (f_exp, 1))
        job(("q", 0), 5, (q_ready, 1))
        for n in range(NHG):
            c = 6 + 3 * n
            job(("g", n), c, (gate_ready, n + 1))
            if n < NHG - 1:
                job(("q", n + 1), c + 1, (q_ready, n + 2))
                job(("f", n + 1), c + 2, (f_exp, n + 2))
        job(("fq", 0), 16, (fq_ready, 1))
        job(("fk", 0), 17, (fk_ready, 1))
        job(("gx", 0), 18, (gx_exp, 1))
        job(("crow",), 19, (c_lin, 1))
        for t in range(TT):
            job(("vfx", t), C_VFX + 3, (v_ready, TT + t + 1))
        for n in range(1, NPAIR):
            job(("fq", n), 22 + 2 * n, (fq_ready, n + 1), on=0)
            job(("fk", n), 23 + 2 * n, (fk_ready, n + 1), on=0)
        for i in range(1, 16):
            job(("gx", i), 29 + i, (gx_exp, i + 1), on=0 if i <= 3 else None)
        for m in range(KD):
            job(("A", m), C_AB + m, (a_used, m + 1))
            job(("B", m), C_AB + m, (b_used, m + 1))
        for h in range(2):
            for m in range(KD):
                job(("mix", h, m), C_O + 8 * h + m, (mix_ready, 8 * h + m + 1))
        for m in range(KD):
            job(("pw", m), C_PW + m // 4, (pw_ready, m + 1))
        for h in range(2):
            for m in range(4):
                job(("pg", h, m), C_PG + m, (pg_done, 4 * h + m + 1))
        for m in range(4, KD):
            job(("pg", m), C_PG + m, (pg_done, 4 + m + 1))
        for g in range(NG):
            for m in range(4):
                job(("ff1", 4 * g + m), C_FFN + 8 * g + m, (relu_done, 4 * g + m + 1))
            if g < NG - 1:
                for m in range(KD):
                    job(("ff2", 8 * g + m), C_FFN + 8 * g + 4 + m // 2, (acc_done, 8 * g + m + 1))
        for n in range(4 * KD):
            m = n % KD
            job(("last", n // KD, m), C_FFN + 8 * NG - 4 + m // 2, (acc_done, 8 * (NG - 1) + n + 1))
            BANK[-1] = (n // 2) % 2
            if n >= 4:
                BEFORE[-1] = len(FREED) - 1 - 4
            elif n >= 2:
                BEFORE[-1] = BEFORE[-3]

        def out_of(*name):
            return dense[SET[JOB[name]]]

        def o_bank(G):
            return dense[1][:, (G % 2) * HALF:(G % 2) * HALF + 64]

        def done(eng, *name):
            eng.wait_ge(mm_done, JOB[name] + 1)

        kview = lambda w: w.rearrange("a (k p) n -> p (a k) n", p=P)
        w_views = {"in": kview(w_in), "o": kview(w_o), "pg": kview(w_pg), "p": kview(w_p),
                   "ff1": kview(w_ff1), "ff2": kview(w_ff2), "a": kview(w_a), "b": kview(w_b)}
        x_t = x.rearrange("a (t p) d -> (a t) p d", p=P)
        out_t = out.rearrange("a (t p) d -> (a t) p d", p=P)

        def vtile(page, t):
            return F(page + t // 2, (t % 2) * HG, HG)

        def level_views(page, off, m):
            v = F(page, off, HALF).rearrange("q (a n) -> q a n", n=2 * m)
            return v[:, :, 0:m], v[:, :, m:2 * m], v[:, :, m - 1:m]

        def row(vec):
            return vec.partition_broadcast(P)

        block = ctx.enter_context(nc.Block())

        @block.sync
        def _(sp):
            def load_mlp_chunk(i, g):
                c = C_FFN + i
                sp.wait_ge(w_split, in_group(lambda g: 8 * g + c - 5, g))
                for half in range(2):
                    dst = F(RAW + c % 2, half * HALF, HALF)
                    if i < 4:
                        src = w_views["ff1"][:, 4 * half:4 * half + 4, bass.ds(g * HALF + P * i, P)]
                    else:
                        src = w_views["ff2"][:, bass.ds(g * 4 + 2 * half, 2), 256 * (i - 4):256 * (i - 3)]
                    sp.dma_start(dst.rearrange("q (k n) -> q k n", k=4 if i < 4 else 2), src,
                                 ).then_inc(w_landed[c % 2], 16)

            def load_chunk(c):
                kind, at = CHUNKS[c][0], CHUNKS[c][-1]
                if c >= 6:
                    sp.wait_ge(w_split, c - 5)
                page, landed = (PG_W0 + c, w0_landed[c]) if c < 4 else (RAW + c % 2, w_landed[c % 2])
                k4 = [F(page, 0, HALF), F(page, HALF, HALF)]
                if kind == "ab":
                    src = [w_views["a"][:, 0:4, at:at + P], w_views["b"][:, 0:4, at:at + P]]
                elif kind == "p":
                    src = [w_views["p"][:, k, at:at + HALF] for k in range(2)]
                else:
                    src = [w_views[kind][:, 4 * i:4 * i + 4, at:at + P] for i in range(2)]
                for dst, s in zip(k4, src):
                    if len(s.shape) == 3:
                        dst = dst.rearrange("q (k n) -> q k n", k=s.shape[1])
                    sp.dma_start(dst, s).then_inc(landed, 16)

            def load_negc(hh):
                if hh >= 2:
                    sp.wait_ge(x_ready, 8 * (hh - 1))
                sp.dma_start(F(PG_NEGC[hh % 2]), row(c_scratch[hh, :])).then_inc(negc_in[hh % 2], 16)

            sp.dma_start(F(PG_X), x_t[0]).then_inc(x_in[0], 16)
            for c in range(C_FFN):
                load_chunk(c)
                if c == 3:
                    for t in range(4, TT):
                        sp.dma_start(F(PG_X + t), x_t[t]).then_inc(x_in[t], 16)
                if c == 5:
                    sp.dma_start(F(PG_T3, 0, P), c_causal).then_inc(consts_in, 16)
                    sp.dma_start(F(PG_T2), c_masks.rearrange("q a n -> q (a n)")).then_inc(consts_in, 16)
                    with nc.allow_non_contiguous_dma(reason="a few hundred words, once"):
                        for i in range(2):
                            sp.dma_start(lbl[:, i, :], hg_lb[i].rearrange("(h q) -> q h", q=P)).then_inc(cols_in, 16)
                        sp.dma_start(ng[:, :], hg_norm_g[0].rearrange("(h q) -> q h", q=P)).then_inc(cols_in, 16)
                        sp.dma_start(fb[0:NFX, :], fox_fb.rearrange("a h -> h a")).then_inc(cols_in, 16)
                if c == 25:
                    sp.wait_ge(c_ready, 1)
                    sp.dma_start(c_scratch[:, :], F(PG_CROW)[0:NFX, :]).then_inc(c_stored, 16)
                    sp.wait_ge(c_stored, 16)
                    load_negc(0)
                    load_negc(1)
                if 29 <= c < 35:
                    load_negc(c - 27)
                if c == C_O + 4:
                    done(sp, "B", KD - 1)
                    sp.dma_start(F(PG_PRAW, 0, 2048).rearrange("q (t d) -> q t d", d=PLE),
                                 p.rearrange("l a (t q) d -> q (l a t) d", q=P)).then_inc(pe_in, 16)
                    sp.dma_start(F(PG_G1), row(ln1_g[0, :])).then_inc(rows1_in, 16)
                    sp.dma_start(F(PG_B1), row(ln1_b[0, :])).then_inc(rows1_in, 16)
                t = c - (C_O + 13)
                if 0 <= t < TT:
                    if t < 3:
                        sp.wait_ge(pe_turned, 2)
                    else:
                        sp.wait_ge(h1_turned, t - 2)
                    sp.dma_start(F(PG_R[t % 3]), h_scratch[t]).then_inc(hr_in[t % 3], 16)
            for i in range(8):
                load_mlp_chunk(i, 0)
            done(sp, "pw", KD - 1)
            sp.dma_start(F(PG_G2), row(ln2_g[0, :])).then_inc(rows2_in, 16)
            sp.dma_start(F(PG_B2), row(ln2_b[0, :])).then_inc(rows2_in, 16)
            with sp.Fori(1, NG) as g:
                for i in range(8):
                    load_mlp_chunk(i, g)
            for t in range(TT):
                if t < TT - 1:
                    sp.wait_ge(fin_ready, t + 1)
                else:
                    sp.wait_ge(last_ready, 1)
                sp.dma_start(out_t[t], F(PG_OUT + t % 2)).then_inc(out_stored[t % 2], 16)
            for i in range(2):
                sp.wait_ge(out_stored[i], 16 * (TT // 2))
                sp.wait_ge(h_stored[i], 16 * (TT // 2))

        @block.gpsimd
        def _(pool):
            for j in (2, 3):
                pool.wait_ge(w0_hi, j + 1)
                nc.gpsimd.tensor_tensor(R(WLO + j), F(PG_W0 + j), R(WHI + j).bitcast(F32),
                                        ALU.subtract).then_inc(w0_split, 1)
            for c in range(4, C_FFN + 8):
                hi, lo = PARTS[c]
                pool.wait_ge(w_landed[c % 2], 32 * (c // 2 - 1))
                if c in HI_BY_ACT:
                    pool.wait_ge(w_hi_act, HI_BY_ACT.index(c) + 1)
                elif LAST_IN[c] is not None:
                    pool.wait_ge(mm_done, USED_BY[LAST_IN[c]] + 1)
                elif c == 19:
                    pool.wait_ge(kt_turned, 2 * NHG)
                    pool.wait_ge(y_done, 2 * (NHG - 1))
                elif c == 24:
                    pool.wait_ge(o_done, 2 * NHG)
                if c not in HI_BY_ACT:
                    nc.gpsimd.tensor_copy(R(hi), F(RAW + c % 2)).then_inc(w_hi, 1)
                    pool.wait_ge(w_hi, c - 3 if c < HI_BY_ACT[0] else c - 3 - len(HI_BY_ACT))
                nc.gpsimd.tensor_tensor(R(lo), F(RAW + c % 2), R(hi).bitcast(F32),
                                        ALU.subtract).then_inc(w_split, 1)
            with pool.Fori(1, NG) as g:
                for i in range(8):
                    chunk = lambda g: C_FFN + 8 * g + i
                    hi, lo = PARTS[chunk(1)]
                    raw = F(RAW + chunk(1) % 2)
                    pool.wait_ge(w_landed[chunk(1) % 2], in_group(lambda g: 32 * (chunk(g) // 2 - 1), g))
                    pool.wait_ge(mm_done, in_group(lambda g: USED_BY[LAST_IN[chunk(g)]] + 1, g))
                    nc.gpsimd.tensor_tensor(R(hi), raw, ones[:, 0:1].to_broadcast([P, 1024]), ALU.mult).then_inc(w_hi, 1)
                    pool.wait_ge(w_hi, in_group(lambda g: chunk(g) - 3 - len(HI_BY_ACT), g))
                    nc.gpsimd.tensor_tensor(R(lo), raw, R(hi).bitcast(F32), ALU.subtract).then_inc(w_split, 1)
            pool.wait_ge(rows2_in, 32)
            for t in range(TT - 1):
                o = F(PG_OUT + t % 2)
                pool.wait_ge(ln2_z, t + 1)
                nc.gpsimd.tensor_tensor(o, o, F(PG_G2), ALU.mult).then_inc(ln2_zg, 1)
                pool.wait_ge(ln2_zg, t + 1)
                nc.gpsimd.tensor_tensor(o, o, F(PG_B2), ALU.add).then_inc(fin_ready, 1)

        @block.tensor
        def _(pe):
            mm = nc.tensor.matmul

            def three_pass(out2, whi, wlo, xhi2, xlo2, first, last):
                for o, x_ in zip(out2, xhi2):
                    mm(o, whi, x_, start=first, stop=False)
                for o, x_ in zip(out2, xlo2):
                    mm(o, whi, x_, start=False, stop=False)
                for o, x_ in zip(out2, xhi2):
                    ins = mm(o, wlo, x_, start=False, stop=last)
                return ins

            def begin(j):
                if CHUNK_OF[j] < 4:
                    pe.wait_ge(w0_split, 4)
                else:
                    pe.wait_ge(w_split, CHUNK_OF[j] - 3)
                if BEFORE[j] is not None:
                    pe.wait_ge(*FREED[BEFORE[j]])

            def end(ins, j):
                ins.then_inc(mm_done, 1)

            def halves(ap):
                return [ap[:, 0:HALF], ap[:, HALF:2 * HALF]]

            def begin_mlp(name, g):
                j = JOB[name(like(g))]
                pe.wait_ge(w_split, in_group(lambda g: CHUNK_OF[JOB[name(g)]] - 3, g))
                pe.wait_ge(FREED[BEFORE[j]][0], in_group(lambda g: FREED[BEFORE[JOB[name(g)]]][1], g))
                return j

            def mlp_job(name, g, *args, **kw):
                for _ in feature_job(name(like(g)), *args, begun=begin_mlp(name, g), **kw):
                    pass

            def feature_job(name, col, stride, acts_hi, acts_lo, ready=None, cut=halves, begun=None):
                j = JOB[name]
                if begun is None:
                    begin(j)
                hi, lo = PARTS[CHUNK_OF[j]]
                xs = cut(acts_hi[0])
                out2 = [o[:, 0:xs[0].shape[-1]] for o in halves(dense[SET[j]][:, :])[BANK[j]:][:len(xs)]]
                K = len(acts_hi)
                for k in range(K):
                    if ready is not None:
                        pe.wait_ge(ready[0], ready[1](k))
                    at = col + k * stride
                    ins = three_pass(out2, R(hi, at, P), R(lo, at, P),
                                     cut(acts_hi[k]), cut(acts_lo[k]), k == 0, k == K - 1)
                    if k == K - 1:
                        end(ins, j)
                    yield

            h_hi_p = [R(XHI + k) for k in range(KD)]
            h_lo_p = [R(XLO + k) for k in range(KD)]

            def value_job(name, t):
                j = JOB[name, t]
                begin(j)
                wide = lambda base, k: R(base, 0, 4096).rearrange(
                    "q (s n) -> q s n", s=4)[:, :, k * P:(k + 1) * P]
                out1 = dense[SET[j]][:, 0:HALF].rearrange("q (s n) -> q s n", s=4)
                for k in range(KD):
                    xh, xl = R(XHI + k, t * P, P), R(XLO + k, t * P, P)
                    mm(out1, xh, wide(WHI, k), start=k == 0, stop=False)
                    mm(out1, xh, wide(WLO, k), start=False, stop=False)
                    ins = mm(out1, xl, wide(WHI, k), start=False, stop=k == KD - 1)
                end(ins, j)

            def std(name):
                return feature_job(name, 0, P, h_hi_p, h_lo_p)

            pe.wait_ge(ident_in, 16)
            pe.wait_ge(const_set, 2)
            for t in range(TT + 1):
                if t < TT:
                    dst = (mixA, mixB)[t % 2]
                    pe.wait_ge(h_ready, t + 1)
                    if t >= 2:
                        pe.wait_ge(h_split, t - 1)
                    for k in range(KD):
                        ins = nc.tensor.transpose(dst[:, k * P:(k + 1) * P], F(PG_X + t, k * P, P), ident[:, :])
                    ins.then_inc(h_turned, 1)
                if t >= 1:
                    pe.wait_ge(h_split, t)
                    value_job("vhg", t - 1)

            for name in (("f", 0), ("q", 0)):
                for _ in std(name):
                    pass

            def hg_step(n, i):
                par = n % 2
                if i < 2:
                    pe.wait_ge(kd_ready, n + 1)
                    if n:
                        pe.wait_ge(rs_ready, 2 * (n - 1) + i + 1)
                    for c in range(4 * i, 4 * i + 4):
                        ins = nc.tensor.transpose(bankM[i][:, (c % 4) * P:(c % 4 + 1) * P],
                                                  F(PG_T2, c * P, P), ident[:, :])
                    ins.then_inc(kt_turned, 1)
                elif i < 18:
                    hl = i - 2
                    lv, hf = hl // 2, hl % 2
                    if lv < LEVELS - 1:
                        pe.wait_ge(ab_ready, 14 * n + hl + 1)
                        base = PG_AB + (hl % 4) // 2
                        lhs = rhs = F(base, (hl % 2) * HALF, HALF)
                    else:
                        pe.wait_ge(q_ready, n + 1)
                        lhs, rhs = F(PG_HK + par, hf * HALF, HALF), F(PG_HQ + par, hf * HALF, HALF)
                    if lv == 0:
                        pe.wait_ge(kt_done, 2 * n + hf + 1)
                    else:
                        pe.wait_ge(pred_done, 16 * n + hl - 1)
                    for c in range(4):
                        ins = mm(bankM[hf][:, c * P:(c + 1) * P], lhs[:, c * P:(c + 1) * P],
                                 rhs[:, c * P:(c + 1) * P], start=True, stop=True)
                    ins.then_inc(lvl_done, 1)
                elif i < 20:
                    u = i - 18
                    pe.wait_ge(pred_done, 16 * n + 14 + u + 1)
                    pe.wait_ge(kt_done, 2 * n + u + 1)
                    pe.wait_ge(v_ready, TT)
                    for c in range(4 * u, min(4 * u + 4, TT - 1)):
                        ins = mm(bankM[u][:, (c % 4) * P:(c % 4 + 1) * P], F(PG_KT, c * P, P),
                                 vtile(PG_VHG, c)[:, n * P:(n + 1) * P], start=True, stop=True)
                    ins.then_inc(upd_done, 1)
                elif i < 22:
                    hf = i - 20
                    pe.wait_ge(st_ready, 2 * n + hf + 1)
                    pe.wait_ge(qe_ready, n + 1)
                    pe.wait_ge(pred_done, 16 * n + 16)
                    for c in range(4 * hf, 4 * hf + 4):
                        o = bankM[2 + hf][:, (c % 4) * P:(c % 4 + 1) * P]
                        ins = mm(o, vtile(PG_VHG, c)[:, n * P:(n + 1) * P], F(PG_S, c * P, P),
                                 start=True, stop=c == 0)
                        if c:
                            ins = mm(o, F(PG_ST, c * P, P), F(PG_T1, c * P, P), start=False, stop=True)
                    ins.then_inc(o_done, 1)
                else:
                    hf = i - 22
                    pe.wait_ge(sq_done, 2 * n + hf + 1)
                    mm(bankM[hf], mean_w[:, :], F(PG_T3, hf * HALF, HALF), start=True,
                       stop=True).then_inc(rms_done, 1)

            def dense_stream(names):
                for name in names:
                    yield from std(name)

            stream = dense_stream([("g", 0), ("q", 1), ("f", 1), ("g", 1), ("q", 2), ("f", 2), ("g", 2),
                                   ("q", 3), ("f", 3), ("g", 3), ("fq", 0), ("fk", 0), ("gx", 0), ("crow",)])
            for step in range(HG_LEAD + 24 * NHG):
                next(stream)
                if step >= HG_LEAD:
                    hg_step(*divmod(step - HG_LEAD, 24))
            for _ in stream:
                pass
            for t in range(TT):
                value_job("vfx", t)

            def scores(G):
                n, e, i = G // 16, (G // 8) % 2, G % 8
                lo = 64 * e
                pe.wait_ge(fk_ready, n + 1)
                pe.wait_ge(fq_ready, n + 1)
                if G:
                    pe.wait_ge(x_ready, G)
                else:
                    pe.wait_ge(y_done, 2 * NHG)
                if G >= 18:
                    pe.wait_ge(yb_done, (G - 18) // 16 + 1)
                q = F(PG_FQ + n % 2, i * P, P)[lo:lo + 64, :]
                k = F(PG_FK + n % 2)[lo:lo + 64, :]
                L = (i + 1) * P
                if L > HALF:
                    mm(mixA[:, 0:HALF], q, k[:, 0:HALF], start=True, stop=True)
                at = HALF if L > HALF else 0
                mm(mixA[:, at:L], q, k[:, at:L], start=True, stop=False)
                mm(mixA[:, L - P:L], identb[:, :], causal[:, :], start=False, stop=True,
                   ).then_inc(qk_done, 1)

            def turn_probs(G):
                i = G % 8
                pe.wait_ge(p_ready, G + 1)
                if G:
                    pe.wait_ge(pt_done, G)
                for j in range(i + 1):
                    ins = nc.tensor.transpose(mixB[:, j * P:(j + 1) * P], F(PG_XP + G % 2, j * P, P), ident[:, :])
                ins.then_inc(p_turned, 1)

            def weigh_values(G):
                i, hh = G % 8, G // 8
                pe.wait_ge(pt_done, G + 1)
                if G >= 2:
                    pe.wait_ge(o_ready, G - 1)
                for j in range(i + 1):
                    ins = mm(o_bank(G), F(PG_PT[G % 2], j * P, P),
                             vtile(PG_VFX, j)[:, 64 * hh:64 * hh + 64], start=j == 0, stop=j == i)
                ins.then_inc(pv_done, 1)

            def turn_outputs(n):
                pe.wait_ge(o_ready, 16 * (n + 1))
                pe.wait_ge(x_ready, min(16 * (n + 1) + 2, 64))
                for i in range(TT):
                    ins = nc.tensor.transpose(mixA[:, i * P:(i + 1) * P], F(PG_O, i * P, P), ident[:, :])
                ins.then_inc(ot_done, 1)

            pe.wait_ge(v_ready, 2 * TT)
            stream = dense_stream([(x, n) for n in range(1, NPAIR) for x in ("fq", "fk")]
                                  + [("gx", i) for i in range(1, 16)])
            next(stream)
            for G in range(16 * NPAIR + 3):
                if G >= 18 and (G - 18) % 16 == 0:
                    turn_outputs((G - 18) // 16)
                if G < 64:
                    scores(G)
                if 1 <= G < 65:
                    turn_probs(G - 1)
                if 2 <= G < 66:
                    weigh_values(G - 2)
                next(stream)
            for _ in stream:
                pass

            for m in range(KD):
                for name, hi, lo, first in (("A", PG_YAH, PG_YAL, 0), ("B", PG_YBH, PG_YBL, 4)):
                    for _ in feature_job((name, m), first * P, P, [R(hi + k) for k in range(4)],
                                         [R(lo + k) for k in range(4)],
                                         (y_split, lambda k: first + k + 1) if m == 0 else None):
                        pass

            def turn_embeddings():
                pe.wait_ge(pe_in, 16)
                pe.wait_ge(yb_done, NPAIR)
                for k in range(2):
                    for t in range(TT):
                        ins = nc.tensor.transpose((mixA, mixB)[k][:, t * P:(t + 1) * P],
                                                  F(PG_PRAW + t // 4, (t % 4) * PLE + k * P, P), ident[:, :])
                    ins.then_inc(pe_turned, 1)

            def turn_mix(t):
                pe.wait_ge(mix_ready, KD * (1 + t // 4))
                if t:
                    pe.wait_ge(r_done, t)
                else:
                    pe.wait_ge(pe_split, 1)
                for k in range(KD):
                    ins = nc.tensor.transpose(mixA[:, k * P:(k + 1) * P], F(PG_MIX + k, t * P, P), ident[:, :])
                ins.then_inc(mt_turned, 1)

            def turn_h1(t):
                pe.wait_ge(h1_ready, t + 1)
                if t:
                    pe.wait_ge(h1_split, t)
                else:
                    pe.wait_ge(pe_split, 2)
                for k in range(KD):
                    ins = nc.tensor.transpose(mixB[:, k * P:(k + 1) * P], F(PG_R[t % 3], k * P, P), ident[:, :])
                ins.then_inc(h1_turned, 1)

            def emb_job(m):
                for _ in feature_job(("pw", m), (m % 4) * P, HALF, [R(PG_PTH + k) for k in range(2)],
                                     [R(PG_PTL + k) for k in range(2)], (pe_split, lambda k: 2) if m == 0 else None):
                    pass

            for h in range(2):
                cut = lambda ap: [ap[:, h * HALF:(h + 1) * HALF]]
                for m in range(KD):
                    for _ in feature_job(("mix", h, m), 0, P, [R(i) for i in PG_GA], [R(i) for i in PG_GB],
                                         (m_split, lambda k: k + 1) if m == h == 0 else None, cut):
                        pass
                    if h == 0 and m == 5:
                        turn_embeddings()
                    if h == 1 and m < 4:
                        turn_mix(m)
                    if h == 1 and 3 <= m < 7:
                        turn_h1(m - 3)
            h1_hi_p = [R(PG_H1H + k) for k in range(KD)]
            h1_lo_p = [R(PG_H1L + k) for k in range(KD)]

            def pg_half(h, m):
                for _ in feature_job(("pg", h, m), 0, P, h1_hi_p, h1_lo_p, None,
                                     lambda ap: [ap[:, h * HALF:(h + 1) * HALF]]):
                    pass

            turn_mix(4)
            for t in range(4, TT):
                beside = [(emb_job, (4 * t - 16 + i,)) for i in range(4)] if t < 6 else [
                    (pg_half, (0, 2 * t - 12 + i)) for i in range(2)]
                for i, (run, args) in enumerate(beside):
                    if t == TT - 1 and i == 1:
                        turn_h1(t)
                    run(*args)
                    if 2 * (i + 1) == len(beside) and t + 1 < TT:
                        turn_mix(t + 1)
                if t < TT - 1:
                    turn_h1(t)
            pe.wait_ge(h1_split, TT)
            for m in range(4):
                pg_half(1, m)
            for m in range(4, KD):
                for _ in feature_job(("pg", m), 0, P, h1_hi_p, h1_lo_p):
                    pass

            act_hi_p = [R(PG_ACTH + k) for k in range(4)]
            act_lo_p = [R(PG_ACTL + k) for k in range(4)]
            def hidden(g):
                for m in range(4):
                    mlp_job(lambda g: ("ff1", 4 * g + m), g, 0, P, h1_hi_p, h1_lo_p)

            def group(g):
                hidden(g)
                for m in range(KD):
                    mlp_job(lambda g: ("ff2", 8 * g + m), g, (m % 2) * P, 256, act_hi_p, act_lo_p,
                            (act_split, lambda k: in_group(lambda g: 4 * g + k + 1, g)) if m == 0 else None)

            group(0)
            with pe.Fori(1, NG - 1) as g:
                group(g)
            hidden(NG - 1)

            def turn_result(t):
                if t >= 2:
                    pe.wait_ge(ln2_z, t - 1)
                for k in range(KD):
                    ins = nc.tensor.transpose((mixA, mixB)[t % 2][:, k * P:(k + 1) * P],
                                              F(PG_ACC[k], t * P, P), ident[:, :])
                ins.then_inc(fin_turned, 1)

            for h in range(4):
                cut = lambda ap: [ap[:, h * 2 * P:(h + 1) * 2 * P]]
                jobs = [feature_job(("last", h, m), (m % 2) * P, 256, act_hi_p, act_lo_p,
                                    (act_split, lambda k: 4 * (NG - 1) + k + 1) if h == 0 and m < 4 else None, cut)
                        for m in range(KD)]
                if h == 0:
                    for job_ in jobs[:4]:
                        for _ in range(3):
                            next(job_)
                for m in range(KD):
                    for _ in jobs[m]:
                        pass
                    if h and m in (1, 5):
                        pe.wait_ge(acc_done, 8 * (NG - 1) + 8 * h)
                        turn_result(2 * (h - 1) + m // 4)
            pe.wait_ge(acc_done, 8 * (NG - 1) + 4 * KD)
            for t in range(TT - 2, TT):
                turn_result(t)

        @block.scalar
        def _(act):
            A = nc.scalar.activation
            count = [0]
            nc.scalar.preload_act_table_set("natural_log_exp_and_others")
            act.dma_start(F(PG_G0), row(ln0_g)).then_inc(rows_in, 16)
            act.dma_start(F(PG_B0), row(ln0_b)).then_inc(rows_in, 16)
            act.dma_start(ident[:, :], c_ident).then_inc(ident_in, 16)
            for t in range(1, 4):
                act.dma_start(F(PG_X + t), x_t[t]).then_inc(x_in[t], 16)

            act.wait_ge(const_set, 4)

            def rstd_estimate(tile):
                i = tile % 2
                act.wait_ge(var_ready, tile + 1)
                A(rstd[:, i, 0:1], mv[:, i, 1:2], ACT.Ln, bias=eps[:, 0:1]).then_inc(act_step, 1)
                act.wait_ge(act_step, tile + 1)
                A(rstd[:, i, 0:1], rstd[:, i, 0:1], ACT.Exp, scale=-0.5).then_inc(rs_est, 1)

            x_hi_all = R(XHI, 0, KD * 1024).rearrange("q (k n) -> q k n", k=KD)

            def store_values(page, name, t, count):
                done(act, name, t)
                nc.scalar.copy(vtile(page, t), out_of(name, t)[:, 0:HG]).then_inc(v_ready, 1)

            rstd_estimate(0)
            for j in range(4):
                act.wait_ge(w0_landed[j], 32)
                nc.scalar.copy(R(WHI + j), F(PG_W0 + j)).then_inc(w0_hi, 1)
            for t in range(TT + 1):
                if t + 1 < TT:
                    rstd_estimate(t + 1)
                if t < TT:
                    act.wait_ge(h_turned, t + 1)
                    nc.scalar.copy(x_hi_all[:, :, t * P:(t + 1) * P],
                                   (mixA, mixB)[t % 2][:, :].rearrange("q (k n) -> q k n", k=KD)).then_inc(h_hi, 1)
                    act.dma_start(h_scratch[t], F(PG_X + t)).then_inc(h_stored[t % 2], 16)
                if t >= 1:
                    store_values(PG_VHG, "vhg", t - 1, 0)

            def neg_exp(page, sem_, *name):
                done(act, *name)
                A(F(page), out_of(*name)[:, :], ACT.Exp, scale=-1.0).then_inc(sem_, 1)

            def own_step(ins):
                count[0] += 1
                ins.then_inc(sig_step, 1)
                act.wait_ge(sig_step, count[0])

            def sig_exp(page, *name):
                done(act, *name)
                own_step(A(F(page), out_of(*name)[:, :], ACT.Exp, scale=-1.0))

            def sig_log(page):
                own_step(A(F(page), F(page), ACT.Ln, bias=1.0))

            def sig_end(page, sem_):
                A(F(page), F(page), ACT.Exp, scale=-1.0).then_inc(sem_, 1)

            def sigmoid(page, sem_, *name):
                done(act, *name)
                A(F(page), out_of(*name)[:, :], ACT.Sigmoid).then_inc(sem_, 1)

            def f_log_part(n):
                act.wait_ge(f_ready, n + 1)
                A(F(PG_HB + n % 2), F(PG_HB + n % 2), ACT.Ln).then_inc(f_log, 1)

            def kd_part(n):
                par = n % 2
                act.wait_ge(kd_sub, n + 1)
                A(eb_last[:, par, :], F(PG_HB + par)[:, P - 1::P], ACT.Exp)
                A(F(PG_T2), F(PG_T2), ACT.Exp).then_inc(kd_exp, 1)

            def eb_part(n):
                if n:
                    act.wait_ge(o_done, 2 * n)
                A(F(PG_T1), F(PG_HB + n % 2), ACT.Exp).then_inc(eb_exp, 1)

            def scaled_copy(page, sem_, scale, *name):
                done(act, *name)
                nc.scalar.mul(F(page), out_of(*name)[:, :], scale).then_inc(sem_, 1)

            act.wait_ge(lb_mx, 1)
            A(lbt[:, 2:4, :], lbt[:, 0:2, :], ACT.Exp).then_inc(lb_exp, 1)
            for i in range(2):
                act.wait_ge(h_stored[i], 16 * (TT // 2))
            sig_exp(PG_HB, "f", 0)
            sig_log(PG_HB)
            sig_end(PG_HB, f_exp)
            f_log_part(0)
            sig_exp(PG_HQ, "q", 0)
            sig_log(PG_HQ)
            sig_end(PG_HQ, q_exp)
            kd_part(0)
            sig_exp(PG_GATE[0], "g", 0)
            sig_log(PG_GATE[0])
            sig_end(PG_GATE[0], g_exp)
            for n in range(NHG):
                nxt = n + 1
                q_page, b_page = PG_HQ + nxt % 2, PG_HB + nxt % 2
                for hl in range(14):
                    act.wait_ge(ab_sub, 14 * n + hl + 1)
                    ab = F(PG_AB + (hl % 4) // 2, (hl % 2) * HALF, HALF)
                    A(ab, ab, ACT.Exp).then_inc(ab_exp, 1)
                    if hl < 2:
                        act.wait_ge(kt_turned, 2 * n + hl + 1)
                        nc.scalar.copy(F(PG_KT, hl * HALF, HALF), bankM[hl]).then_inc(kt_done, 1)
                    elif hl == 2:
                        eb_part(n)
                    elif n == NHG - 1:
                        if hl == 8:
                            scaled_copy(PG_FQ, fq_ready, 0.125, "fq", 0)
                    elif hl == 4:
                        if n:
                            act.wait_ge(y_done, 2 * n)
                        sig_exp(q_page, "q", nxt)
                    elif hl == 5:
                        sig_log(q_page)
                    elif hl == 6:
                        sig_end(q_page, q_exp)
                    elif hl == 11:
                        if n:
                            act.wait_ge(y_done, 2 * n)
                        sig_exp(b_page, "f", nxt)
                    elif hl == 12:
                        sig_log(b_page)
                    elif hl == 13:
                        sig_end(b_page, f_exp)
                if n < NHG - 1:
                    f_log_part(nxt)
                    kd_part(nxt)
                else:
                    scaled_copy(PG_FK, fk_ready, 1.0, "fk", 0)
                for hf in range(2):
                    act.wait_ge(o_done, 2 * n + hf + 1)
                    A(F(PG_T3, hf * HALF, HALF), bankM[2 + hf], ACT.Square).then_inc(sq_done, 1)
                if nxt < NHG:
                    if n:
                        act.wait_ge(y_done, 2 * n)
                    sig_exp(PG_GATE[nxt % 2], "g", nxt)
                    sig_log(PG_GATE[nxt % 2])
                for hf in range(2):
                    t3 = F(PG_T3, hf * HALF, HALF)
                    act.wait_ge(rms_done, 2 * n + hf + 1)
                    A(t3, bankM[hf], ACT.Ln, bias=eps[:, 1:2]).then_inc(rms_log, 1)
                    act.wait_ge(rms_log, 2 * n + hf + 1)
                    A(t3, t3, ACT.Exp, scale=-0.5).then_inc(rs_ready, 1)
                if nxt < NHG:
                    sig_end(PG_GATE[nxt % 2], g_exp)
            neg_exp(PG_GA[0], gx_exp, "gx", 0)

            tmp = F(PG_XP)[0:NFX, :]
            act.wait_ge(c_abs, 1)
            A(tmp, tmp, ACT.Exp, scale=-1.0).then_inc(c_exp, 1)
            act.wait_ge(c_exp, 1)
            A(tmp, tmp, ACT.Ln, bias=1.0).then_inc(c_log, 1)
            for t in range(TT):
                store_values(PG_VFX, "vfx", t, 8)

            G_PAGES = PG_GA + PG_GB
            act.wait_ge(c_stored, 16)
            for G in range(16 * NPAIR + 3):
                if G % 8 == 7 and G < 64:
                    k = G // 8
                    n = k // 2 + 1
                    if k >= 6:
                        neg_exp(G_PAGES[k - 5], gx_exp, "gx", k - 5)
                    elif k % 2 == 0:
                        scaled_copy(PG_FQ + n % 2, fq_ready, 0.125, "fq", n)
                    else:
                        scaled_copy(PG_FK + n % 2, fk_ready, 1.0, "fk", n)
                if G >= 18 and (G - 18) % 16 == 0:
                    n = (G - 18) // 16
                    act.wait_ge(ot_done, n + 1)
                    nc.scalar.copy(F(PG_YB + n), mixA[:, :]).then_inc(yb_done, 1)
                if G < 64:
                    L = (G % 8 + 1) * P
                    act.wait_ge(nmx_ready, G + 1)
                    x_ = F(PG_XP + G % 2, 0, L)
                    if G >= 4:
                        act.wait_ge(rinv_ready, G - 3)
                    A(x_, x_, ACT.Exp, bias=nmx[:, G % 2, :], accum_out=psm[:, G % 4, :]).then_inc(p_ready, 1)
                if 1 <= G < 65:
                    L = ((G - 1) % 8 + 1) * P
                    act.wait_ge(p_turned, G)
                    if G >= 3:
                        act.wait_ge(pv_done, G - 2)
                    nc.scalar.copy(F(PG_PT[(G - 1) % 2], 0, L), mixB[:, 0:L]).then_inc(pt_done, 1)
            for i in range(3):
                sig_log(G_PAGES[i])
                sig_end(G_PAGES[i], gx_ready)
            for i in range(3, 15):
                sigmoid(G_PAGES[i], gx_exp, "gx", i)

            done(act, "gx", 15)
            for k in range(4):
                nc.scalar.copy(R(PG_YAH + k), F(PG_YA + k)).then_inc(y_hi, 1)
            sigmoid(G_PAGES[15], gx_exp, "gx", 15)
            for k in range(4):
                nc.scalar.copy(R(PG_YBH + k), F(PG_YB + k)).then_inc(y_hi, 1)
            for m in range(KD):
                act.wait_ge(m_sum, m + 1)
                nc.scalar.copy(R(PG_GA[m]), F(PG_M1 + 2 * (m % 2))).then_inc(m_hi, 1)

            nc.scalar.preload_act_table_set("natural_log_exp_and_others")

            def pe_parts():
                for k in range(2):
                    act.wait_ge(pe_turned, k + 1)
                    nc.scalar.copy(R(PG_PTH + k), (mixA, mixB)[k][:, :]).then_inc(pe_hi, 1)

            h1_hi_all = R(PG_H1H, 0, KD * 1024).rearrange("q (k n) -> q k n", k=KD)

            def h1_high(t):
                act.wait_ge(h1_turned, t + 1)
                nc.scalar.copy(h1_hi_all[:, :, t * P:(t + 1) * P],
                               mixB[:, :].rearrange("q (k n) -> q k n", k=KD)).then_inc(h1_hi, 1)

            for h in range(2):
                for m in range(KD):
                    done(act, "mix", h, m)
                    nc.scalar.copy(F(PG_MIX + m, h * HALF, HALF),
                                   out_of("mix", h, m)[:, 0:HALF]).then_inc(mix_ready, 1)
                    c = C_O + 8 * h + m + 4
                    if c in HI_BY_ACT:
                        act.wait_ge(w_landed[c % 2], 32 * (c // 2 - 1))
                        nc.scalar.copy(R(PARTS[c][0]), F(RAW + c % 2)).then_inc(w_hi_act, 1)
                    if h == 0 and m == 5:
                        pe_parts()
                    if h == 1 and 3 <= m < 7:
                        h1_high(m - 3)
                    if h == 1 and m < 4:
                        rstd_estimate(TT + m)
            for t in range(4, TT):
                rstd_estimate(TT + t)
                for i in range(4 if t < 6 else 0):
                    scaled_copy(PG_ACC[4 * t - 16 + i], pw_ready, 1.0, "pw", 4 * t - 16 + i)
                for m in (2 * t - 12, 2 * t - 11) if t >= 6 else ():
                    if m == 3:
                        h1_high(t)
                    done(act, "pg", 0, m)
                    nc.scalar.copy(F(PG_SG[m], 0, HALF), out_of("pg", 0, m)[:, 0:HALF]).then_inc(pg_done, 1)
                if t < TT - 1:
                    h1_high(t)
            for m in range(KD):
                sg = PG_SG[m % 4]
                if m < 4:
                    act.wait_ge(pg_done, m + 1)
                    A(F(sg, 0, HALF), F(sg, 0, HALF), ACT.Sigmoid)
                    done(act, "pg", 1, m)
                    A(F(sg, HALF, HALF), out_of("pg", 1, m)[:, 0:HALF], ACT.Sigmoid).then_inc(pg_done, 1)
                else:
                    act.wait_ge(acc_init, m - 3)
                    sigmoid(sg, pg_done, "pg", m)
            nc.scalar.preload_act_table_set("natural_log_exp_and_others")
            act.wait_ge(acc_init, KD)

            def hidden(g):
                for m in range(4):
                    act.wait_ge(mm_done, in_group(lambda g: JOB["ff1", 4 * g + m] + 1, g))
                    if not (isinstance(g, int) and 4 * g + m < 2):
                        act.wait_ge(act_split, in_group(lambda g: 4 * g + m - 1, g))
                    A(F(PG_RELU[m % 2]), out_of("ff1", 4 * like(g) + m)[:, :], ACT.Relu).then_inc(relu_done, 1)
                    act.wait_ge(relu_done, in_group(lambda g: 4 * g + m + 1, g))
                    A(R(PG_ACTH + m), F(PG_RELU[m % 2]), ACT.Square).then_inc(act_hi, 1)

            hidden(0)
            with act.Fori(1, NG) as g:
                hidden(g)
            for t in range(TT):
                rstd_estimate(2 * TT + t)
                act.wait_ge(ln2_scale, t + 1)
                if t >= 2:
                    act.wait_ge(out_stored[t % 2], 16 * (t // 2))
                A(F(PG_OUT + t % 2), (mixA, mixB)[t % 2][:, :], ACT.Identity, scale=rstd[:, t % 2, 2:3],
                  bias=rstd[:, t % 2, 1:2]).then_inc(ln2_z, 1)

        @block.vector
        def _(dve):
            V = nc.vector
            count = [0]

            def then(ins):
                count[0] += 1
                ins.then_inc(dve_step, 1)
                dve.wait_ge(dve_step, count[0])

            V.memset(ones[:, :], 1.0).then_inc(const_set, 1)
            V.memset(mean_w[:, :], 1.0 / P).then_inc(const_set, 1)
            V.memset(eps[:, 0:1], LN_EPS).then_inc(const_set, 1)
            V.memset(eps[:, 1:2], RMS_EPS).then_inc(const_set, 1)
            def norm_stats(src, i):
                V.bn_stats(stats[:, i, 0, :], src[:, 0:HALF])
                then(V.bn_stats(stats[:, i, 1, :], src[:, HALF:]))
                V.bn_aggr(mv[:, i, :], stats[:, i, :, :]).then_inc(var_ready, 1)

            def newton(i):
                est, work, res = (rstd[:, i, j:j + 1] for j in range(3))
                then(V.tensor_tensor(work, est, est, ALU.mult))
                then(V.scalar_tensor_tensor(out=work, in0=mv[:, i, 1:2], scalar=LN_EPS, in1=work,
                                            op0=ALU.add, op1=ALU.mult))
                then(V.tensor_scalar(work, work, -0.5, 1.5, ALU.mult, ALU.add))
                then(V.tensor_tensor(res, est, work, ALU.mult))

            def norm_apply(dst, src, i, g, b, tile):
                res = rstd[:, i, 2:3]
                dve.wait_ge(var_ready, tile + 1)
                then(V.scalar_tensor_tensor(out=dst, in0=src, scalar=mv[:, i, 0:1], in1=g,
                                            op0=ALU.subtract, op1=ALU.mult))
                dve.wait_ge(rs_est, tile + 1)
                newton(i)
                return V.scalar_tensor_tensor(out=dst, in0=dst, scalar=res, in1=b,
                                              op0=ALU.mult, op1=ALU.add)

            def low_part(lo_all, hi_all, src, t):
                cols = slice(t * P, (t + 1) * P)
                return V.tensor_tensor(lo_all[:, :, cols], src[:, :].rearrange("q (k n) -> q k n", k=KD),
                                       hi_all[:, :, cols].bitcast(F32), ALU.subtract)

            all8 = lambda page: R(page, 0, KD * 1024).rearrange("q (k n) -> q k n", k=KD)
            for t in range(-1, TT + 1):
                if t + 1 < TT:
                    dve.wait_ge(x_in[t + 1], 16)
                    norm_stats(F(PG_X + t + 1), (t + 1) % 2)
                if 0 <= t < TT:
                    if t == 0:
                        dve.wait_ge(rows_in, 32)
                    norm_apply(F(PG_X + t), F(PG_X + t), t % 2, F(PG_G0), F(PG_B0), t).then_inc(h_ready, 1)
                if t == 0:
                    for j in range(2):
                        dve.wait_ge(w0_hi, j + 1)
                        V.tensor_tensor(R(WLO + j), F(PG_W0 + j), R(WHI + j).bitcast(F32),
                                        ALU.subtract).then_inc(w0_split, 1)
                if t >= 1:
                    dve.wait_ge(h_hi, t)
                    low_part(all8(XLO), all8(XHI), (mixA, mixB)[(t - 1) % 2], t - 1).then_inc(h_split, 1)
            for i in range(2):
                dve.wait_ge(h_stored[i], 16 * (TT // 2))
            dve.wait_ge(ident_in, 16)
            dve.wait_ge(consts_in, 32)
            V.tensor_copy(identb[:, :], ident[:, :])
            V.tensor_copy(causal[:, :], F(PG_T3, 0, P))
            then(V.tensor_copy(masks[:, :, :], F(PG_T2).rearrange("q (a n) -> q a n", n=P)))
            then(V.memset(F(PG_S), 0.0))

            dve.wait_ge(cols_in, 64)
            then(V.tensor_tensor(lbt[:, 2, :], lbl[:, 0, :], lbl[:, 1, :], ALU.max))
            V.tensor_tensor(lbt[:, 0, :], lbl[:, 0, :], lbt[:, 2, :], ALU.subtract)
            V.tensor_tensor(lbt[:, 1, :], lbl[:, 1, :], lbt[:, 2, :], ALU.subtract).then_inc(lb_mx, 1)
            dve.wait_ge(lb_exp, 1)
            then(V.tensor_tensor(lbt[:, 0, :], lbt[:, 2, :], lbt[:, 3, :], ALU.add))
            then(V.reciprocal(lbt[:, 1, :], lbt[:, 0, :]))
            then(V.tensor_tensor(lb[:, :], lbt[:, 2, :], lbt[:, 1, :], ALU.mult))
            then(V.tensor_scalar(omlb[:, :], lb[:, :], -1.0, 1.0, ALU.mult, ALU.add))

            def q_part(n):
                q = F(PG_HQ + n % 2)
                dve.wait_ge(q_exp, n + 1)
                V.tensor_tensor(q, out_of("q", n)[:, :], q, ALU.mult).then_inc(q_ready, 1)

            def f_part(n):
                b, k = F(PG_HB + n % 2), F(PG_HK + n % 2)
                dve.wait_ge(f_exp, n + 1)
                then(V.tensor_scalar(b, b, omlb[:, n:n + 1], lb[:, n:n + 1], ALU.mult, ALU.add))
                then(V.tensor_scalar(k, b, -1.0, 1.0, ALU.mult, ALU.add))
                V.tensor_scalar(b, b, F_FLOOR, None, ALU.max).then_inc(f_ready, 1)

            def decay_part(n):
                b = F(PG_HB + n % 2)
                dve.wait_ge(f_log, n + 1)
                for c in range(TT):
                    ins = V.tensor_tensor_scan(b[:, c * P:(c + 1) * P], ones[:, :], b[:, c * P:(c + 1) * P],
                                               0.0, ALU.mult, ALU.add)
                ins.then_inc(b_ready, 1)
                dve.wait_ge(b_ready, n + 1)
                bt = b.rearrange("q (c n) -> q c n", n=P)
                if n:
                    dve.wait_ge(kt_turned, 2 * n)
                V.tensor_tensor(F(PG_T2).rearrange("q (c n) -> q c n", n=P),
                                bt[:, :, P - 1:P].to_broadcast([P, TT, P]), bt, ALU.subtract).then_inc(kd_sub, 1)

            def kd_part(n):
                dve.wait_ge(kd_exp, n + 1)
                V.tensor_tensor(F(PG_T2), F(PG_T2), F(PG_HK + n % 2), ALU.mult).then_inc(kd_ready, 1)

            def gate_part(n):
                dve.wait_ge(g_exp, n + 1)
                gate = F(PG_GATE[n % 2])
                V.tensor_tensor(gate, out_of("g", n)[:, :], gate, ALU.mult).then_inc(gate_ready, 1)

            def level_sub(n, hl):
                m, hf = 64 >> (hl // 2), hl % 2
                early, late, mid = level_views(PG_HB + n % 2, hf * HALF, m)
                to_early, to_late, _ = level_views(PG_AB + (hl % 4) // 2, (hl % 2) * HALF, m)
                if hl >= 4:
                    dve.wait_ge(lvl_done, 16 * n + hl - 3)
                mid = mid.to_broadcast([P, HALF // (2 * m), m])
                V.tensor_tensor(to_early, mid, early, ALU.subtract)
                V.tensor_tensor(to_late, late, mid, ALU.subtract).then_inc(ab_sub, 1)

            def level_mul(n, hl):
                m, hf = 64 >> (hl // 2), hl % 2
                early, late, _ = level_views(PG_AB + (hl % 4) // 2, (hl % 2) * HALF, m)
                k = level_views(PG_HK + n % 2, hf * HALF, m)[0]
                q = level_views(PG_HQ + n % 2, hf * HALF, m)[1]
                dve.wait_ge(ab_exp, 14 * n + hl + 1)
                V.tensor_tensor(early, early, k, ALU.mult)
                V.tensor_tensor(late, late, q, ALU.mult).then_inc(ab_ready, 1)

            def level_take(n, hl):
                lv, hf = hl // 2, hl % 2
                dve.wait_ge(lvl_done, 16 * n + hl + 1)
                V.copy_predicated(F(PG_S, hf * HALF, HALF).rearrange("q (c n) -> q c n", n=P),
                                  masks[:, lv:lv + 1, :].to_broadcast([P, 4, P]),
                                  bankM[hf].rearrange("q (c n) -> q c n", n=P)).then_inc(pred_done, 1)

            def states(n, u):
                dve.wait_ge(upd_done, 2 * n + u + 1)
                last = min(4 * u + 4, TT - 1) - 1
                for c in range(4 * u, last + 1):
                    new, U = F(PG_ST, (c + 1) * P, P), bankM[u][:, (c % 4) * P:(c % 4 + 1) * P]
                    if c == 0:
                        ins = V.tensor_copy(new, U)
                    else:
                        ins = V.scalar_tensor_tensor(out=new, in0=F(PG_ST, c * P, P),
                                                     scalar=eb_last[:, n % 2, c:c + 1], in1=U,
                                                     op0=ALU.mult, op1=ALU.add)
                    if c < last:
                        then(ins)
                ins.then_inc(st_ready, 1)
                dve.wait_ge(st_ready, 2 * n + u + 1)

            def head_out(n, hf):
                t3 = F(PG_T3, hf * HALF, HALF)
                dve.wait_ge(rs_ready, 2 * n + hf + 1)
                then(V.tensor_tensor(t3, bankM[2 + hf], t3, ALU.mult))
                V.scalar_tensor_tensor(out=F(PG_YA + n, hf * HALF, HALF), in0=t3, scalar=ng[:, n:n + 1],
                                       in1=F(PG_GATE[n % 2], hf * HALF, HALF), op0=ALU.mult, op1=ALU.mult).then_inc(y_done, 1)

            f_part(0)
            decay_part(0)
            q_part(0)
            kd_part(0)
            for n in range(NHG):
                for i in range(19):
                    if i < 14:
                        level_sub(n, i)
                    if 1 <= i < 15:
                        level_mul(n, i - 1)
                    if i >= 3:
                        level_take(n, i - 3)
                    if i == 3:
                        gate_part(n)
                    if i == 5:
                        dve.wait_ge(eb_exp, n + 1)
                        V.tensor_tensor(F(PG_T1), F(PG_T1), F(PG_HQ + n % 2), ALU.mult).then_inc(qe_ready, 1)
                    if n < NHG - 1:
                        if i == 9:
                            q_part(n + 1)
                        if i == 15:
                            f_part(n + 1)
                        if i == 17:
                            decay_part(n + 1)
                states(n, 0)
                if n < NHG - 1:
                    kd_part(n + 1)
                states(n, 1)
                for hf in range(2):
                    head_out(n, hf)

            z, tmp = F(PG_CROW)[0:NFX, :], F(PG_XP)[0:NFX, :]
            done(dve, "crow")
            V.tensor_scalar(z, out_of("crow")[0:NFX, :], fb[0:NFX, :], None, ALU.add).then_inc(c_lin, 1)
            dve.wait_ge(c_lin, 1)
            V.scalar_tensor_tensor(out=tmp, in0=z, scalar=-1.0, in1=z, op0=ALU.mult, op1=ALU.max).then_inc(c_abs, 1)
            dve.wait_ge(c_log, 1)
            then(V.scalar_tensor_tensor(out=z, in0=z, scalar=0.0, in1=tmp, op0=ALU.min, op1=ALU.subtract))
            then(V.memset(tmp, 1.0))
            then(V.tensor_tensor_scan(tmp, tmp, z, 0.0, ALU.mult, ALU.add))
            V.tensor_scalar(z, tmp, -1.0, None, ALU.mult).then_inc(c_ready, 1)

            for G in range(16 * NPAIR + 2):
                if G < 64:
                    hh, L = G // 8, (G % 8 + 1) * P
                    dve.wait_ge(qk_done, G + 1)
                    if G % 8 == 0:
                        dve.wait_ge(negc_in[hh % 2], 16 * (hh // 2 + 1))
                    if G == 0:
                        dve.wait_ge(c_ready, 1)
                    if G >= 2:
                        dve.wait_ge(p_turned, G - 1)
                    V.tensor_tensor_reduce(out=F(PG_XP + G % 2, 0, L), in0=mixA[:, 0:L],
                                           in1=F(PG_NEGC[hh % 2], 0, L), scale=1.0, scalar=-3.0e38,
                                           op0=ALU.add, op1=ALU.max,
                                           accum_out=mx[:, G % 2, :]).then_inc(x_ready, 1)
                    dve.wait_ge(x_ready, G + 1)
                    V.tensor_scalar(nmx[:, G % 2, :], mx[:, G % 2, :], -1.0, None, ALU.mult).then_inc(nmx_ready, 1)
                if G >= 2:
                    g, n, e, i = G - 2, (G - 2) // 16, ((G - 2) // 8) % 2, (G - 2) % 8
                    dve.wait_ge(p_ready, g + 1)
                    V.reciprocal(rinv[:, g % 2, :], psm[:, g % 4, :]).then_inc(rinv_ready, 1)
                    dve.wait_ge(rinv_ready, g + 1)
                    dve.wait_ge(pv_done, g + 1)
                    if g % 16 == 0 and n:
                        dve.wait_ge(ot_done, n)
                    V.tensor_scalar(F(PG_O, i * P + 64 * e, 64), o_bank(g), rinv[:, g % 2, :], None,
                                    ALU.mult).then_inc(o_ready, 1)

            for k in range(8):
                dve.wait_ge(y_hi, k + 1)
                src, hi, lo = ((F(PG_YA + k), PG_YAH + k, PG_YAL + k) if k < 4
                               else (F(PG_YB + k - 4), PG_YBH + k - 4, PG_YBL + k - 4))
                V.tensor_tensor(R(lo), src, R(hi).bitcast(F32), ALU.subtract).then_inc(y_split, 1)
            dve.wait_ge(gx_ready, 3)
            dve.wait_ge(gx_exp, 16)
            for m in range(KD + 1):
                if m < KD:
                    t1, t2 = F(PG_M1 + 2 * (m % 2)), F(PG_M2 + 2 * (m % 2))
                    if m >= 2:
                        dve.wait_ge(m_split, m - 1)
                    done(dve, "A", m)
                    V.tensor_tensor(t1, out_of("A", m)[:, :], F(PG_GA[m]), ALU.mult).then_inc(a_used, 1)
                    done(dve, "B", m)
                    V.tensor_tensor(t2, out_of("B", m)[:, :], F(PG_GB[m]), ALU.mult).then_inc(b_used, 1)
                    dve.wait_ge(b_used, m + 1)
                    V.tensor_tensor(t1, t1, t2, ALU.add).then_inc(m_sum, 1)
                if m >= 1:
                    i = m - 1
                    dve.wait_ge(m_hi, i + 1)
                    V.tensor_tensor(R(PG_GB[i]), F(PG_M1 + 2 * (i % 2)), R(PG_GA[i]).bitcast(F32),
                                    ALU.subtract).then_inc(m_split, 1)
            for k in range(2):
                dve.wait_ge(pe_hi, k + 1)
                V.tensor_tensor(R(PG_PTL + k), (mixA, mixB)[k][:, :], R(PG_PTH + k).bitcast(F32),
                                ALU.subtract).then_inc(pe_split, 1)

            def h1_low(t):
                dve.wait_ge(h1_hi, t + 1)
                low_part(all8(PG_H1L), all8(PG_H1H), mixB, t).then_inc(h1_split, 1)

            dve.wait_ge(rows1_in, 32)
            for t in range(TT + 1):
                if t == TT // 2:
                    h1_low(t - 2)
                    h1_low(t - 1)
                if t < TT:
                    r = F(PG_R[t % 3])
                    dve.wait_ge(hr_in[t % 3], 16 * (t // 3 + 1))
                    dve.wait_ge(mt_turned, t + 1)
                    V.scalar_tensor_tensor(out=r, in0=r, scalar=ALPHA, in1=mixA[:, :], op0=ALU.mult,
                                           op1=ALU.add).then_inc(r_done, 1)
                    dve.wait_ge(r_done, t + 1)
                    norm_stats(r, t % 2)
                    norm_apply(r, r, t % 2, F(PG_G1), F(PG_B1), TT + t).then_inc(h1_ready, 1)
                if 2 <= t < 4:
                    h1_low(t - 2)
                elif t > 4:
                    h1_low(t - 1)

            for m in range(KD):
                sg, acc = F(PG_SG[m % 4]), F(PG_ACC[m])
                dve.wait_ge(pg_done, 4 + m + 1)
                dve.wait_ge(pw_ready, m + 1)
                then(V.tensor_tensor(acc, acc, sg, ALU.mult))
                then(V.scalar_tensor_tensor(out=acc, in0=R(PG_H1H + m).bitcast(F32), scalar=ALPHA, in1=acc,
                                            op0=ALU.mult, op1=ALU.add))
                V.scalar_tensor_tensor(out=acc, in0=R(PG_H1L + m).bitcast(F32), scalar=ALPHA, in1=acc,
                                       op0=ALU.mult, op1=ALU.add).then_inc(acc_init, 1)
            dve.wait_ge(acc_init, KD)

            def hidden(g):
                for m in range(4):
                    count_ = in_group(lambda g: 4 * g + m + 1, g)
                    r, sq = F(PG_RELU[m % 2]), F(PG_SQ[m % 2])
                    dve.wait_ge(relu_done, count_)
                    V.tensor_tensor(sq, r, r, ALU.mult).then_inc(act_sq, 1)
                    dve.wait_ge(act_sq, count_)
                    dve.wait_ge(act_hi, count_)
                    V.tensor_tensor(R(PG_ACTL + m), sq, R(PG_ACTH + m).bitcast(F32),
                                    ALU.subtract).then_inc(act_split, 1)

            def group(g):
                hidden(g)
                for m in range(KD):
                    acc = F(PG_ACC[m])
                    dve.wait_ge(mm_done, in_group(lambda g: JOB["ff2", 8 * g + m] + 1, g))
                    if not (isinstance(g, int) and g == 0):
                        dve.wait_ge(acc_done, in_group(lambda g: 8 * (g - 1) + m + 1, g))
                    V.tensor_tensor(acc, out_of("ff2", 8 * like(g) + m)[:, :], acc, ALU.add).then_inc(acc_done, 1)

            group(0)
            with dve.Fori(1, NG - 1) as g:
                group(g)
            hidden(NG - 1)

            def result_tile(t):
                i = t % 2
                work, res = rstd[:, i, 1:2], rstd[:, i, 2:3]
                dve.wait_ge(fin_turned, t + 1)
                norm_stats((mixA, mixB)[i][:, :], i)
                dve.wait_ge(var_ready, 2 * TT + t + 1)
                dve.wait_ge(rs_est, 2 * TT + t + 1)
                newton(i)
                V.scalar_tensor_tensor(out=work, in0=mv[:, i, 0:1], scalar=-1.0, in1=res,
                                       op0=ALU.mult, op1=ALU.mult).then_inc(ln2_scale, 1)

            dve.wait_ge(rows2_in, 32)
            for h in range(4):
                for m in range(KD):
                    acc = F(PG_ACC[m], h * 2 * P, 2 * P)
                    at = BANK[JOB["last", h, m]] * HALF
                    done(dve, "last", h, m)
                    dve.wait_ge(acc_done, 8 * (NG - 2) + m + 1)
                    V.tensor_tensor(acc, out_of("last", h, m)[:, at:at + 2 * P], acc, ALU.add).then_inc(acc_done, 1)
                    if h and m in (1, 5):
                        result_tile(2 * (h - 1) + m // 4)
            for t in range(TT - 2, TT):
                result_tile(t)
            o = F(PG_OUT + 1)
            dve.wait_ge(ln2_z, TT)
            then(V.tensor_tensor(o, o, F(PG_G2), ALU.mult))
            V.tensor_tensor(o, o, F(PG_B2), ALU.add).then_inc(last_ready, 1)


_INS = ["x", "p", "ln0_g", "ln0_b", "w_in", "hg_lb", "hg_norm_g", "fox_fb", "w_a", "w_b", "w_o", "ln1_g", "ln1_b",
        "w_ff1", "w_ff2", "w_pg", "w_p", "ln2_g", "ln2_b"]


def constants():
    eye = np.eye(P, dtype=np.float32)
    s, t = np.arange(P)[:, None], np.arange(P)[None, :]
    causal = np.where(t > s, -1.0e30, 0.0).astype(np.float32)
    masks = np.zeros((P, LEVELS, P), np.float32)
    for lv in range(LEVELS - 1):
        m = 64 >> lv
        masks[:, lv, :] = (s // (2 * m) == t // (2 * m)) & (s % (2 * m) < m) & (t % (2 * m) >= m)
    masks[:, LEVELS - 1, :] = s == t
    return {"c_ident": eye, "c_causal": causal, "c_masks": masks}


def kernel(**inputs):
    import numpy as _np
    import concourse.bacc as _bacc
    from concourse import mybir as _mybir
    from concourse.bass_utils import run_bass_kernel_spmd as _run

    nc = _bacc.Bacc("TRN2", target_bir_lowering=False, num_devices=1)
    arrays, args = {}, []
    named = [(n, _np.ascontiguousarray(inputs[n])) for n in _INS] + list(constants().items())
    for name, a in named:
        arrays[f"in_{name}"] = a
        args.append(nc.dram_tensor(f"in_{name}", a.shape, _mybir.dt.from_np(a.dtype), kind="ExternalInput").ap())
    args.append(nc.dram_tensor("h_scratch", (TT, P, D), F32).ap())
    args.append(nc.dram_tensor("c_scratch", (NFX, S), F32).ap())
    args.append(nc.dram_tensor("out_h", (1, S, D), F32, kind="ExternalOutput").ap())
    block_kernel(nc, *args)
    r = _run(nc, [arrays], core_ids=[0])
    return r.results[0]["out_h"]
```
